# Optimizing a Trainium2 kernel written in Bass

```python
import math
import jax, jax.numpy as jnp
from jax import lax
import numpy as np

D_MODEL = 1024
BATCH = 1
SEQ = 256
DEPTH = 2

N_MIXERS = 4
ALPHA = (2 * DEPTH) ** 0.25
BETA = (8 * DEPTH) ** -0.25
LN_EPS = 1e-5

ML_HEADS = 4
ML_DV = D_MODEL // ML_HEADS
ML_DK = ML_DV // 2
ML_CHUNK = 64
ML_IN = 2 * ML_HEADS * ML_DK + 2 * D_MODEL + 4 * ML_HEADS

GLA_HEADS = 4
GLA_DK = D_MODEL // 2 // GLA_HEADS
GLA_DV = D_MODEL // GLA_HEADS
GLA_RANK = 16
GLA_TAU = 16.0
GLA_CHUNK = 32
GLA_IN = 2 * GLA_HEADS * GLA_DK + 2 * D_MODEL + 2 * GLA_RANK

LRU_WIDTH = D_MODEL
LRU_BLOCKS = 4
LRU_BW = LRU_WIDTH // LRU_BLOCKS
CONV_WIDTH = 4
LRU_C = 8.0
LRU_IN = 2 * LRU_WIDTH

MLA_HEADS = 8
MLA_NOPE = 128
MLA_ROPE = 64
MLA_DV = 128
MLA_Q_RANK = 384
MLA_KV_RANK = 256
MLA_IN = MLA_Q_RANK + MLA_KV_RANK + MLA_ROPE
ROPE_THETA = 10000.0
Q_BLOCK = 128

N_EXPERTS = 16
EXPERT_FF = 1024
CAPACITY_FACTOR = 2

N_MLSTM = (DEPTH - 0 + N_MIXERS - 1) // N_MIXERS
N_GLA = (DEPTH - 1 + N_MIXERS - 1) // N_MIXERS
N_LRU = (DEPTH - 2 + N_MIXERS - 1) // N_MIXERS
N_MLA = (DEPTH - 3 + N_MIXERS - 1) // N_MIXERS


def layer_norm(x, g, b):
    xf = x.astype(jnp.float32)
    mu = jnp.mean(xf, axis=-1, keepdims=True)
    var = jnp.mean(jnp.square(xf - mu), axis=-1, keepdims=True)
    return ((xf - mu) * lax.rsqrt(var + LN_EPS) * g + b).astype(x.dtype)

def rms_norm(x, g):
    xf = x.astype(jnp.float32)
    return (xf * lax.rsqrt(jnp.mean(jnp.square(xf), axis=-1, keepdims=True) + LN_EPS) * g).astype(x.dtype)

def head_norm(h, g):
    hf = h.astype(jnp.float32)
    mu = jnp.mean(hf, axis=-1, keepdims=True)
    var = jnp.mean(jnp.square(hf - mu), axis=-1, keepdims=True)
    hn = (hf - mu) * lax.rsqrt(var + LN_EPS)
    return hn.reshape(h.shape[0], h.shape[1], -1) * g.astype(jnp.float32)

def to_chunks(t, L):
    B, S = t.shape[0], t.shape[1]
    t = t.reshape((B, S // L, L) + t.shape[2:])
    return jnp.moveaxis(t, (1, 2), (0, 3))

def from_chunks(t):
    t = jnp.moveaxis(t, (0, 3), (1, 2))
    return t.reshape((t.shape[0], t.shape[1] * t.shape[2]) + t.shape[3:])

def flip_seq(t):
    return jnp.flip(t, axis=1)

def mlstm_chunked(q, k, v, ig, fg):
    B, S, H, DK = q.shape
    DV = v.shape[-1]
    L = ML_CHUNK
    mask = jnp.tril(jnp.ones((L, L), dtype=bool))

    def step(carry, inp):
        C, n, m = carry
        qb, kb, vb, ib, fb = inp
        b = jnp.cumsum(jax.nn.log_sigmoid(fb), axis=-1)
        g = b[..., -1]
        logD = jnp.where(mask, b[..., :, None] - b[..., None, :] + ib[..., None, :], -jnp.inf)
        inter = b + m[..., None]
        m_t = jnp.maximum(inter, jnp.max(logD, axis=-1))
        s = jnp.einsum('bhtd,bhsd->bhts', qb, kb) * jnp.exp(logD - m_t[..., None])
        w_inter = jnp.exp(inter - m_t)
        num = jnp.einsum('bhts,bhsv->bhtv', s, vb) + w_inter[..., None] * jnp.einsum('bhtd,bhdv->bhtv', qb, C)
        den = jnp.sum(s, axis=-1) + w_inter * jnp.einsum('bhtd,bhd->bht', qb, n)
        h = num / jnp.maximum(jnp.abs(den), jnp.exp(-m_t))[..., None]
        lw = g[..., None] - b + ib
        m_new = jnp.maximum(g + m, jnp.max(lw, axis=-1))
        ws = jnp.exp(lw - m_new[..., None])
        wc = jnp.exp(g + m - m_new)
        kw = kb * ws[..., None]
        C = wc[..., None, None] * C + jnp.einsum('bhsd,bhsv->bhdv', kw, vb)
        n = wc[..., None] * n + jnp.sum(kw, axis=-2)
        return (C, n, m_new), h

    init = (jnp.zeros((B, H, DK, DV), jnp.float32), jnp.zeros((B, H, DK), jnp.float32),
            jnp.zeros((B, H), jnp.float32))
    xs = (to_chunks(q, L), to_chunks(k, L), to_chunks(v, L), to_chunks(ig, L), to_chunks(fg, L))
    _, h = lax.scan(step, init, xs)
    return from_chunks(h)

def mlstm_mixer(x, w_in, gate_b, norm_g, w_out):
    B, S, _ = x.shape
    f32 = jnp.float32
    qk = ML_HEADS * ML_DK
    z = x @ w_in
    q, k, v, o, gates = jnp.split(z, [qk, 2 * qk, 2 * qk + D_MODEL, 2 * qk + 2 * D_MODEL], axis=-1)
    q = q.reshape(B, S, ML_HEADS, ML_DK).astype(f32) * (ML_DK ** -0.5)
    k = k.reshape(B, S, ML_HEADS, ML_DK).astype(f32)
    v = v.reshape(B, S, ML_HEADS, ML_DV).astype(f32)
    gates = gates.reshape(B, S, 2, 2, ML_HEADS).astype(f32) + gate_b.astype(f32)
    h_fwd = mlstm_chunked(q, k, v, gates[:, :, 0, 0], gates[:, :, 0, 1])
    h_bwd = flip_seq(mlstm_chunked(flip_seq(q), flip_seq(k), flip_seq(v),
                                   flip_seq(gates[:, :, 1, 0]), flip_seq(gates[:, :, 1, 1])))
    h = head_norm(h_fwd + h_bwd, norm_g).astype(x.dtype)
    return (jax.nn.sigmoid(o) * h) @ w_out

def gla_chunked(q, k, v, loga):
    B, S, H, DK = q.shape
    DV = v.shape[-1]
    L = GLA_CHUNK
    mask = jnp.tril(jnp.ones((L, L), dtype=bool))[:, :, None]

    def step(state, inp):
        qb, kb, vb, ab = inp
        b = jnp.cumsum(ab, axis=-2)
        dec = jnp.exp(jnp.where(mask, b[:, :, :, None, :] - b[:, :, None, :, :], -jnp.inf))
        A = jnp.einsum('bhtd,bhtsd,bhsd->bhts', qb, dec, kb)
        o = jnp.einsum('bhts,bhsv->bhtv', A, vb) + jnp.einsum('bhtd,bhdv->bhtv', qb * jnp.exp(b), state)
        g = b[:, :, -1, :]
        state = jnp.exp(g)[..., None] * state + jnp.einsum('bhsd,bhsv->bhdv', kb * jnp.exp(g[:, :, None, :] - b), vb)
        return state, o

    init = jnp.zeros((B, H, DK, DV), jnp.float32)
    xs = (to_chunks(q, L), to_chunks(k, L), to_chunks(v, L), to_chunks(loga, L))
    _, o = lax.scan(step, init, xs)
    return from_chunks(o)

def gla_mixer(x, w_in, gate_w, gate_b, norm_g, w_out):
    B, S, _ = x.shape
    f32 = jnp.float32
    qk = GLA_HEADS * GLA_DK
    z = x @ w_in
    q, k, v, r, glr = jnp.split(z, [qk, 2 * qk, 2 * qk + D_MODEL, 2 * qk + 2 * D_MODEL], axis=-1)
    q = q.reshape(B, S, GLA_HEADS, GLA_DK).astype(f32) * (GLA_DK ** -0.5)
    k = k.reshape(B, S, GLA_HEADS, GLA_DK).astype(f32)
    v = v.reshape(B, S, GLA_HEADS, GLA_DV).astype(f32)
    glr = glr.reshape(B, S, 2, GLA_RANK).astype(f32)
    loga = jax.nn.log_sigmoid(jnp.einsum('bsgr,grk->bsgk', glr, gate_w.astype(f32)) + gate_b.astype(f32)) / GLA_TAU
    loga = loga.reshape(B, S, 2, GLA_HEADS, GLA_DK)
    o_fwd = gla_chunked(q, k, v, loga[:, :, 0])
    o_bwd = flip_seq(gla_chunked(flip_seq(q), flip_seq(k), flip_seq(v), flip_seq(loga[:, :, 1])))
    o = head_norm(o_fwd + o_bwd, norm_g).astype(x.dtype)
    return (jax.nn.silu(r) * o) @ w_out

def rglru_direction(u, wa, ba, wx, bx, lam):
    B, S, W = u.shape
    ub = u.reshape(B, S, LRU_BLOCKS, LRU_BW)
    r = jax.nn.sigmoid(jnp.einsum('bsni,nij->bsnj', ub, wa).reshape(B, S, W) + ba)
    i = jax.nn.sigmoid(jnp.einsum('bsni,nij->bsnj', ub, wx).reshape(B, S, W) + bx)
    log_a = LRU_C * r * jax.nn.log_sigmoid(lam)
    a = jnp.exp(log_a)
    gated = jnp.sqrt(-jnp.expm1(2.0 * log_a)) * (i * u)

    def step(h, inp):
        a_t, g_t = inp
        h = a_t * h + g_t
        return h, h

    _, hs = lax.scan(step, jnp.zeros((B, W), jnp.float32), (jnp.swapaxes(a, 0, 1), jnp.swapaxes(gated, 0, 1)))
    return jnp.swapaxes(hs, 0, 1)

def rglru_mixer(x, w_in, conv_w, conv_b, gate_a_w, gate_a_b, gate_x_w, gate_x_b, lam, w_out):
    f32 = jnp.float32
    z = x @ w_in
    gate_branch, u = jnp.split(z, [LRU_WIDTH], axis=-1)
    u = lax.conv_general_dilated(u, conv_w[:, None, :].astype(u.dtype), window_strides=(1,),
                                 padding=[(CONV_WIDTH // 2, CONV_WIDTH - 1 - CONV_WIDTH // 2)],
                                 dimension_numbers=('NWC', 'WIO', 'NWC'),
                                 feature_group_count=LRU_WIDTH) + conv_b
    u = u.astype(f32)
    h_fwd = rglru_direction(u, gate_a_w[0].astype(f32), gate_a_b[0].astype(f32), gate_x_w[0].astype(f32),
                            gate_x_b[0].astype(f32), lam[0].astype(f32))
    h_bwd = flip_seq(rglru_direction(flip_seq(u), gate_a_w[1].astype(f32), gate_a_b[1].astype(f32),
                                     gate_x_w[1].astype(f32), gate_x_b[1].astype(f32), lam[1].astype(f32)))
    h = (h_fwd + h_bwd).astype(x.dtype)
    return (jax.nn.gelu(gate_branch) * h) @ w_out

def apply_rope(t, cos, sin):
    half = t.shape[-1] // 2
    t1, t2 = t[..., :half], t[..., half:]
    return jnp.concatenate([t1 * cos - t2 * sin, t2 * cos + t1 * sin], axis=-1)

def mla_mixer(x, positions, w_in, q_norm_g, kv_norm_g, w_uq, w_ukv, w_out):
    B, S, _ = x.shape
    f32 = jnp.float32
    z = x @ w_in
    cq, ckv, k_rope = jnp.split(z, [MLA_Q_RANK, MLA_Q_RANK + MLA_KV_RANK], axis=-1)
    q = (rms_norm(cq, q_norm_g) @ w_uq).reshape(B, S, MLA_HEADS, MLA_NOPE + MLA_ROPE)
    kv = (rms_norm(ckv, kv_norm_g) @ w_ukv).reshape(B, S, MLA_HEADS, MLA_NOPE + MLA_DV)
    q_nope, q_rope = jnp.split(q, [MLA_NOPE], axis=-1)
    k_nope, v = jnp.split(kv, [MLA_NOPE], axis=-1)
    half = MLA_ROPE // 2
    freq = ROPE_THETA ** (-jnp.arange(half, dtype=f32) / half)
    ang = positions.astype(f32)[..., None] * freq
    cos = jnp.cos(ang).astype(x.dtype)
    sin = jnp.sin(ang).astype(x.dtype)
    q_rope = apply_rope(q_rope, cos[:, :, None, :], sin[:, :, None, :])
    k_rope = apply_rope(k_rope, cos, sin)
    scale = (MLA_NOPE + MLA_ROPE) ** -0.5
    nq = S // Q_BLOCK
    qn_blocks = jnp.moveaxis(q_nope.reshape(B, nq, Q_BLOCK, MLA_HEADS, MLA_NOPE), 1, 0)
    qr_blocks = jnp.moveaxis(q_rope.reshape(B, nq, Q_BLOCK, MLA_HEADS, MLA_ROPE), 1, 0)

    def attend(blk):
        qn, qr = blk
        s = (jnp.einsum('bqhd,bkhd->bhqk', qn, k_nope) + jnp.einsum('bqhd,bkd->bhqk', qr, k_rope)).astype(f32) * scale
        p = jax.nn.softmax(s, axis=-1).astype(v.dtype)
        return jnp.einsum('bhqk,bkhv->bqhv', p, v)

    out = lax.map(attend, (qn_blocks, qr_blocks))
    out = jnp.moveaxis(out, 0, 1).reshape(B, S, MLA_HEADS * MLA_DV)
    return out @ w_out

def ec_moe(x, w_router, w_gate, w_up, w_down):
    B, N, _ = x.shape
    cap = CAPACITY_FACTOR * N // N_EXPERTS
    aff = jax.nn.softmax(jnp.einsum('bnd,de->bne', x, w_router).astype(jnp.float32), axis=-1)
    gates, idx = lax.top_k(jnp.swapaxes(aff, 1, 2), cap)
    bidx = jnp.arange(B)[:, None, None]
    xin = x[bidx, idx]
    h = jax.nn.silu(jnp.einsum('becd,edf->becf', xin, w_gate)) * jnp.einsum('becd,edf->becf', xin, w_up)
    out = jnp.einsum('becf,efd->becd', h, w_down) * gates[..., None].astype(x.dtype)
    return jnp.zeros_like(x).at[bidx, idx].add(out.astype(x.dtype))

def first_inputs(seed: int = 0) -> dict:
    key = jax.random.key(seed)
    keys = iter(jax.random.split(key, 64))
    f32 = jnp.float32

    def nrm(shape, scale):
        return jax.random.normal(next(keys), shape, f32) * scale

    def gain(shape):
        return 1.0 + nrm(shape, 0.02)

    D = D_MODEL
    x = jax.random.normal(next(keys), (BATCH, SEQ, D), f32)
    positions = (jnp.arange(SEQ, dtype=jnp.int32)[None, :]
                 + jax.random.randint(next(keys), (BATCH, 1), 0, SEQ, dtype=jnp.int32))
    mlstm_w_in = nrm((N_MLSTM, D, ML_IN), D ** -0.5)
    ig_b = nrm((N_MLSTM, 2, 1, ML_HEADS), 0.1)
    fg_b = 3.0 + 3.0 * jax.random.uniform(next(keys), (N_MLSTM, 2, 1, ML_HEADS), f32)
    mlstm_gate_b = jnp.concatenate([ig_b, fg_b], axis=2)
    mlstm_norm_g = gain((N_MLSTM, D))
    mlstm_w_out = nrm((N_MLSTM, D, D), BETA * D ** -0.5)
    gla_w_in = nrm((N_GLA, D, GLA_IN), D ** -0.5)
    gla_gate_w = nrm((N_GLA, 2, GLA_RANK, GLA_HEADS * GLA_DK), GLA_RANK ** -0.5)
    gla_gate_b = nrm((N_GLA, 2, GLA_HEADS * GLA_DK), 0.1)
    gla_norm_g = gain((N_GLA, D))
    gla_w_out = nrm((N_GLA, D, D), BETA * D ** -0.5)
    lru_w_in = nrm((N_LRU, D, LRU_IN), D ** -0.5)
    lru_conv_w = nrm((N_LRU, CONV_WIDTH, LRU_WIDTH), CONV_WIDTH ** -0.5)
    lru_conv_b = nrm((N_LRU, LRU_WIDTH), 0.02)
    lru_gate_a_w = nrm((N_LRU, 2, LRU_BLOCKS, LRU_BW, LRU_BW), LRU_BW ** -0.5)
    lru_gate_a_b = nrm((N_LRU, 2, LRU_WIDTH), 0.1)
    lru_gate_x_w = nrm((N_LRU, 2, LRU_BLOCKS, LRU_BW, LRU_BW), LRU_BW ** -0.5)
    lru_gate_x_b = nrm((N_LRU, 2, LRU_WIDTH), 0.1)
    a0 = jax.random.uniform(next(keys), (N_LRU, 2, LRU_WIDTH), f32, minval=0.9, maxval=0.999)
    s0 = a0 ** (1.0 / LRU_C)
    lru_lambda = jnp.log(s0) - jnp.log1p(-s0)
    lru_w_out = nrm((N_LRU, LRU_WIDTH, D), BETA * LRU_WIDTH ** -0.5)
    mla_w_in = nrm((N_MLA, D, MLA_IN), D ** -0.5)
    mla_q_norm_g = gain((N_MLA, MLA_Q_RANK))
    mla_kv_norm_g = gain((N_MLA, MLA_KV_RANK))
    mla_w_uq = nrm((N_MLA, MLA_Q_RANK, MLA_HEADS * (MLA_NOPE + MLA_ROPE)), MLA_Q_RANK ** -0.5)
    mla_w_ukv = nrm((N_MLA, MLA_KV_RANK, MLA_HEADS * (MLA_NOPE + MLA_DV)), MLA_KV_RANK ** -0.5)
    mla_w_out = nrm((N_MLA, MLA_HEADS * MLA_DV, D), BETA * (MLA_HEADS * MLA_DV) ** -0.5)
    moe_router = nrm((DEPTH, D, N_EXPERTS), D ** -0.5)
    moe_w_gate = nrm((DEPTH, N_EXPERTS, D, EXPERT_FF), D ** -0.5)
    moe_w_up = nrm((DEPTH, N_EXPERTS, D, EXPERT_FF), D ** -0.5)
    moe_w_down = nrm((DEPTH, N_EXPERTS, EXPERT_FF, D), BETA * EXPERT_FF ** -0.5)
    ln_g = gain((DEPTH, 2, D))
    ln_b = nrm((DEPTH, 2, D), 0.02)
    return {
        'x': x, 'positions': positions,
        'mlstm_w_in': mlstm_w_in, 'mlstm_gate_b': mlstm_gate_b, 'mlstm_norm_g': mlstm_norm_g, 'mlstm_w_out': mlstm_w_out,
        'gla_w_in': gla_w_in, 'gla_gate_w': gla_gate_w, 'gla_gate_b': gla_gate_b, 'gla_norm_g': gla_norm_g, 'gla_w_out': gla_w_out,
        'lru_w_in': lru_w_in, 'lru_conv_w': lru_conv_w, 'lru_conv_b': lru_conv_b,
        'lru_gate_a_w': lru_gate_a_w, 'lru_gate_a_b': lru_gate_a_b, 'lru_gate_x_w': lru_gate_x_w, 'lru_gate_x_b': lru_gate_x_b,
        'lru_lambda': lru_lambda, 'lru_w_out': lru_w_out,
        'mla_w_in': mla_w_in, 'mla_q_norm_g': mla_q_norm_g, 'mla_kv_norm_g': mla_kv_norm_g,
        'mla_w_uq': mla_w_uq, 'mla_w_ukv': mla_w_ukv, 'mla_w_out': mla_w_out,
        'moe_router': moe_router, 'moe_w_gate': moe_w_gate, 'moe_w_up': moe_w_up, 'moe_w_down': moe_w_down,
        'ln_g': ln_g, 'ln_b': ln_b,
    }

def first_block(x, positions,
              mlstm_w_in, mlstm_gate_b, mlstm_norm_g, mlstm_w_out,
              gla_w_in, gla_gate_w, gla_gate_b, gla_norm_g, gla_w_out,
              lru_w_in, lru_conv_w, lru_conv_b, lru_gate_a_w, lru_gate_a_b, lru_gate_x_w, lru_gate_x_b,
              lru_lambda, lru_w_out,
              mla_w_in, mla_q_norm_g, mla_kv_norm_g, mla_w_uq, mla_w_ukv, mla_w_out,
              moe_router, moe_w_gate, moe_w_up, moe_w_down,
              ln_g, ln_b):
    for i in range(DEPTH):
        m = i % N_MIXERS
        j = i // N_MIXERS
        if m == 0:
            h = mlstm_mixer(x, mlstm_w_in[j], mlstm_gate_b[j], mlstm_norm_g[j], mlstm_w_out[j])
        elif m == 1:
            h = gla_mixer(x, gla_w_in[j], gla_gate_w[j], gla_gate_b[j], gla_norm_g[j], gla_w_out[j])
        elif m == 2:
            h = rglru_mixer(x, lru_w_in[j], lru_conv_w[j], lru_conv_b[j], lru_gate_a_w[j], lru_gate_a_b[j],
                            lru_gate_x_w[j], lru_gate_x_b[j], lru_lambda[j], lru_w_out[j])
        else:
            h = mla_mixer(x, positions, mla_w_in[j], mla_q_norm_g[j], mla_kv_norm_g[j],
                          mla_w_uq[j], mla_w_ukv[j], mla_w_out[j])
        x = layer_norm(ALPHA * x + h, ln_g[i, 0], ln_b[i, 0])
        y = ec_moe(x, moe_router[i], moe_w_gate[i], moe_w_up[i], moe_w_down[i])
        x = layer_norm(ALPHA * x + y, ln_g[i, 1], ln_b[i, 1])
    return x


DEPTH_2 = 1

N_HEADS = 16
HEAD_DIM = D_MODEL // N_HEADS
D_FF = ((8 * D_MODEL // 3 + 255) // 256) * 256
CONV_WIDTH_2 = 3
N_MIXERS_2 = 2
MOBA_BLOCK = 256
MOBA_TOPK = 3
MOBA_QCHUNK = 32
SB_QBLOCK = 128
REL_BUCKETS = 32
REL_MAX_DIST = 128
NORM_EPS = 1e-6
NEG = -1e30


def rms_norm_2(x, g):
    xf = x.astype(jnp.float32)
    y = xf * lax.rsqrt(jnp.mean(xf * xf, axis=-1, keepdims=True) + NORM_EPS)
    return (y * g.astype(jnp.float32)).astype(x.dtype)

def rel_bucket(dist):
    n = jnp.maximum(dist, 0)
    max_exact = REL_BUCKETS // 2
    nf = jnp.maximum(n, 1).astype(jnp.float32)
    large = max_exact + (jnp.log(nf / max_exact) / math.log(REL_MAX_DIST / max_exact)
                         * (REL_BUCKETS - max_exact)).astype(jnp.int32)
    large = jnp.minimum(large, REL_BUCKETS - 1)
    return jnp.where(n < max_exact, n, large)

def moba_attention(q, k, v, rel_bias):
    B, H, S, Dh = q.shape
    BS = MOBA_BLOCK
    QC = MOBA_QCHUNK
    nb = -(-S // BS)
    pad = nb * BS - S
    kp = jnp.pad(k, ((0, 0), (0, 0), (0, pad), (0, 0))).reshape(B, H, nb, BS, Dh)
    vp = jnp.pad(v, ((0, 0), (0, 0), (0, pad), (0, 0))).reshape(B, H, nb, BS, Dh)
    scale = Dh ** -0.5

    pos = jnp.arange(S)
    qblk = pos // BS
    kmean = jnp.mean(kp.astype(jnp.float32), axis=3)
    gate = jnp.einsum('bhsd,bhnd->bhsn', q.astype(jnp.float32), kmean)
    past = jnp.arange(nb)[None, :] < qblk[:, None]
    gate = jnp.where(past, gate, NEG)
    kk = min(MOBA_TOPK, nb)
    _, top_idx = lax.top_k(gate, kk)
    valid = jnp.arange(kk)[None, :] < qblk[:, None]

    nc = S // QC
    q_c = q.reshape(B, H, nc, QC, Dh).transpose(2, 0, 1, 3, 4)
    idx_c = top_idx.reshape(B, H, nc, QC, kk).transpose(2, 0, 1, 3, 4)
    valid_c = valid.reshape(nc, QC, kk)
    bi = jnp.arange(B)[:, None, None]
    hi = jnp.arange(H)[None, :, None]
    hi4 = jnp.arange(H)[None, :, None, None]
    offs = jnp.arange(BS)

    def chunk(args):
        ci, qi, idx, vld = args
        qpos = ci * QC + jnp.arange(QC)
        own = (ci * QC) // BS
        k_own = lax.dynamic_index_in_dim(kp, own, axis=2, keepdims=False)
        v_own = lax.dynamic_index_in_dim(vp, own, axis=2, keepdims=False)
        kpos_own = own * BS + offs
        s_own = jnp.einsum('bhqd,bhkd->bhqk', qi, k_own).astype(jnp.float32) * scale
        s_own = s_own + rel_bias[:, rel_bucket(qpos[:, None] - kpos_own[None, :])].astype(jnp.float32)
        s_own = jnp.where(kpos_own[None, :] <= qpos[:, None], s_own, NEG)
        logits = []
        for j in range(kk):
            blk = idx[..., j]
            kg = kp[bi, hi, blk]
            s = jnp.einsum('bhqd,bhqkd->bhqk', qi, kg).astype(jnp.float32) * scale
            kpos = blk[..., None] * BS + offs
            bias = rel_bias[hi4, rel_bucket(qpos[None, None, :, None] - kpos)].astype(jnp.float32)
            logits.append(jnp.where(vld[None, None, :, j, None], s + bias, NEG))
        logits.append(s_own)
        p = jax.nn.softmax(jnp.concatenate(logits, axis=-1), axis=-1).astype(v.dtype)
        out = jnp.einsum('bhqk,bhkd->bhqd', p[..., kk * BS:], v_own)
        for j in range(kk):
            vg = vp[bi, hi, idx[..., j]]
            out = out + jnp.einsum('bhqk,bhqkd->bhqd', p[..., j * BS:(j + 1) * BS], vg)
        return out

    out = lax.map(chunk, (jnp.arange(nc), q_c, idx_c, valid_c))
    return out.transpose(1, 2, 0, 3, 4).reshape(B, H, S, Dh)

def stick_breaking_attention(q, k, v):
    B, H, S, Dh = q.shape
    QB = SB_QBLOCK
    nq = S // QB
    scale = Dh ** -0.5
    kpos = jnp.arange(S)
    q_b = q.reshape(B, H, nq, QB, Dh).transpose(2, 0, 1, 3, 4)

    def block(args):
        bidx, qi = args
        qpos = bidx * QB + jnp.arange(QB)
        z = jnp.einsum('bhqd,bhkd->bhqk', qi, k).astype(jnp.float32) * scale
        strict = kpos[None, :] < qpos[:, None]
        log_beta = jax.nn.log_sigmoid(z)
        log_1mb = jnp.where(strict, jax.nn.log_sigmoid(-z), 0.0)
        tail = lax.cumsum(log_1mb, axis=3, reverse=True) - log_1mb
        a = jnp.where(strict, jnp.exp(log_beta + tail), 0.0)
        return jnp.einsum('bhqk,bhkd->bhqd', a.astype(v.dtype), v)

    out = lax.map(block, (jnp.arange(nq), q_b))
    return out.transpose(1, 2, 0, 3, 4).reshape(B, H, S, Dh)

def conv_ffn(y, w_up, conv_w, conv_b, w_down):
    u = y @ w_up
    c = u.shape[-1]
    u = lax.conv_general_dilated(u, conv_w[:, None, :], window_strides=(1,),
                                 padding=[(CONV_WIDTH_2 - 1, 0)],
                                 dimension_numbers=('NWC', 'WIO', 'NWC'),
                                 feature_group_count=c) + conv_b
    gate, val = jnp.split(u, 2, axis=-1)
    return (jax.nn.silu(gate) * val) @ w_down

def second_inputs(seed: int = 0) -> dict:
    key = jax.random.key(seed)
    ks = jax.random.split(key, 12)
    D, F = D_MODEL, D_FF
    f32 = jnp.float32
    return {
        "x": jax.random.normal(ks[0], (BATCH, SEQ, D), f32),
        "attn_norm": 1.0 + 0.02 * jax.random.normal(ks[1], (DEPTH_2, D), f32),
        "w_qkv": jax.random.normal(ks[2], (DEPTH_2, D, 3 * D), f32) * D ** -0.5,
        "w_o": jax.random.normal(ks[3], (DEPTH_2, D, D), f32) * D ** -0.5,
        "rel_bias": 0.5 * jax.random.normal(ks[4], (N_HEADS, REL_BUCKETS), f32),
        "ffn_norm": 1.0 + 0.02 * jax.random.normal(ks[5], (DEPTH_2, D), f32),
        "w_up": jax.random.normal(ks[6], (DEPTH_2, D, 2 * F), f32) * D ** -0.5,
        "conv_w": jax.random.normal(ks[7], (DEPTH_2, CONV_WIDTH_2, 2 * F), f32) * CONV_WIDTH_2 ** -0.5,
        "conv_b": 0.02 * jax.random.normal(ks[8], (DEPTH_2, 2 * F), f32),
        "w_down": jax.random.normal(ks[9], (DEPTH_2, F, D), f32) * F ** -0.5,
        "final_norm": 1.0 + 0.02 * jax.random.normal(ks[10], (D,), f32),
    }

def second_block(x, attn_norm, w_qkv, w_o, rel_bias, ffn_norm, w_up, conv_w, conv_b, w_down, final_norm):
    B, S, D = x.shape
    h = x
    for i in range(DEPTH_2):
        y = rms_norm_2(h, attn_norm[i])
        qkv = (y @ w_qkv[i]).reshape(B, S, 3, N_HEADS, HEAD_DIM)
        q = qkv[:, :, 0].transpose(0, 2, 1, 3)
        k = qkv[:, :, 1].transpose(0, 2, 1, 3)
        v = qkv[:, :, 2].transpose(0, 2, 1, 3)
        if i % N_MIXERS_2 == 0:
            o = moba_attention(q, k, v, rel_bias)
        else:
            o = stick_breaking_attention(q, k, v)
        h = h + o.transpose(0, 2, 1, 3).reshape(B, S, D) @ w_o[i]
        y = rms_norm_2(h, ffn_norm[i])
        h = h + conv_ffn(y, w_up[i], conv_w[i], conv_b[i], w_down[i])
    return rms_norm_2(h, final_norm)


def setup_inputs(seed=0):
    out = dict(first_inputs(seed))
    for name, value in second_inputs(seed + 1).items():
        if name != "x":
            out[name + "_2"] = value
    return out


def reference(
    x, positions, mlstm_w_in, mlstm_gate_b, mlstm_norm_g, mlstm_w_out, gla_w_in, gla_gate_w,
    gla_gate_b, gla_norm_g, gla_w_out, lru_w_in, lru_conv_w, lru_conv_b, lru_gate_a_w,
    lru_gate_a_b, lru_gate_x_w, lru_gate_x_b, lru_lambda, lru_w_out, mla_w_in, mla_q_norm_g,
    mla_kv_norm_g, mla_w_uq, mla_w_ukv, mla_w_out, moe_router, moe_w_gate, moe_w_up, moe_w_down,
    ln_g, ln_b, attn_norm_2, w_qkv_2, w_o_2, rel_bias_2, ffn_norm_2, w_up_2, conv_w_2, conv_b_2,
    w_down_2, final_norm_2,
):
    x = first_block(
        x, positions, mlstm_w_in, mlstm_gate_b, mlstm_norm_g, mlstm_w_out, gla_w_in, gla_gate_w,
        gla_gate_b, gla_norm_g, gla_w_out, lru_w_in, lru_conv_w, lru_conv_b, lru_gate_a_w,
        lru_gate_a_b, lru_gate_x_w, lru_gate_x_b, lru_lambda, lru_w_out, mla_w_in, mla_q_norm_g,
        mla_kv_norm_g, mla_w_uq, mla_w_ukv, mla_w_out, moe_router, moe_w_gate, moe_w_up,
        moe_w_down, ln_g, ln_b,
    )
    return second_block(
        x, attn_norm_2, w_qkv_2, w_o_2, rel_bias_2, ffn_norm_2, w_up_2, conv_w_2, conv_b_2,
        w_down_2, final_norm_2,
    )


_drawn_inputs = setup_inputs


def setup_inputs(seed=0):
    import zlib

    import numpy as np

    out = dict(_drawn_inputs(seed))
    spreads = {}
    factors = {'mlstm_norm_g': 8.0,
     'gla_gate_b': 5.401,
     'gla_norm_g': 8.0,
     'attn_norm_2': 7.44,
     'ffn_norm_2': 3.907,
     'conv_b_2': 3.917,
     'final_norm_2': 2.865}
    for name, (base, spread) in spreads.items():
        noise = np.random.default_rng([zlib.crc32(name.encode()), seed]).standard_normal(out[name].shape)
        drawn = base * np.exp(spread * noise) if base else spread * noise
        out[name] = __import__('jax').numpy.asarray(drawn.astype(out[name].dtype))
    for name, factor in factors.items():
        out[name] = (out[name] * factor).astype(out[name].dtype)
    return out
```

```python
import math
from contextlib import ExitStack

import numpy as np
import concourse.bass as bass
from concourse import mybir

ALU = mybir.AluOpType
ACT = mybir.ActivationFunctionType
AX = mybir.AxisListType
F32 = mybir.dt.float32
U8 = mybir.dt.uint8

P = 128
S = 256
TT = S // P
D = 1024
KC = D // P
DEPTH = 2
ALPHA = (2 * DEPTH) ** 0.25
LN_EPS = 1e-5
RMS_EPS = 1e-6
BIG = 1e30

H = 4
DK = 128
DV = 256
VW = DV + 1
GLA_TAU = 16.0
RANK = 16

E = 16
CAP = 2 * S // E
EG = P // CAP
NG = E // EG

AH = 16
AD = 64
BUCKETS = 32
MAXDIST = 128
FF = 2816
FB = FF // P
UPT = FF // S

SLOTS = 8
TILE = 4096
TPE = 6
T_MLSTM = 0
T_MOE = [8, 112]
T_GLA = 104
T_QKV = 208
T_WO = 214
T_UP = 216
T_DOWN = T_UP + UPT
N_DOWN = (FB + 3) // 4
LEVELS = [64, 32, 16, 8, 4, 2, 1]
WROW = 3 * P


def constants():
    i = np.arange(P)
    ident = np.eye(P, dtype=np.float32)
    flip = ident[::-1].copy()
    after = np.where(i[:, None] > i[None, :], BIG, 0).astype(np.float32)
    before = np.where(i[:, None] < i[None, :], BIG, 0).astype(np.float32)
    slots = np.tile(np.arange(1, CAP + 1, dtype=np.float32), (P, 1))
    main = np.concatenate([ident, flip, after, before, slots], 1)
    n = np.arange(64)
    masks = np.zeros((P, 2, len(LEVELS), 64), np.float32)
    for lv, L in enumerate(LEVELS):
        same = (i[:, None] // (2 * L)) == (n[None, :] // L)
        left = ((i % (2 * L)) < L)[:, None]
        masks[:, 0, lv] = same & left
        masks[:, 1, lv] = same & ~left
    dist = np.arange(S)[::-1]
    half = BUCKETS // 2
    nf = np.maximum(dist, 1).astype(np.float32)
    large = half + (np.log(nf / np.float32(half)) / np.float32(math.log(MAXDIST / half))
                    * np.float32(BUCKETS - half)).astype(np.int32)
    bucket = np.where(dist < half, dist, np.minimum(large, BUCKETS - 1))
    onehot = (np.arange(BUCKETS)[:, None] == bucket[None, :]).astype(np.float32)
    return main, masks.reshape(P, -1), onehot


def build(nc, t, out):
    with ExitStack() as ctx:
        build_in(nc, t, out, ctx)


def build_in(nc, t, out, ctx):
    def sem(name):
        return ctx.enter_context(nc.semaphore(name))

    def sbuf(name, cols, dt=F32):
        return ctx.enter_context(nc.sbuf_tensor(name, [P, cols], dt))

    ring = sbuf("weight_ring", SLOTS * TILE)
    consts = sbuf("consts", 4 * P + CAP)
    ident = consts[:, 0:P]
    flip = consts[:, P:2 * P]
    mask_after = consts[:, 2 * P:3 * P]
    mask_before = consts[:, 3 * P:4 * P]
    slot_ids = consts[:, 4 * P:4 * P + CAP]
    ones = sbuf("ones", 8)
    router_t = sbuf("router", DEPTH * KC * E)
    level_masks = sbuf("level_masks", 2 * len(LEVELS) * 64, U8)
    x_tok_t = sbuf("x_tok", TT * D)
    xT_t = sbuf("xT", KC * S)
    acc_t = sbuf("acc", TT * D)
    gb_t = sbuf("norm_rows", 2 * D)
    ng_t = sbuf("head_gain", D)
    small = sbuf("small", 256)
    wglr_t = sbuf("gla_gate_columns", KC * 2 * RANK)
    room = sbuf("phase_room", 9600)

    x_tok = x_tok_t[:, :].rearrange("p (t d) -> p t d", t=TT)
    acc = acc_t[:, :].rearrange("p (t d) -> p t d", t=TT)
    xT = xT_t[:, :].rearrange("p (k s) -> p k s", k=KC)
    gain_row = gb_t[:, 0:D]
    bias_row = gb_t[:, D:2 * D]

    def rooms(*sizes):
        at, got = 0, []
        for n in sizes:
            got.append(room[:, at:at + n])
            at += n
        assert at <= 9600, at
        return got

    stats = small[:, 0:48].rearrange("p (n s) -> p n s", s=6)
    meanvar = small[:, 48:64].rearrange("p (n s) -> p n s", s=2)
    spread = small[:, 64:72]
    inv_spread = small[:, 72:80]

    qkT_t, v_t, gate_t, mix_t = rooms(2 * H * S, TT * H * VW, TT * D, 3448)
    qT = qkT_t[:, 0:H * S]
    kT = qkT_t[:, H * S:2 * H * S]
    v_aug = v_t.rearrange("p (t h w) -> p t h w", t=TT, w=VW)
    gate = gate_t.rearrange("p (t d) -> p t d", t=TT)
    gates_all = gate_t[0:16, 0:S]
    row_soft = mix_t[0:H, 248:760]
    row_m = mix_t[0:H, 760:1272]
    row_b = mix_t[0:H, 1272:1784]
    row_a = gb_t[0:H, 0:512]
    row_max = gb_t[0:H, 512:1024]
    wgate = mix_t[:, 1784:1784 + 128].rearrange("p (k n) -> p k n", k=KC)
    decay = mix_t[:, 1912:1912 + 2 * 2 * 384].rearrange("p (b d n) -> p b d n", b=2, d=2)
    gate_bias = small[0:16, 80:81]
    a_cols = small[:, 96:112]
    floor_cols = small[:, 112:128]
    den = small[:, 128:132]
    inv_den = small[:, 132:136]
    b_t = mix_t[:, 0:2 * H * S]
    b_cum = b_t.rearrange("p (n s) -> p n s", s=S)
    q_dec = mix_t[:, 2048:3072].rearrange("p (d n) -> p d n", d=2)
    wglr = wglr_t[:, :].rearrange("p (k n) -> p k n", k=KC)
    k_dec = acc_t[:, :].rearrange("p (d n) -> p d n", d=2)
    diffs = gb_t[:, :].rearrange("p (d w n) -> p d w n", d=2, w=2)
    gate_w_sb = room[0:2 * RANK, 7840:8864].rearrange("p (d n) -> p d n", d=2)
    gate_b_rows = room[0:8, 8864:8992]
    glrT = room[0:2 * RANK, 8992:9248]
    attn_row = room[:, 7840:8864]
    gate_b_cols = small[:, 80:88]
    A = xT_t[:, :].rearrange("p (s h t) -> p s h t", s=TT, h=H)

    (xin_t, sel_t, selg_t, selgT_t, selgrp_t, hid_t, sil_t, hidT_t, exp_t, aff_t,
     affT_t, work_t, picked_t) = rooms(
        1024, 1024, 1024, 1024, 256, 512, 512, 512, 1024, 32, 256, 256, 256)
    xinT = xin_t.rearrange("p (k n) -> p k n", k=KC)
    sel = sel_t.rearrange("p (t n) -> p t n", t=TT)
    selg = selg_t.rearrange("p (t n) -> p t n", t=TT)
    hid = hid_t.rearrange("p (b n) -> p b n", b=2)
    hidT = hidT_t.rearrange("p (b c n) -> p b c n", b=2, c=2)
    silu_g = sil_t.rearrange("p (b n) -> p b n", b=2)
    w_router = router_t[:, :].rearrange("p (l k n) -> p l k n", l=DEPTH, k=KC)
    aff = aff_t.rearrange("p (t e) -> p t e", t=TT)
    top8 = small[0:E, 160:192]
    row_max_r = small[:, 136:138]
    row_sum_r = small[:, 138:140]
    inv_sum_r = small[:, 140:142]

    aqk_t, av_t, prob_t, probT_t = rooms(16 * S, TT * D, 768, 768)
    aqk = aqk_t.rearrange("p (n s) -> p n s", s=S)
    av = av_t.rearrange("p (t d) -> p t d", t=TT)
    probs = prob_t.rearrange("p (b n) -> p b n", b=2)
    probsT = probT_t.rearrange("p (b n) -> p b n", b=2)
    bias_flip = acc_t[:, :].rearrange("p (b h n) -> p b h n", b=2, h=4)
    neg_max = small[:, 144:148]
    prob_sum = small[:, 148:152]
    inv_prob = small[:, 152:156]
    rel_T = room[0:BUCKETS, 8900:8916]
    dist_hot = room[0:BUCKETS, 8400:8400 + S]
    bias_rows = room[0:AH, 8960:8960 + WROW]

    ffh_t, conv_t, convw_t, _ = rooms(FB * S, 2 * 1024, 4 * 2 * FB, 984)
    convrow_t = room[:, 8864:8864 + 4 * P]
    ffh = ffh_t.rearrange("p (n s) -> p n s", s=S)
    conv = conv_t.rearrange("p (b n s) -> p b n s", b=2, s=S)
    conv_cols = convw_t.rearrange("p (j n) -> p j n", j=4)
    conv_rows = convrow_t[0:2 * FB, :].rearrange("p (j n) -> p j n", j=4)
    square_sum = small[:, 156:158]

    PS = [ctx.enter_context(nc.psum_tensor(f"bank{i}", [P, 512], F32)) for i in range(8)]

    bias_dram = nc.dram_tensor("bias_rows_dram", (AH, WROW), F32, kind="Internal")

    landed = [sem(f"landed{i}") for i in range(SLOTS)]
    tile_used = sem("tile_used")
    const_landed = sem("const_landed")
    x_landed = sem("x_landed")
    small_landed = [sem(f"small_landed{i}") for i in range(6)]
    rows_landed = sem("rows_landed")
    gain_landed = sem("gain_landed")
    router_landed = sem("router_landed")
    attn_row_landed = sem("attn_row_landed")
    ones_ready = sem("ones_ready")
    masks_ready = sem("masks_ready")
    tokens_ready = sem("tokens_ready")
    tr_done = sem("tr_done")
    tr_act = sem("tr_act")
    tr_dve = sem("tr_dve")
    proj_act = sem("proj_act")
    proj_dve = sem("proj_dve")
    gate_ready = sem("gate_ready")
    hn_var, hn_sd = sem("hn_var"), sem("hn_sd")
    ln_var, ln_sd = sem("ln_var"), sem("ln_sd")
    dve_seq = sem("dve_seq")
    act_seq = sem("act_seq")
    gates_done, gates_biased, gates_split = sem("gates_done"), sem("gates_biased"), sem("gates_split")
    gate_soft, gate_rows, gate_colsd, gate_scalars = (
        sem("gate_soft"), sem("gate_rows"), sem("gate_cols"), sem("gate_scalars"))
    mb_done, scores_done, decay_done = sem("mb_done"), sem("scores_done"), sem("decay_done")
    weights_done, num_done, head_out = sem("weights_done"), sem("num_done"), sem("head_out")
    glr_done, glr_copied, z_done, z_ready, z_soft, b_ready = (
        sem("glr_done"), sem("glr_copied"), sem("z_done"), sem("z_ready"), sem("z_soft"), sem("b_ready"))
    glr_zero = sem("glr_zero")
    diffs_done, decays_exp, scaled_done, prod_done, placed = (
        sem("diffs_done"), sem("decays_exp"), sem("scaled_done"), sem("prod_done"), sem("placed"))
    diag_done, gla_out = sem("diag_done"), sem("gla_out")
    logits_done, aff_exp, aff_ready, affT_done, slots_ready, slotsT_done, sel_ready, selT_done, selT_copied = (
        sem("logits_done"), sem("aff_exp"), sem("aff_ready"), sem("affT_done"), sem("slots_ready"),
        sem("slotsT_done"), sem("sel_ready"), sem("selT_done"), sem("selT_copied"))
    router_max, acc_init, sel_grp = sem("router_max"), sem("acc_init"), sem("sel_grp")
    xin_done, xin_act, xin_dve = sem("xin_done"), sem("xin_act"), sem("xin_dve")
    silu_done, hid_done = sem("silu_done"), sem("hid_done")
    hidT_done, hidT_copied = sem("hidT_done"), sem("hidT_copied")
    exp_act, exp_dve = sem("exp_act"), sem("exp_dve")
    comb_done, acc_added = sem("comb_done"), sem("acc_added")
    relb_done, relb_copied, relb_stored = sem("relb_done"), sem("relb_copied"), sem("relb_stored")
    bias_landed = [sem("bias_landed0"), sem("bias_landed1")]
    rms_sq, rms_var, rms_sd, x_sum = sem("rms_sq"), sem("rms_var"), sem("rms_sd"), sem("x_sum")
    s_done, max_done, probs_exp, p_ready, pt_done, pt_copied, o_done, o_copied = (
        sem("s_done"), sem("max_done"), sem("probs_exp"), sem("p_ready"), sem("pt_done"),
        sem("pt_copied"), sem("o_done"), sem("o_copied"))
    convT_done, convT_copied, taps_done, conv_done, ff_silu, ff_ready = (
        sem("convT_done"), sem("convT_copied"), sem("taps_done"), sem("conv_done"),
        sem("ff_silu"), sem("ff_ready"))
    out_landed = sem("out_landed")

    def slot(n):
        s = n % SLOTS
        return ring[:, s * TILE:(s + 1) * TILE]

    def arrived(pe, n, more=0):
        pe.wait_ge(landed[n % SLOTS], 16 * (n // SLOTS + 1) + more)

    class Chain:
        def __init__(self, eng, s):
            self.eng, self.s, self.n = eng, s, 0

        def link(self, ins):
            self.n += 1
            ins.then_inc(self.s, 1)
            self.eng.wait_ge(self.s, self.n)

    U_X0, U_Y0, U_M0, U_X1, U_Y1, U_M1, U_ATT, U_FFN = range(8)

    def act_count(stage, i):
        return 6 * stage + i + 1

    def dve_count(stage, i):
        return 4 * stage + (i + 1 if stage == 2 else min(i + 1, 4))

    block = ctx.enter_context(nc.Block())

    @block.sync
    def _(sp):
        def free(n):
            if n >= SLOTS:
                sp.wait_ge(tile_used, n - SLOTS + 1)

        def load(n, src, dst=None):
            free(n)
            sp.dma_start(slot(n) if dst is None else dst, src).then_inc(landed[n % SLOTS], 16)

        def columns(n, w, first, count):
            v = w.rearrange("(k p) n -> p k n", p=P)
            for j in range(count):
                load(n + j, v[:, :, first + 512 * j:first + 512 * (j + 1)],
                     slot(n + j).rearrange("p (k n) -> p k n", k=KC))

        def experts(layer):
            ws = [t[w][layer].rearrange("e (r k p) n -> e r p k n", p=P, k=4)
                  for w in ("moe_w_gate", "moe_w_up", "moe_w_down")]
            base = T_MOE[layer]
            with sp.Fori(0, NG) as g:
                for j in range(EG):
                    for c in range(TPE):
                        n = TPE * j + c
                        sp.wait_ge(tile_used, g * (EG * TPE) + (base + n - SLOTS + 1))
                        sp.dma_start(slot(n).rearrange("p (k n) -> p k n", k=4),
                                     ws[c // 2][bass.ds(g * EG + j, 1), c % 2].rearrange("e p k n -> p (e k) n")
                                     ).then_inc(landed[n % SLOTS], 16)

        sp.dma_start(x_tok, t["x"][0].rearrange("(t p) d -> p t d", p=P)).then_inc(x_landed, 16)
        sp.dma_start(consts[:, :], t["const_main"]).then_inc(const_landed, 16)
        sp.dma_start(rel_T, t["rel_bias_2"].rearrange("h b -> b h"), allow_slow_non_contiguous=True
                     ).then_inc(small_landed[1], 16)
        sp.dma_start(dist_hot, t["const_onehot"]).then_inc(small_landed[1], 16)
        sp.dma_start(wgate, t["mlstm_w_in"][0].rearrange("(k p) n -> p k n", p=P)[:, :, 3072:3088]
                     ).then_inc(small_landed[0], 16)
        sp.dma_start(gate_bias, t["mlstm_gate_b"][0].rearrange("a b (c o) -> (a b c) o", o=1)
                     ).then_inc(small_landed[0], 16)
        columns(T_MLSTM, t["mlstm_w_in"][0], 0, 6)
        columns(T_MLSTM + 6, t["mlstm_w_out"][0], 0, 2)
        experts(0)
        columns(T_GLA, t["gla_w_in"][0], 0, 6)
        columns(T_GLA + 6, t["gla_w_out"][0], 0, 2)
        experts(1)
        columns(T_QKV, t["w_qkv_2"][0], 0, 6)
        columns(T_WO, t["w_o_2"][0], 0, 2)
        up = t["w_up_2"][0].rearrange("(k p) (h n) -> p k h n", p=P, h=2)
        for i in range(UPT):
            n = T_UP + i
            free(n)
            dst = slot(n).rearrange("p (k h n) -> p k h n", k=KC, h=2)
            for h in range(2):
                sp.dma_start(dst[:, :, h, :], up[:, :, h, S * i:S * (i + 1)]).then_inc(landed[n % SLOTS], 16)
        down = t["w_down_2"][0].rearrange("(k p) n -> p k n", p=P)
        for i in range(N_DOWN):
            n = T_DOWN + i
            k = min(4, FB - 4 * i)
            load(n, down[:, 4 * i:4 * i + k, :], slot(n)[:, 0:k * D].rearrange("p (k n) -> p k n", k=k))

    def up_landed(n):
        twice = sum(1 for m in range(T_UP, min(n + 1, T_DOWN)) if m % SLOTS == n % SLOTS)
        return 16 * (n // SLOTS + 1 + twice)

    @block.gpsimd
    def _(pool):
        def row(dst, src, s):
            pool.dma_start(dst, src.partition_broadcast(P)).then_inc(s, 16)

        def norm_rows(g, b):
            row(gain_row, g, rows_landed)
            row(bias_row, b, rows_landed)

        nc.gpsimd.memset(ones[:, :], 1.0).then_inc(ones_ready, 1)
        nc.gpsimd.memset(v_aug[:, :, :, DV:VW], 1.0).then_inc(ones_ready, 1)
        nc.gpsimd.memset(bias_rows[:, S:WROW], -BIG).then_inc(ones_ready, 1)
        masks_f32 = acc_t[:, 0:2 * len(LEVELS) * 64]
        pool.dma_start(masks_f32, t["const_masks"]).then_inc(small_landed[2], 16)
        row(ng_t[:, :], t["mlstm_norm_g"][0], gain_landed)
        pool.dma_start(w_router, t["moe_router"].rearrange("l (k p) n -> p l k n", p=P)).then_inc(router_landed, 16)
        pool.dma_start(wglr, t["gla_w_in"][0].rearrange("(k p) n -> p k n", p=P)[:, :, 3072:3104]
                       ).then_inc(small_landed[5], 16)
        pool.wait_ge(small_landed[2], 16)
        nc.gpsimd.tensor_copy(level_masks[:, :], masks_f32).then_inc(masks_ready, 1)
        pool.wait_ge(relb_copied, 1)
        pool.wait_ge(ones_ready, 3)
        pool.dma_start(bias_dram.ap(), bias_rows).then_inc(relb_stored, 16)

        def output_gate(layer):
            pool.wait_ge(proj_act, act_count(layer, 5))
            pool.wait_ge(gain_landed, 16 * (layer + 1))
            for i in range(TT):
                last = nc.gpsimd.tensor_tensor(gate[:, i], gate[:, i], ng_t[:, :], ALU.mult)
            last.then_inc(gate_ready, 1)

        def moe_small(layer, u_moe):
            pool.wait_ge(tokens_ready, u_moe)
            norm_rows(t["ln_g"][layer, 1], t["ln_b"][layer, 1])
            for i in range(TT):
                last = nc.gpsimd.tensor_scalar(acc[:, i], x_tok[:, i], ALPHA, 0.0, ALU.mult, ALU.add)
            last.then_inc(acc_init, 1)

        output_gate(0)
        pool.wait_ge(weights_done, H)
        norm_rows(t["ln_g"][0, 0], t["ln_b"][0, 0])
        moe_small(0, U_M0)
        row(ng_t[:, :], t["gla_norm_g"][0], gain_landed)
        nc.gpsimd.memset(gate_w_sb, 0.0).then_inc(glr_zero, 1)
        pool.wait_ge(glr_zero, 1)
        for d in range(2):
            pool.dma_start(gate_w_sb[RANK * d:RANK * (d + 1), d], t["gla_gate_w"][0, d]).then_inc(small_landed[3], 16)
        pool.dma_start(gate_b_rows, t["gla_gate_b"][0].rearrange("d (n p) -> (d n) p", p=P)
                       ).then_inc(small_landed[3], 16)
        pool.wait_ge(b_ready, 1)
        for i in range(2 * (len(LEVELS) + 1)):
            d, L = i % 2, P >> (i // 2)
            b = b_t[:, d * H * S:(d + 1) * H * S].rearrange("p (n w l) -> p n w l", w=2, l=L)
            left, right = b[:, :, 0, :], b[:, :, 1, :]
            nb = H * S // (2 * L)
            border = (left[:, :, L - 1:L] if d == 0 else right[:, :, 0:1]).to_broadcast([P, nb, L])
            qs, ks = (right, left) if d == 0 else (left, right)
            if i >= 2:
                pool.wait_ge(decays_exp, i - 1)
            dq = diffs[:, d, 0].rearrange("p (n l) -> p n l", l=L)
            dk = diffs[:, d, 1].rearrange("p (n l) -> p n l", l=L)
            nc.gpsimd.tensor_tensor(dq, qs, border, ALU.subtract)
            nc.gpsimd.tensor_tensor(dk, border, ks, ALU.subtract).then_inc(diffs_done, 1)
            if i == 5:
                output_gate(1)
        pool.wait_ge(decays_exp, 2 * (len(LEVELS) + 1))
        norm_rows(t["ln_g"][1, 0], t["ln_b"][1, 0])
        moe_small(1, U_M1)
        row(attn_row, t["attn_norm_2"][0], attn_row_landed)
        for j in range(3):
            pool.dma_start(conv_rows[:, j], t["conv_w_2"][0, j].rearrange("(n p) -> n p", p=P)
                           ).then_inc(small_landed[4], 16)
        pool.dma_start(conv_rows[:, 3], t["conv_b_2"][0].rearrange("(n p) -> n p", p=P)
                       ).then_inc(small_landed[4], 16)
        row(ng_t[:, :], t["final_norm_2"], gain_landed)
        pool.wait_ge(tokens_ready, U_ATT)
        row(bias_row, t["ffn_norm_2"][0], rows_landed)
        pool.wait_ge(relb_stored, 16)
        pool.wait_ge(tr_done, 4 * (U_ATT + 1))
        for g in range(AH // 4):
            if g >= 2:
                pool.wait_ge(s_done, 4 * (g - 1))
            src = bass.AP(bias_dram, 4 * g * WROW, [[1, P], [WROW, 4], [1, S]])
            pool.dma_start(bias_flip[:, g % 2], src).then_inc(bias_landed[g % 2], 16)
        pool.wait_ge(tokens_ready, U_FFN + 2)
        pool.dma_start(out[0].rearrange("(t p) d -> p t d", p=P), acc).then_inc(out_landed, 16)
        pool.wait_ge(out_landed, 16)

    @block.tensor
    def _(pe):
        mm = nc.tensor.matmul
        turn = nc.tensor.transpose

        def transposes(src, use):
            if use == U_X0:
                pe.wait_ge(x_landed, 16)
                pe.wait_ge(const_landed, 16)
            else:
                pe.wait_ge(tokens_ready, use + (use >= U_ATT))
            for b in range(KC // 2):
                for kk in range(2):
                    k = 2 * b + kk
                    for i in range(TT):
                        last = turn(PS[b][:, kk * S + i * P:kk * S + (i + 1) * P],
                                    src[:, i, k * P:(k + 1) * P], ident)
                last.then_inc(tr_done, 1)
            pe.wait_ge(tr_act, 2 * (use + 1))
            pe.wait_ge(tr_dve, 2 * (use + 1))

        def project(n, stage, i, channel_tiles):
            b0 = 2 * (i % 2)
            arrived(pe, n + i)
            w = slot(n + i).rearrange("p (k n) -> p k n", k=KC)
            if i >= 2:
                pe.wait_ge(proj_act, act_count(stage, i - 2))
                pe.wait_ge(proj_dve, dve_count(stage, i - 2))
            if i < channel_tiles:
                for c in range(4):
                    for k in range(KC):
                        last = mm(PS[b0 + c // 2][:, (c % 2) * S:(c % 2 + 1) * S], w[:, k, c * P:(c + 1) * P],
                                  xT[:, k, :], start=(k == 0), stop=(k == KC - 1))
            else:
                for tt in range(TT):
                    for k in range(KC):
                        last = mm(PS[b0 + tt][:, :], xT[:, k, tt * P:(tt + 1) * P], w[:, k, :],
                                  start=(k == 0), stop=(k == KC - 1))
            last.then_inc(tile_used, 1)

        def out_project(n):
            for j in range(2):
                arrived(pe, n + j)
                w = slot(n + j).rearrange("p (k n) -> p k n", k=KC)
                for tt in range(TT):
                    for k in range(KC):
                        last = mm(PS[2 * j + tt][:, :], xT[:, k, tt * P:(tt + 1) * P], w[:, k, :],
                                  start=(k == 0), stop=(k == KC - 1))
                last.then_inc(tile_used, 1)

        def mlstm():
            transposes(x_tok, U_X0)
            pe.wait_ge(small_landed[1], 32)
            mm(PS[7][0:AH, 0:S], rel_T, dist_hot, start=True, stop=True).then_inc(relb_done, 1)
            pe.wait_ge(small_landed[0], 32)
            for k in range(KC):
                last = mm(PS[4][0:16, 0:S], wgate[:, k, :], xT[:, k, :], start=(k == 0), stop=(k == KC - 1))
            last.then_inc(gates_done, 1)
            pe.wait_ge(gates_biased, 1)
            for d in range(2):
                for kind in range(2):
                    c = 4 * (2 * d + kind)
                    last = mm(PS[5 + kind][0:H, d * S:(d + 1) * S], ident[0:16, c:c + H], gates_all,
                              start=True, stop=True)
            last.then_inc(gates_split, 1)
            for i in range(6):
                project(T_MLSTM, 0, i, 2)
                if i == 1:
                    pe.wait_ge(gate_rows, 1)
                    pe.wait_ge(relb_copied, 1)
                    for q, rows in enumerate((row_a, row_m)):
                        for d in range(2):
                            for tt in range(TT):
                                c = ((q * 2 + d) * 2 + tt) * H
                                last = turn(PS[7][:, c:c + H], rows[:, d * S + tt * P:d * S + (tt + 1) * P],
                                            ident[0:H, 0:H])
                    last.then_inc(gate_colsd, 1)
            pe.wait_ge(gate_scalars, 1)
            pe.wait_ge(ones_ready, 3)
            pe.wait_ge(proj_act, act_count(0, 3))
            pe.wait_ge(proj_dve, dve_count(0, 3))

            def head_scores(h):
                if h >= 1:
                    pe.wait_ge(decay_done, h)
                pick = ident[0:H, h:h + 1].to_broadcast([H, P])
                for d in range(2):
                    b = PS[4 + d]
                    for s in range(TT):
                        t0, t1 = (s, TT) if d == 0 else (0, s + 1)
                        c0 = (0, 2)[s] if d == 0 else (0, 1)[s]
                        mm(b[:, c0 * P:(c0 + t1 - t0) * P], pick, row_max[:, d * S + t0 * P:d * S + t1 * P],
                           start=True, stop=False, skip_group_check=True)
                        cm = (c0 + s - t0) * P
                        last = mm(b[:, cm:cm + P], ident, mask_after if d == 0 else mask_before,
                                  start=False, stop=True, skip_group_check=True)
                last.then_inc(mb_done, 1)
                if h >= 2:
                    pe.wait_ge(weights_done, h - 1)
                for s in range(TT):
                    last = mm(PS[6 + h % 2][:, s * S:(s + 1) * S], kT[:, h * S + s * P:h * S + (s + 1) * P],
                              qT[:, h * S:(h + 1) * S], start=True, stop=True)
                last.then_inc(scores_done, 1)

            def head_sums(h):
                pe.wait_ge(weights_done, h + 1)
                if h >= 1:
                    pe.wait_ge(head_out, h)
                w = decay[:, h % 2]
                for tt in range(TT):
                    for d in range(2):
                        srcs = range(tt + 1) if d == 0 else range(tt, TT)
                        for s in srcs:
                            c = ((0, 2)[s] + tt - s if d == 0 else (0, 1)[s] + tt) * P
                            last = mm(PS[2 * tt + d][:, 0:VW], w[:, d, c:c + P], v_aug[:, s, h, :],
                                      start=(s == srcs[0]), stop=(s == srcs[-1]))
                last.then_inc(num_done, 1)

            head_scores(0)
            for h in range(H):
                if h + 1 < H:
                    head_scores(h + 1)
                head_sums(h)
            transposes(acc, U_Y0)
            out_project(T_MLSTM + 6)

        def gla():
            transposes(x_tok, U_X1)
            pe.wait_ge(small_landed[5], 16)
            for k in range(KC):
                last = mm(PS[4][0:2 * RANK, 0:S], wglr[:, k, :], xT[:, k, :], start=(k == 0), stop=(k == KC - 1))
            last.then_inc(glr_done, 1)
            project(T_GLA, 1, 0, 2)
            pe.wait_ge(small_landed[3], 48)
            turn(PS[5][:, 0:8], gate_b_rows, ident[0:8, 0:8]).then_inc(glr_done, 1)
            pe.wait_ge(glr_copied, 2)
            for n in range(2 * H):
                last = mm(PS[4 + n // 2][:, (n % 2) * S:(n % 2 + 1) * S],
                          gate_w_sb[:, n // H, (n % H) * P:(n % H + 1) * P], glrT, start=True, stop=True)
            last.then_inc(z_done, 1)
            for i in range(1, 6):
                project(T_GLA, 1, i, 2)
            pe.wait_ge(proj_act, act_count(1, 5))
            pe.wait_ge(proj_dve, dve_count(1, 3))
            for tt in range(TT):
                for h in range(H):
                    c = h * S + tt * P
                    last = mm(PS[2 + tt][:, h * P:(h + 1) * P], kT[:, c:c + P], qT[:, c:c + P], start=True, stop=True)
                last.then_inc(diag_done, 1)
            for i in range(2 * (len(LEVELS) + 1)):
                d = i % 2
                pe.wait_ge(scaled_done, i + 1)
                if i >= 2:
                    pe.wait_ge(placed, i - 1)
                for h in range(H):
                    if i < 2:
                        last = mm(PS[d][:, h * P:(h + 1) * P], k_dec[:, d, h * S + d * P:h * S + (d + 1) * P],
                                  q_dec[:, d, h * P:(h + 1) * P], start=True, stop=True)
                        continue
                    for s in range(TT):
                        c = (s * H + h) * 64
                        last = mm(PS[d][:, c:c + 64], k_dec[:, d, h * S + s * P:h * S + (s + 1) * P],
                                  q_dec[:, d, h * P + s * 64:h * P + (s + 1) * 64], start=True, stop=True)
                last.then_inc(prod_done, 1)
            pe.wait_ge(placed, 2 * (len(LEVELS) + 1))
            for tt in range(TT):
                for h in range(H):
                    for s in range(TT):
                        last = mm(PS[2 * tt + h // 2][:, (h % 2) * DV:(h % 2 + 1) * DV],
                                  A[:, s, h, tt * P:(tt + 1) * P], v_aug[:, s, h, 0:DV],
                                  start=(s == 0), stop=(s == TT - 1))
            last.then_inc(gla_out, 1)
            transposes(acc, U_Y1)
            out_project(T_GLA + 6)

        def moe(layer, use):
            transposes(x_tok, use)
            pe.wait_ge(router_landed, 16)
            for tt in range(TT):
                for k in range(KC):
                    last = mm(PS[4][:, tt * E:(tt + 1) * E], xT[:, k, tt * P:(tt + 1) * P], w_router[:, layer, k, :],
                              start=(k == 0), stop=(k == KC - 1))
            last.then_inc(logits_done, 1)
            pe.wait_ge(aff_ready, layer + 1)
            for tt in range(TT):
                last = turn(PS[5][0:E, tt * P:(tt + 1) * P], aff[:, tt, :], ident)
            last.then_inc(affT_done, 1)
            pe.wait_ge(slots_ready, layer + 1)
            for tt in range(TT):
                last = turn(PS[6][:, tt * E:(tt + 1) * E], picked_t[0:E, tt * P:(tt + 1) * P], ident[0:E, 0:E])
            last.then_inc(slotsT_done, 1)
            pe.wait_ge(sel_ready, layer + 1)
            for g in range(NG):
                for tt in range(TT):
                    last = turn(PS[g // 2][:, (g % 2) * S + tt * P:(g % 2) * S + (tt + 1) * P],
                                selg[:, tt, g * P:(g + 1) * P], ident)
            last.then_inc(selT_done, 1)
            pe.wait_ge(selT_copied, layer + 1)
            base, n0, m0 = T_MOE[layer], E * layer, NG * layer
            with pe.Fori(0, NG) as g:
                pe.wait_ge(acc_added, g + m0)
                for k in range(KC):
                    for tt in range(TT):
                        last = mm(PS[k // 4][:, (k % 4) * P:(k % 4 + 1) * P], x_tok[:, tt, k * P:(k + 1) * P],
                                  sel[:, tt, bass.ts(g, P)], start=(tt == 0), stop=(tt == TT - 1))
                last.then_inc(xin_done, 1)
                pe.wait_ge(xin_act, g + (m0 + 1))
                pe.wait_ge(xin_dve, g + (m0 + 1))
                for j in range(EG):
                    half = (j % 2) * S

                    def tile(c):
                        n = TPE * j + c
                        pe.wait_ge(landed[n % SLOTS], g * (16 * EG * TPE // SLOTS)
                                   + 16 * ((base + n) // SLOTS + 1))
                        return slot(n).rearrange("p (k n) -> p k n", k=4)

                    def up_products(c0, bank):
                        for r in range(2):
                            w = tile(c0 + r)
                            for k in range(4):
                                for q in range(4):
                                    last = mm(bank[q * CAP:(q + 1) * CAP, half:half + S],
                                              xinT[:, 4 * r + k, j * CAP:(j + 1) * CAP],
                                              w[:, k, q * S:(q + 1) * S],
                                              start=(r == 0 and k == 0), stop=(r == 1 and k == 3),
                                              skip_group_check=True)
                            last.then_inc(tile_used, 1)

                    pe.wait_ge(silu_done, g * EG + (n0 + j + 1))
                    up_products(0, PS[2])
                    pe.wait_ge(hid_done, g * EG + (n0 + j + 1))
                    up_products(2, PS[3])
                    pe.wait_ge(hid_done, g * EG + (n0 + j + 3))
                    for c in range(2):
                        last = turn(PS[6][:, half + c * P:half + (c + 1) * P],
                                    hid[:, j % 2, c * P:(c + 1) * P], ident)
                    last.then_inc(hidT_done, 1)
                    pe.wait_ge(hidT_copied, g * EG + (n0 + j + 1))
                    pe.wait_ge(exp_act, g * EG + (n0 + j + 1))
                    pe.wait_ge(exp_dve, g * EG + (n0 + j + 1))
                    for r in range(2):
                        w = tile(4 + r)
                        for k in range(4):
                            kk = 4 * r + k
                            for i in range(2):
                                last = mm(PS[4 + i][j * CAP:(j + 1) * CAP, :],
                                          hidT[:, j % 2, kk % 2, (kk // 2) * CAP:(kk // 2 + 1) * CAP],
                                          w[:, k, i * 512:(i + 1) * 512],
                                          start=(kk == 0), stop=(kk == KC - 1), skip_group_check=True)
                        last.then_inc(tile_used, 1)
                pe.wait_ge(exp_act, g * EG + (n0 + 2 * EG))
                pe.wait_ge(exp_dve, g * EG + (n0 + 2 * EG))
                pe.wait_ge(sel_grp, g + (m0 + 1))
                for tt in range(TT):
                    for i in range(2):
                        last = mm(PS[(7, 6, 0, 1)[2 * tt + i]][:, :], selgrp_t[:, tt * P:(tt + 1) * P],
                                  exp_t[:, i * 512:(i + 1) * 512], start=True, stop=True)
                last.then_inc(comb_done, 1)

        def attention():
            transposes(acc, U_ATT)
            for i in range(6):
                project(T_QKV, 2, i, 4)
            pe.wait_ge(proj_act, act_count(2, 5))
            pe.wait_ge(proj_dve, dve_count(2, 5))

            def scores(h):
                if h >= 2:
                    pe.wait_ge(probs_exp, h - 1)
                if h % 4 == 0:
                    pe.wait_ge(bias_landed[(h // 4) % 2], 16 * (h // 8 + 1))
                b = PS[4 + h % 2]
                r = slice(AD * (h % 2), AD * (h % 2 + 1))
                bias = bias_flip[:, (h // 4) % 2, h % 4]
                mm(b[:, 0:P], flip, bias[:, P:S], start=True, stop=False, skip_group_check=True)
                mm(b[:, 0:P], aqk[r, h // 2, 0:P], aqk[r, 8 + h // 2, 0:P], start=False, stop=True,
                   skip_group_check=True)
                mm(b[:, P:P + S], flip, bias, start=True, stop=False, skip_group_check=True)
                mm(b[:, P:P + S], aqk[r, h // 2, P:S], aqk[r, 8 + h // 2, :], start=False, stop=True,
                   skip_group_check=True).then_inc(s_done, 1)

            def turn_probs(h):
                pe.wait_ge(p_ready, h + 1)
                if h >= 2:
                    pe.wait_ge(pt_copied, h - 1)
                b, pr = PS[6 + h % 2], probs[:, h % 2]
                for c in range(3):
                    last = turn(b[:, c * P:(c + 1) * P], pr[:, c * P:(c + 1) * P], ident)
                last.then_inc(pt_done, 1)

            def values(h):
                pe.wait_ge(pt_copied, h + 1)
                if h % 2 == 0 and h >= 4:
                    pe.wait_ge(o_copied, h // 2 - 1)
                r = slice(AD * (h % 2), AD * (h % 2 + 1))
                b, pT = PS[(h // 2) % 2], probsT[:, h % 2]
                mm(b[r, 0:S], av[:, 0, h * AD:(h + 1) * AD], pT[:, 0:S], start=True, stop=False,
                   skip_group_check=True)
                mm(b[r, P:S], av[:, 1, h * AD:(h + 1) * AD], pT[:, S:S + P], start=False, stop=True,
                   skip_group_check=True).then_inc(o_done, 1)

            scores(0)
            for h in range(AH):
                if h + 1 < AH:
                    scores(h + 1)
                turn_probs(h)
                if h >= 1:
                    values(h - 1)
            values(AH - 1)
            pe.wait_ge(o_copied, AH // 2)
            out_project(T_WO)

        def ffn():
            transposes(acc, U_FFN)
            pe.wait_ge(small_landed[4], 64)
            for j in range(4):
                last = turn(PS[6][:, j * 2 * FB:(j + 1) * 2 * FB], conv_rows[:, j, :], ident[0:2 * FB, 0:2 * FB])
            last.then_inc(convT_done, 1)
            for i in range(UPT):
                n = T_UP + i
                pe.wait_ge(landed[n % SLOTS], up_landed(n))
                if i >= 3:
                    pe.wait_ge(conv_done, i - 2)
                w = slot(n).rearrange("p (k n) -> p k n", k=KC)
                b0 = 2 * (i % 3)
                for c in range(4):
                    for k in range(KC):
                        last = mm(PS[b0 + c // 2][:, (c % 2) * S:(c % 2 + 1) * S], w[:, k, c * P:(c + 1) * P],
                                  xT[:, k, :], start=(k == 0), stop=(k == KC - 1))
                last.then_inc(tile_used, 1)
            pe.wait_ge(ff_ready, UPT)
            for i in range(N_DOWN):
                n = T_DOWN + i
                pe.wait_ge(landed[n % SLOTS], up_landed(n))
                w = slot(n).rearrange("p (k n) -> p k n", k=4)
                for k in range(4 * i, min(4 * i + 4, FB)):
                    for tt in range(TT):
                        for j in range(2):
                            last = mm(PS[2 * j + tt][:, :], ffh[:, k, tt * P:(tt + 1) * P],
                                      w[:, k - 4 * i, j * 512:(j + 1) * 512], start=(k == 0), stop=(k == FB - 1))
                last.then_inc(tile_used, 1)

        mlstm()
        moe(0, U_M0)
        gla()
        moe(1, U_M1)
        attention()
        ffn()

    @block.scalar
    def _(act):
        f = nc.scalar.activation
        chain = Chain(act, act_seq)
        link = chain.link

        def copy_transposes(use):
            for b in (0, 2):
                act.wait_ge(tr_done, 4 * use + b + 1)
                f(xT_t[:, b * 512:(b + 1) * 512], PS[b][:, :], ACT.Copy).then_inc(tr_act, 1)

        def take_projection(stage, n, i):
            act.wait_ge(tile_used, n + i + 1)
            b0 = 2 * (i % 2)
            if stage == 2:
                if i < 4:
                    dst = aqk_t[:, (4 * i) * S:(4 * i + 2) * S]
                    last = f(dst, PS[b0][:, :], ACT.Copy, scale=(AD ** -0.5 if i < 2 else 1.0))
                else:
                    last = f(av[:, 0, (i - 4) * 512:(i - 3) * 512], PS[b0][:, :], ACT.Copy)
            elif i < 2:
                last = f(qkT_t[:, i * H * S:i * H * S + 512], PS[b0][:, :], ACT.Copy,
                         scale=(DK ** -0.5 if i == 0 else 1.0))
            elif i < 4:
                last = f(v_aug[:, 0, 2 * (i - 2):2 * (i - 1), 0:DV],
                         PS[b0][:, :].rearrange("p (h w) -> p h w", w=DV), ACT.Copy)
            else:
                fn = ACT.Sigmoid if stage == 0 else ACT.Silu
                for tt in range(TT):
                    last = f(gate[:, tt, (i - 4) * 512:(i - 3) * 512], PS[b0 + tt][:, :], fn)
            last.then_inc(proj_act, 1)

        def root(var_sem, sd_sem, count, width):
            act.wait_ge(var_sem, count)
            f(spread[:, 0:width], spread[:, 0:width], ACT.Sqrt).then_inc(sd_sem, 1)

        def mlstm():
            copy_transposes(U_X0)
            act.wait_ge(relb_done, 1)
            f(bias_rows[:, 0:S], PS[7][0:AH, 0:S], ACT.Copy).then_inc(relb_copied, 1)
            act.wait_ge(gates_done, 1)
            f(gates_all, PS[4][0:16, 0:S], ACT.Identity, bias=gate_bias).then_inc(gates_biased, 1)
            act.wait_ge(gates_split, 1)
            link(f(row_soft, PS[6][0:H, :], ACT.Abs))
            link(f(row_soft, row_soft, ACT.Exp, scale=-1.0))
            f(row_soft, row_soft, ACT.Ln, bias=1.0).then_inc(gate_soft, 1)
            for i in range(6):
                take_projection(0, T_MLSTM, i)
                if i == 1:
                    act.wait_ge(gate_colsd, 1)
                    f(a_cols, PS[7][:, 0:16], ACT.Copy)
                    link(f(floor_cols, PS[7][:, 16:32], ACT.Exp, scale=-1.0))
                    act.sem_inc(gate_scalars, 1)
            act.wait_ge(relb_stored, 16)
            for h in range(H):
                act.wait_ge(mb_done, h + 1)
                if h >= 2:
                    act.wait_ge(num_done, h - 1)
                w = decay[:, h % 2]
                for d in range(2):
                    for s in range(TT):
                        c0, c1 = ((0, 256), (256, 384))[s] if d == 0 else ((0, 128), (128, 384))[s]
                        col = (d * 2 + s) * H + h
                        last = f(w[:, d, c0:c1], PS[4 + d][:, c0:c1], ACT.Exp, bias=a_cols[:, col:col + 1],
                                 scale=-1.0)
                last.then_inc(decay_done, 1)
            root(hn_var, hn_sd, 1, 2 * H)
            copy_transposes(U_Y0)
            root(ln_var, ln_sd, 1, TT)

        def gla():
            copy_transposes(U_X1)
            act.wait_ge(glr_done, 1)
            f(glrT, PS[4][0:2 * RANK, 0:S], ACT.Copy).then_inc(glr_copied, 1)
            take_projection(1, T_GLA, 0)
            act.wait_ge(glr_done, 2)
            f(gate_b_cols, PS[5][:, 0:8], ACT.Copy).then_inc(glr_copied, 1)
            act.wait_ge(z_ready, 1)
            link(f(acc_t[:, :], b_t, ACT.Abs))
            link(f(acc_t[:, :], acc_t[:, :], ACT.Exp, scale=-1.0))
            f(acc_t[:, :], acc_t[:, :], ACT.Ln, bias=1.0).then_inc(z_soft, 1)
            for i in range(1, 6):
                take_projection(1, T_GLA, i)
            for i in range(2 * (len(LEVELS) + 1)):
                d = i % 2
                act.wait_ge(diffs_done, i + 1)
                if i >= 2:
                    act.wait_ge(scaled_done, i - 1)
                f(PS[4 + 2 * d][:, :], diffs[:, d, 0], ACT.Exp, scale=1.0 / GLA_TAU)
                f(PS[5 + 2 * d][:, :], diffs[:, d, 1], ACT.Exp, scale=1.0 / GLA_TAU).then_inc(decays_exp, 1)
            root(hn_var, hn_sd, 2, 2 * H)
            copy_transposes(U_Y1)
            root(ln_var, ln_sd, 3, TT)

        def moe(layer, use):
            copy_transposes(use)
            act.wait_ge(router_max, layer + 1)
            for tt in range(TT):
                last = f(aff[:, tt, :], PS[4][:, tt * E:(tt + 1) * E], ACT.Exp, bias=row_max_r[:, tt:tt + 1],
                         accum_out=row_sum_r[:, tt:tt + 1])
            last.then_inc(aff_exp, 1)
            act.wait_ge(selT_done, layer + 1)
            f(selgT_t[:, 0:512], PS[0][:, :], ACT.Copy)
            f(selgT_t[:, 512:1024], PS[1][:, :], ACT.Copy).then_inc(selT_copied, 1)
            base, n0, m0 = T_MOE[layer], E * layer, NG * layer
            with act.Fori(0, NG) as g:
                act.wait_ge(xin_done, g + (m0 + 1))
                f(xin_t[:, 0:512], PS[0][:, :], ACT.Copy).then_inc(xin_act, 1)
                for j in range(EG):
                    half = (j % 2) * S
                    act.wait_ge(tile_used, g * (EG * TPE) + (base + TPE * j + 2))
                    act.wait_ge(hid_done, g * EG + (n0 + j + 1))
                    f(silu_g[:, j % 2], PS[2][:, half:half + S], ACT.Silu).then_inc(silu_done, 1)
                    act.wait_ge(hidT_done, g * EG + (n0 + j + 1))
                    f(hidT_t[:, half:half + S], PS[6][:, half:half + S], ACT.Copy).then_inc(hidT_copied, 1)
                    act.wait_ge(tile_used, g * (EG * TPE) + (base + TPE * j + 6))
                    act.wait_ge(comb_done, g + m0)
                    r = slice(j * CAP, (j + 1) * CAP)
                    f(exp_t[r, 0:512], PS[4][r, :], ACT.Copy).then_inc(exp_act, 1)
            root(ln_var, ln_sd, 2 * layer + 2, TT)

        def rms(u, src):
            act.wait_ge(x_sum, u)
            for tt in range(TT):
                last = f(acc[:, tt], src[:, tt], ACT.Square, accum_out=square_sum[:, tt:tt + 1])
            last.then_inc(rms_sq, 1)
            root(rms_var, rms_sd, u, TT)

        def attention():
            rms(1, x_tok)
            copy_transposes(U_ATT)
            for i in range(6):
                take_projection(2, T_QKV, i)

            def exps(h):
                act.wait_ge(max_done, h + 1)
                if h >= 2:
                    act.wait_ge(pt_done, h - 1)
                b, c = PS[4 + h % 2], 2 * (h % 2)
                f(probs[:, h % 2, 0:P], b[:, 0:P], ACT.Exp, bias=neg_max[:, c:c + 1],
                  accum_out=prob_sum[:, c:c + 1])
                f(probs[:, h % 2, P:P + S], b[:, P:P + S], ACT.Exp, bias=neg_max[:, c + 1:c + 2],
                  accum_out=prob_sum[:, c + 1:c + 2]).then_inc(probs_exp, 1)

            exps(0)
            for h in range(AH):
                if h + 1 < AH:
                    exps(h + 1)
                act.wait_ge(pt_done, h + 1)
                if h >= 2:
                    act.wait_ge(o_done, h - 1)
                f(probsT[:, h % 2], PS[6 + h % 2][:, 0:3 * P], ACT.Copy).then_inc(pt_copied, 1)

        def ffn():
            rms(2, x_tok)
            copy_transposes(U_FFN)
            act.wait_ge(convT_done, 1)
            f(convw_t, PS[6][:, 0:8 * FB], ACT.Copy).then_inc(convT_copied, 1)
            act.wait_ge(convT_copied, 1)

            def taps(i):
                act.wait_ge(tile_used, T_UP + i + 1)
                if i >= 2:
                    act.wait_ge(ff_ready, i - 1)
                for c in range(4):
                    n = 2 * i + c % 2 + FB * (c // 2)
                    last = f(conv[:, i % 2, c], PS[2 * (i % 3) + c // 2][:, (c % 2) * S:(c % 2 + 1) * S],
                             ACT.Identity, scale=conv_cols[:, 2, n:n + 1], bias=conv_cols[:, 3, n:n + 1])
                last.then_inc(taps_done, 1)

            taps(0)
            for i in range(UPT):
                if i + 1 < UPT:
                    taps(i + 1)
                act.wait_ge(conv_done, i + 1)
                f(conv[:, i % 2, 0:2], conv[:, i % 2, 0:2], ACT.Silu).then_inc(ff_silu, 1)
            rms(3, x_tok)

        act.sem_inc(silu_done, 2)
        act.sem_inc(exp_act, EG)
        mlstm()
        moe(0, U_M0)
        gla()
        moe(1, U_M1)
        attention()
        ffn()

    @block.vector
    def _(dve):
        v = nc.vector
        chain = Chain(dve, dve_seq)
        link = chain.link

        def copy_transposes(use):
            for b in (1, 3):
                dve.wait_ge(tr_done, 4 * use + b + 1)
                v.tensor_copy(xT_t[:, b * 512:(b + 1) * 512], PS[b][:, :]).then_inc(tr_dve, 1)

        def take_projection(stage, n, i):
            dve.wait_ge(tile_used, n + i + 1)
            b = PS[2 * (i % 2) + 1]
            if stage == 2:
                if i < 4:
                    last = v.tensor_scalar(aqk_t[:, (4 * i + 2) * S:(4 * i + 4) * S], b[:, :],
                                           AD ** -0.5 if i < 2 else 1.0, None, ALU.mult)
                else:
                    last = v.tensor_copy(av[:, 1, (i - 4) * 512:(i - 3) * 512], b[:, :])
            elif i < 2:
                last = v.tensor_scalar(qkT_t[:, i * H * S + 512:(i + 1) * H * S], b[:, :],
                                       DK ** -0.5 if i == 0 else 1.0, None, ALU.mult)
            else:
                last = v.tensor_copy(v_aug[:, 1, 2 * (i - 2):2 * (i - 1), 0:DV],
                                     b[:, :].rearrange("p (h w) -> p h w", w=DV))
            last.then_inc(proj_dve, 1)

        def head_norm(layer):
            a = acc_t[:, :].rearrange("p (n w) -> p n w", w=DV)
            for n in range(2 * H):
                last = v.bn_stats(stats[:, n], a[:, n])
            link(last)
            for n in range(2 * H):
                last = v.bn_aggr(meanvar[:, n], stats[:, n])
            link(last)
            v.tensor_scalar(spread, meanvar[:, :, 1], LN_EPS, None, ALU.add).then_inc(hn_var, 1)
            dve.wait_ge(hn_sd, layer + 1)
            link(v.reciprocal(inv_spread, spread))
            for n in range(2 * H):
                last = v.tensor_scalar(a[:, n], a[:, n], meanvar[:, n, 0:1], inv_spread[:, n:n + 1],
                                       ALU.subtract, ALU.mult)
            link(last)
            dve.wait_ge(gate_ready, layer + 1)
            v.tensor_tensor(acc_t[:, :], acc_t[:, :], gate_t, ALU.mult).then_inc(tokens_ready, 1)

        def layer_norm(use):
            for n in range(2 * TT):
                last = v.bn_stats(stats[:, n], acc_t[:, n * 512:(n + 1) * 512])
            link(last)
            for tt in range(TT):
                last = v.bn_aggr(meanvar[:, tt], stats[:, 2 * tt:2 * tt + 2].rearrange("p n s -> p (n s)"))
            link(last)
            v.tensor_scalar(spread[:, 0:TT], meanvar[:, 0:TT, 1], LN_EPS, None, ALU.add).then_inc(ln_var, 1)
            dve.wait_ge(ln_sd, use + 1)
            link(v.reciprocal(inv_spread[:, 0:TT], spread[:, 0:TT]))
            for tt in range(TT):
                last = v.tensor_scalar(x_tok[:, tt], acc[:, tt], meanvar[:, tt, 0:1], inv_spread[:, tt:tt + 1],
                                       ALU.subtract, ALU.mult)
            link(last)
            dve.wait_ge(rows_landed, 32 * (use + 1))
            link(v.tensor_tensor(x_tok, x_tok, gain_row.unsqueeze(1).to_broadcast([P, TT, D]), ALU.mult))
            v.tensor_tensor(x_tok, x_tok, bias_row.unsqueeze(1).to_broadcast([P, TT, D]), ALU.add
                            ).then_inc(tokens_ready, 1)

        def add_residual(n):
            for j in range(2):
                dve.wait_ge(tile_used, n + j + 1)
                for tt in range(TT):
                    last = v.scalar_tensor_tensor(acc[:, tt, j * 512:(j + 1) * 512],
                                                  x_tok[:, tt, j * 512:(j + 1) * 512], ALPHA, PS[2 * j + tt][:, :],
                                                  ALU.mult, ALU.add)
            link(last)

        def mlstm():
            copy_transposes(U_X0)
            dve.wait_ge(gates_split, 1)
            fg, ig = PS[6][0:H, :], PS[5][0:H, :]
            dve.wait_ge(gate_soft, 1)
            link(v.scalar_tensor_tensor(row_m, fg, 0.0, row_soft, ALU.min, ALU.subtract))
            dve.wait_ge(ones_ready, 1)
            one = ones[0:H, 0:1].to_broadcast([H, S])

            def along(ap, d):
                r = ap[:, d * S:(d + 1) * S]
                return r if d == 0 else r[:, ::-1]

            for d in range(2):
                last = v.tensor_tensor_scan(along(row_b, d), one, along(row_m, d), 0.0, ALU.mult, ALU.add)
            link(last)
            link(v.tensor_tensor(row_a, ig, row_b, ALU.subtract))
            for d in range(2):
                last = v.tensor_tensor_scan(along(row_max, d), one, along(row_a, d), 0.0, ALU.mult, ALU.max)
            link(last)
            v.tensor_tensor(row_m, row_b, row_max, ALU.add).then_inc(gate_rows, 1)
            for i in range(4):
                take_projection(0, T_MLSTM, i)

            def weigh(h):
                dve.wait_ge(decay_done, h + 1)
                dve.wait_ge(scores_done, h + 1)
                w, sc = decay[:, h % 2], PS[6 + h % 2]
                for d, c, n, q in ((0, 0, 256, 0), (0, 256, 128, 384), (1, 0, 128, 0), (1, 128, 256, 256)):
                    last = v.tensor_tensor(w[:, d, c:c + n], w[:, d, c:c + n], sc[:, q:q + n], ALU.mult)
                last.then_inc(weights_done, 1)

            def take_head(h):
                dve.wait_ge(num_done, h + 1)
                for o in range(4):
                    last = v.tensor_reduce(den[:, o:o + 1], PS[o][:, DV:VW], AX.X, ALU.max,
                                           apply_absolute_value=True)
                link(last)
                floor = floor_cols.rearrange("p (d t h) -> p t d h", d=2, t=TT)[:, :, :, h]
                dens = den.rearrange("p (t d) -> p t d", t=TT)
                link(v.tensor_tensor(dens, dens, floor, ALU.max))
                link(v.reciprocal(inv_den, den))
                for tt in range(TT):
                    last = v.tensor_scalar(acc[:, tt, h * DV:(h + 1) * DV], PS[2 * tt][:, 0:DV],
                                           inv_den[:, 2 * tt:2 * tt + 1], None, ALU.mult)
                link(last)
                for tt in range(TT):
                    last = v.scalar_tensor_tensor(acc[:, tt, h * DV:(h + 1) * DV], PS[2 * tt + 1][:, 0:DV],
                                                  inv_den[:, 2 * tt + 1:2 * tt + 2], acc[:, tt, h * DV:(h + 1) * DV],
                                                  ALU.mult, ALU.add)
                last.then_inc(head_out, 1)

            dve.wait_ge(gate_scalars, 1)
            dve.wait_ge(masks_ready, 1)
            weigh(0)
            for h in range(H):
                if h + 1 < H:
                    weigh(h + 1)
                take_head(h)
            dve.wait_ge(head_out, H)
            head_norm(0)
            copy_transposes(U_Y0)
            add_residual(T_MLSTM + 6)
            layer_norm(0)

        def gla():
            copy_transposes(U_X1)
            take_projection(1, T_GLA, 0)
            dve.wait_ge(z_done, 1)
            dve.wait_ge(glr_copied, 2)
            for n in range(2 * H):
                last = v.tensor_scalar(b_cum[:, n], PS[4 + n // 2][:, (n % 2) * S:(n % 2 + 1) * S],
                                       gate_b_cols[:, n:n + 1], None, ALU.add)
            last.then_inc(z_ready, 1)
            dve.wait_ge(z_soft, 1)
            link(v.scalar_tensor_tensor(acc_t[:, :], b_t, 0.0, acc_t[:, :], ALU.min, ALU.subtract))
            for n in range(2 * H):
                o, i = b_cum[:, n], acc_t[:, n * S:(n + 1) * S]
                if n >= H:
                    o, i = o[:, ::-1], i[:, ::-1]
                last = v.tensor_tensor_scan(o, ones[:, 0:1].to_broadcast([P, S]), i, 0.0, ALU.mult, ALU.add)
            last.then_inc(b_ready, 1)
            dve.wait_ge(b_ready, 1)
            for i in range(1, 4):
                take_projection(1, T_GLA, i)
            dve.wait_ge(proj_act, act_count(1, 3))
            dve.wait_ge(proj_dve, dve_count(1, 3))

            def scale(i):
                d, L = i % 2, P >> (i // 2)
                dve.wait_ge(decays_exp, i + 1)
                if i >= 2:
                    dve.wait_ge(prod_done, i - 1)
                qv = qT.rearrange("p (n w l) -> p n w l", w=2, l=L)
                kv = kT.rearrange("p (n w l) -> p n w l", w=2, l=L)
                ko = k_dec[:, d].rearrange("p (n w l) -> p n w l", w=2, l=L)
                hq, hk = (1, 0) if d == 0 else (0, 1)
                v.tensor_tensor(q_dec[:, d].rearrange("p (n l) -> p n l", l=L), qv[:, :, hq, :],
                                PS[4 + 2 * d][:, :].rearrange("p (n l) -> p n l", l=L), ALU.mult)
                v.tensor_tensor(ko[:, :, hk, :], kv[:, :, hk, :],
                                PS[5 + 2 * d][:, :].rearrange("p (n l) -> p n l", l=L), ALU.mult
                                ).then_inc(scaled_done, 1)

            def place(i):
                d, L = i % 2, P >> (i // 2)
                dve.wait_ge(prod_done, i + 1)
                if i >= 1:
                    dve.wait_ge(placed, i)
                if i < 2:
                    last = v.tensor_copy(A[:, d, :, (1 - d) * P:(2 - d) * P],
                                         PS[d][:, :].rearrange("p (h n) -> p h n", h=H))
                else:
                    mask = level_masks[:, (d * len(LEVELS) + i // 2 - 1) * 64:(d * len(LEVELS) + i // 2) * 64]
                    for s in range(TT):
                        to = A[:, s, :, s * P:(s + 1) * P].rearrange("p h (n w l) -> p h n w l", w=2, l=L)
                        src = PS[d][:, s * H * 64:(s + 1) * H * 64]
                        pick = mask.rearrange("p (n l) -> p n l", l=L).unsqueeze(1)
                        last = v.copy_predicated(to[:, :, :, 1 - d, :], pick.to_broadcast([P, H, 64 // L, L]),
                                                 src.rearrange("p (h n l) -> p h n l", h=H, l=L))
                last.then_inc(placed, 1)

            scale(0)
            scale(1)
            for tt in range(TT):
                dve.wait_ge(diag_done, tt + 1)
                last = v.scalar_tensor_tensor(A[:, tt, :, tt * P:(tt + 1) * P],
                                              PS[2 + tt][:, :].rearrange("p (h n) -> p h n", h=H), 2.0,
                                              ident.unsqueeze(1).to_broadcast([P, H, P]), ALU.mult, ALU.mult)
            link(last)
            n_levels = 2 * (len(LEVELS) + 1)
            for i in range(n_levels):
                place(i)
                if i + 2 < n_levels:
                    scale(i + 2)
            dve.wait_ge(gla_out, 1)
            for b in range(4):
                last = v.tensor_copy(acc_t[:, b * 512:(b + 1) * 512], PS[b][:, :])
            link(last)
            head_norm(1)
            copy_transposes(U_Y1)
            add_residual(T_GLA + 6)
            layer_norm(2)

        def moe(layer, use):
            copy_transposes(use)
            dve.wait_ge(logits_done, layer + 1)
            v.tensor_reduce(row_max_r, PS[4][:, 0:TT * E].rearrange("p (t e) -> p t e", t=TT), AX.X, ALU.max,
                            negate=True).then_inc(router_max, 1)
            dve.wait_ge(aff_exp, layer + 1)
            link(v.reciprocal(inv_sum_r, row_sum_r))
            for tt in range(TT):
                last = v.tensor_scalar(aff[:, tt, :], aff[:, tt, :], inv_sum_r[:, tt:tt + 1], None, ALU.mult)
            last.then_inc(aff_ready, 1)
            dve.wait_ge(affT_done, layer + 1)
            work, pick, count = affT_t[0:E, :], picked_t[0:E, :], work_t[0:E, :]
            link(v.tensor_copy(work, PS[5][0:E, 0:S]))
            for r in range(CAP // 8):
                top = top8[:, 8 * r:8 * r + 8]
                link(v.max(top, work))
                link(v.match_replace(work, top, work, -1.0))
            link(v.tensor_scalar(pick, work, 0.0, None, ALU.is_lt))
            link(v.tensor_tensor_scan(count, ones[0:E, 0:1].to_broadcast([E, S]), pick, 0.0, ALU.mult, ALU.add))
            v.tensor_tensor(pick, pick, count, ALU.mult).then_inc(slots_ready, 1)
            dve.wait_ge(slotsT_done, layer + 1)
            for tt in range(TT):
                last = v.tensor_tensor(sel[:, tt].rearrange("p (e c) -> p e c", c=CAP),
                                       slot_ids.unsqueeze(1).to_broadcast([P, E, CAP]),
                                       PS[6][:, tt * E:(tt + 1) * E].unsqueeze(2).to_broadcast([P, E, CAP]),
                                       ALU.is_equal)
            link(last)
            for tt in range(TT):
                last = v.tensor_tensor(selg[:, tt].rearrange("p (e c) -> p e c", c=CAP),
                                       sel[:, tt].rearrange("p (e c) -> p e c", c=CAP),
                                       aff[:, tt, :].unsqueeze(2).to_broadcast([P, E, CAP]), ALU.mult)
            last.then_inc(sel_ready, 1)
            dve.wait_ge(selT_copied, layer + 1)
            dve.wait_ge(acc_init, layer + 1)
            base, n0, m0 = T_MOE[layer], E * layer, NG * layer
            with dve.Fori(0, NG) as g:
                dve.wait_ge(xin_done, g + (m0 + 1))
                v.tensor_copy(xin_t[:, 512:1024], PS[1][:, :]).then_inc(xin_dve, 1)
                dve.wait_ge(comb_done, g + m0)
                v.tensor_scalar(selgrp_t, selgT_t[:, bass.ts(g, S)], 1.0, None, ALU.mult).then_inc(sel_grp, 1)
                for j in range(EG):
                    half = (j % 2) * S
                    dve.wait_ge(silu_done, g * EG + (n0 + j + 3))
                    dve.wait_ge(tile_used, g * (EG * TPE) + (base + TPE * j + 4))
                    v.tensor_tensor(hid[:, j % 2], silu_g[:, j % 2], PS[3][:, half:half + S], ALU.mult
                                    ).then_inc(hid_done, 1)
                    dve.wait_ge(tile_used, g * (EG * TPE) + (base + TPE * j + 6))
                    r = slice(j * CAP, (j + 1) * CAP)
                    v.tensor_copy(exp_t[r, 512:1024], PS[5][r, :]).then_inc(exp_dve, 1)
                dve.wait_ge(comb_done, g + (m0 + 1))
                dve.wait_ge(acc_added, g + m0)
                for tt in range(TT):
                    for j in range(2):
                        dst = acc[:, tt, j * 512:(j + 1) * 512]
                        last = v.tensor_tensor(dst, dst, PS[(7, 6, 0, 1)[2 * tt + j]][:, :], ALU.add)
                last.then_inc(acc_added, 1)
            dve.wait_ge(acc_added, m0 + NG)
            layer_norm(2 * layer + 1)

        def rms(u, src, dst, gain, gain_sem, gain_count):
            dve.wait_ge(rms_sq, u)
            v.tensor_scalar(spread[:, 0:TT], square_sum, 1.0 / D, RMS_EPS, ALU.mult, ALU.add).then_inc(rms_var, 1)
            dve.wait_ge(rms_sd, u)
            link(v.reciprocal(inv_spread[:, 0:TT], spread[:, 0:TT]))
            dve.wait_ge(gain_sem, gain_count)
            for tt in range(TT):
                last = v.scalar_tensor_tensor(dst[:, tt], src[:, tt], inv_spread[:, tt:tt + 1], gain,
                                              ALU.mult, ALU.mult)
            last.then_inc(tokens_ready, 1)

        def add_to_stream(n):
            dve.wait_ge(tile_used, n + 1)
            for j in range(2):
                for tt in range(TT):
                    dst = x_tok[:, tt, j * 512:(j + 1) * 512]
                    last = v.tensor_tensor(dst, dst, PS[2 * j + tt][:, :], ALU.add)
            last.then_inc(x_sum, 1)

        def attention():
            dve.wait_ge(tokens_ready, U_ATT)
            dve.sem_inc(x_sum, 1)
            rms(1, x_tok, acc, attn_row, attn_row_landed, 16)
            copy_transposes(U_ATT)
            for i in range(6):
                take_projection(2, T_QKV, i)

            def maxima(h):
                dve.wait_ge(s_done, h + 1)
                b, c = PS[4 + h % 2], 2 * (h % 2)
                v.tensor_reduce(neg_max[:, c:c + 1], b[:, 0:P], AX.X, ALU.max, negate=True)
                v.tensor_reduce(neg_max[:, c + 1:c + 2], b[:, P:P + S], AX.X, ALU.max, negate=True
                                ).then_inc(max_done, 1)

            maxima(0)
            for h in range(AH):
                if h + 1 < AH:
                    maxima(h + 1)
                dve.wait_ge(probs_exp, h + 1)
                c, pr = 2 * (h % 2), probs[:, h % 2]
                link(v.reciprocal(inv_prob[:, c:c + 2], prob_sum[:, c:c + 2]))
                v.tensor_scalar(pr[:, 0:P], pr[:, 0:P], inv_prob[:, c:c + 1], None, ALU.mult)
                v.tensor_scalar(pr[:, P:P + S], pr[:, P:P + S], inv_prob[:, c + 1:c + 2], None, ALU.mult
                                ).then_inc(p_ready, 1)
                if h % 2 == 0 and h >= 2:
                    copy_heads(h // 2 - 1)
            copy_heads(AH // 2 - 1)
            add_to_stream(T_WO + 1)

        def copy_heads(pair):
            dve.wait_ge(o_done, 2 * pair + 2)
            v.tensor_copy(xT[:, pair, :], PS[pair % 2][:, 0:S]).then_inc(o_copied, 1)

        def ffn():
            rms(2, x_tok, acc, bias_row, rows_landed, 32 * 4 + 16)
            copy_transposes(U_FFN)
            dve.wait_ge(convT_copied, 1)

            def convolve(i):
                dve.wait_ge(taps_done, i + 1)
                for back in (1, 2):
                    for c in range(4):
                        n = 2 * i + c % 2 + FB * (c // 2)
                        u = PS[2 * (i % 3) + c // 2][:, (c % 2) * S:(c % 2 + 1) * S - back]
                        dst = conv[:, i % 2, c, back:S]
                        last = v.scalar_tensor_tensor(dst, u, conv_cols[:, 2 - back, n:n + 1], dst, ALU.mult, ALU.add)
                    if back == 1:
                        link(last)
                last.then_inc(conv_done, 1)

            convolve(0)
            for i in range(UPT):
                if i + 1 < UPT:
                    convolve(i + 1)
                dve.wait_ge(ff_silu, i + 1)
                dve.wait_ge(conv_done, i + 1)
                v.tensor_tensor(ffh[:, 2 * i:2 * i + 2, :], conv[:, i % 2, 0:2], conv[:, i % 2, 2:4], ALU.mult
                                ).then_inc(ff_ready, 1)
            add_to_stream(T_DOWN + N_DOWN - 1)
            rms(3, x_tok, acc, ng_t[:, :], gain_landed, 48)

        dve.sem_inc(hid_done, 2)
        dve.sem_inc(exp_dve, EG)
        mlstm()
        moe(0, U_M0)
        gla()
        moe(1, U_M1)
        attention()
        ffn()


_INS = ["x", "mlstm_w_in", "mlstm_gate_b", "mlstm_norm_g", "mlstm_w_out", "gla_w_in", "gla_gate_w",
        "gla_gate_b", "gla_norm_g", "gla_w_out", "moe_router", "moe_w_gate", "moe_w_up", "moe_w_down",
        "ln_g", "ln_b", "attn_norm_2", "w_qkv_2", "w_o_2", "rel_bias_2", "ffn_norm_2", "w_up_2",
        "conv_w_2", "conv_b_2", "w_down_2", "final_norm_2"]


def kernel(**inputs):
    import concourse.bacc as bacc
    from concourse.bass_utils import run_bass_kernel_spmd

    nc = bacc.Bacc("TRN2", target_bir_lowering=False, num_devices=1)
    main, masks, onehot = constants()
    arrays = {name: np.ascontiguousarray(inputs[name]) for name in _INS}
    arrays |= {"const_main": main, "const_masks": masks, "const_onehot": onehot}
    tensors = {name: nc.dram_tensor(f"in_{name}", a.shape, mybir.dt.from_np(a.dtype), kind="ExternalInput").ap()
               for name, a in arrays.items()}
    out = nc.dram_tensor("out_x", (1, S, D), F32, kind="ExternalOutput").ap()
    build(nc, tensors, out)
    r = run_bass_kernel_spmd(nc, [{f"in_{name}": a for name, a in arrays.items()}], core_ids=[0])
    return r.results[0]["out_x"]
```

```python
import math
from contextlib import ExitStack

import numpy as np
import concourse.bass as bass
from concourse import mybir

ALU = mybir.AluOpType
ACT = mybir.ActivationFunctionType
AX = mybir.AxisListType
F32 = mybir.dt.float32
U8 = mybir.dt.uint8

P = 128
S = 256
TT = S // P
D = 1024
KC = D // P
DEPTH = 2
ALPHA = (2 * DEPTH) ** 0.25
LN_EPS = 1e-5
RMS_EPS = 1e-6
BIG = 1e30

H = 4
DK = 128
DV = 256
VW = DV + 1
GLA_TAU = 16.0
RANK = 16

E = 16
CAP = 2 * S // E
EG = P // CAP
NG = E // EG

AH = 16
AD = 64
BUCKETS = 32
MAXDIST = 128
FF = 2816
FB = FF // P
UPT = FF // S

SLOTS = 8
TILE = 4096
TPE = 6
T_MLSTM = 0
T_MOE = [8, 112]
T_GLA = 104
T_QKV = 208
T_WO = 214
T_UP = 216
T_DOWN = T_UP + UPT
N_DOWN = (FB + 3) // 4
LEVELS = [64, 32, 16, 8, 4, 2, 1]
WROW = 3 * P


def constants():
    i = np.arange(P)
    ident = np.eye(P, dtype=np.float32)
    flip = ident[::-1].copy()
    after = np.where(i[:, None] > i[None, :], BIG, 0).astype(np.float32)
    before = np.where(i[:, None] < i[None, :], BIG, 0).astype(np.float32)
    slots = np.tile(np.arange(1, CAP + 1, dtype=np.float32), (P, 1))
    n = np.arange(DEPTH * E)
    logit_of = (i[:, None] % (DEPTH * E) == n[None, :]).astype(np.float32)
    main = np.concatenate([ident, flip, after, before, slots, logit_of], 1)
    n = np.arange(64)
    masks = np.zeros((P, 2, len(LEVELS), 64), np.float32)
    for lv, L in enumerate(LEVELS):
        same = (i[:, None] // (2 * L)) == (n[None, :] // L)
        left = ((i % (2 * L)) < L)[:, None]
        masks[:, 0, lv] = same & left
        masks[:, 1, lv] = same & ~left
    dist = np.arange(S)[::-1]
    half = BUCKETS // 2
    nf = np.maximum(dist, 1).astype(np.float32)
    large = half + (np.log(nf / np.float32(half)) / np.float32(math.log(MAXDIST / half))
                    * np.float32(BUCKETS - half)).astype(np.int32)
    bucket = np.where(dist < half, dist, np.minimum(large, BUCKETS - 1))
    onehot = (np.arange(BUCKETS)[:, None] == bucket[None, :]).astype(np.float32)
    return main, masks.reshape(P, -1), onehot


def build(nc, t, out):
    with ExitStack() as ctx:
        build_in(nc, t, out, ctx)


def build_in(nc, t, out, ctx):
    def sem(name):
        return ctx.enter_context(nc.semaphore(name))

    def sbuf(name, cols, dt=F32):
        return ctx.enter_context(nc.sbuf_tensor(name, [P, cols], dt))

    ring = sbuf("weight_ring", SLOTS * TILE)
    consts = sbuf("consts", 4 * P + CAP + DEPTH * E)
    ident = consts[:, 0:P]
    flip = consts[:, P:2 * P]
    mask_after = consts[:, 2 * P:3 * P]
    mask_before = consts[:, 3 * P:4 * P]
    slot_ids = consts[:, 4 * P:4 * P + CAP]
    logit_of = consts[:, 4 * P + CAP:4 * P + CAP + DEPTH * E]
    ones = sbuf("ones", 8)
    ln_eps, rms_eps = ones[:, 1:2], ones[:, 2:3]
    router_t = sbuf("router", DEPTH * KC * E)
    level_masks = sbuf("level_masks", 2 * len(LEVELS) * 64, U8)
    x_tok_t = sbuf("x_tok", TT * D)
    xT_t = sbuf("xT", KC * S)
    acc_t = sbuf("acc", TT * D)
    gb_t = sbuf("norm_rows", 2 * D)
    ng_t = sbuf("head_gain", D)
    small = sbuf("small", 256)
    wglr_t = sbuf("gla_gate_columns", KC * 2 * RANK)
    room = sbuf("phase_room", 9600)

    x_tok = x_tok_t[:, :].rearrange("p (t d) -> p t d", t=TT)
    acc = acc_t[:, :].rearrange("p (t d) -> p t d", t=TT)
    xT = xT_t[:, :].rearrange("p (k s) -> p k s", k=KC)
    gain_row = gb_t[:, 0:D]
    bias_row = gb_t[:, D:2 * D]

    def rooms(*sizes):
        at, got = 0, []
        for n in sizes:
            got.append(room[:, at:at + n])
            at += n
        assert at <= 9600, at
        return got

    stats = small[:, 0:48].rearrange("p (n s) -> p n s", s=6)
    meanvar = small[:, 48:64].rearrange("p (n s) -> p n s", s=2)
    inv_spread = small[:, 72:80]
    deviation = small[:, 64:72]

    qkT_t, v_t, gate_t, mix_t = rooms(2 * H * S, TT * H * VW, TT * D, 3448)
    qT = qkT_t[:, 0:H * S]
    kT = qkT_t[:, H * S:2 * H * S]
    v_aug = v_t.rearrange("p (t h w) -> p t h w", t=TT, w=VW)
    gate = gate_t.rearrange("p (t d) -> p t d", t=TT)
    gates_all = gate_t[0:16, 0:S]
    row_soft = mix_t[0:H, 248:760]
    row_m = mix_t[0:H, 760:1272]
    row_b = mix_t[0:H, 1272:1784]
    row_a = gb_t[0:H, 0:512]
    row_max = gb_t[0:H, 512:1024]
    wgate = mix_t[:, 1784:1784 + 128].rearrange("p (k n) -> p k n", k=KC)
    decay = mix_t[:, 1912:1912 + 2 * 2 * 384].rearrange("p (b d n) -> p b d n", b=2, d=2)
    gate_bias = small[0:16, 80:81]
    a_cols = small[:, 96:112]
    floor_cols = small[:, 112:128]
    den = small[:, 128:132]
    inv_den = small[:, 132:136]
    b_t = mix_t[:, 0:2 * H * S]
    b_cum = b_t.rearrange("p (n s) -> p n s", s=S)
    q_dec = mix_t[:, 2048:3072].rearrange("p (d n) -> p d n", d=2)
    wglr = wglr_t[:, :].rearrange("p (k n) -> p k n", k=KC)
    k_dec = acc_t[:, :].rearrange("p (d n) -> p d n", d=2)
    diffs = gate[:, :, 512:1024]
    gate_w_sb = room[0:2 * RANK, 7840:8864].rearrange("p (d n) -> p d n", d=2)
    gate_b_rows = room[0:8, 8864:8992]
    glrT = room[0:2 * RANK, 8992:9248]
    attn_row = room[:, 7840:8864]
    gate_b_cols = small[:, 80:88]
    A = gb_t[:, :].rearrange("p (s h t) -> p s h t", s=TT, h=H)

    (xin_t, sel_t, selg_t, turned_t, hid, silu_g, exp_t, aff_t,
     affT_t, work_t, picked_t, part_t) = rooms(
        1024, 1024, S, 2 * S, S, S, 1024, 32, 256, 256, 256, S)
    xinT = xin_t.rearrange("p (k n) -> p k n", k=KC)
    sel = sel_t.rearrange("p (t n) -> p t n", t=TT)
    selg = selg_t.rearrange("p (t n) -> p t n", t=TT)
    hidT = turned_t[:, 0:S].rearrange("p (c n) -> p c n", c=2)
    selT = turned_t[:, S:2 * S]
    w_router = router_t[:, :].rearrange("p (k l n) -> p k l n", l=DEPTH, k=KC)
    aff = aff_t.rearrange("p (t e) -> p t e", t=TT)
    top8 = small[0:E, 160:192]
    row_max_r = small[:, 136:138]
    row_sum_r = small[:, 138:140]
    inv_sum_r = small[:, 140:142]

    aqk_t, av_t, prob_t, probT_t = rooms(16 * S, TT * D, 768, 768)
    aqk = aqk_t.rearrange("p (n s) -> p n s", s=S)
    av = av_t.rearrange("p (t d) -> p t d", t=TT)
    probs = prob_t.rearrange("p (b n) -> p b n", b=2)
    probsT = probT_t.rearrange("p (b n) -> p b n", b=2)
    bias_flip = acc_t[:, :].rearrange("p (b h n) -> p b h n", b=2, h=4)
    neg_max = small[:, 144:148]
    prob_sum = small[:, 148:152]
    inv_prob = small[:, 152:156]
    rel_T = room[0:BUCKETS, 8900:8916]
    dist_hot = room[0:BUCKETS, 8400:8400 + S]
    bias_rows = room[0:AH, 8960:8960 + WROW]

    ffh_t, conv_t, convw_t, _ = rooms(FB * S, 2 * 1024, 4 * 2 * FB, 984)
    convrow_t = room[:, 8864:8864 + 4 * P]
    ffh = ffh_t.rearrange("p (n s) -> p n s", s=S)
    conv = conv_t.rearrange("p (b n s) -> p b n s", b=2, s=S)
    conv_cols = convw_t.rearrange("p (j n) -> p j n", j=4)
    conv_rows = convrow_t[0:2 * FB, :].rearrange("p (j n) -> p j n", j=4)
    square_sum = small[:, 156:158]

    PS = [ctx.enter_context(nc.psum_tensor(f"bank{i}", [P, 512], F32)) for i in range(8)]

    bias_dram = nc.dram_tensor("bias_rows_dram", (AH, WROW), F32, kind="Internal")

    landed = [sem(f"landed{i}") for i in range(SLOTS)]
    tile_used = sem("tile_used")
    const_landed = sem("const_landed")
    x_landed = sem("x_landed")
    small_landed = [sem(f"small_landed{i}") for i in range(6)]
    rows_landed = sem("rows_landed")
    gain_landed = sem("gain_landed")
    router_landed = sem("router_landed")
    attn_row_landed = sem("attn_row_landed")
    ones_ready = sem("ones_ready")
    masks_ready = sem("masks_ready")
    tokens_ready = sem("tokens_ready")
    tr_done = sem("tr_done")
    tr_act = sem("tr_act")
    tr_dve = sem("tr_dve")
    proj_act = sem("proj_act")
    proj_dve = sem("proj_dve")
    piece_done = sem("piece_done")
    piece_out = sem("piece_out")
    gate_ready = sem("gate_ready")
    dve_seq = sem("dve_seq")
    act_seq = sem("act_seq")
    gates_done, gates_biased, gates_split = sem("gates_done"), sem("gates_biased"), sem("gates_split")
    gate_soft, gate_rows, gate_colsd, gate_scalars = (
        sem("gate_soft"), sem("gate_rows"), sem("gate_cols"), sem("gate_scalars"))
    mb_done, scores_done, decay_done = sem("mb_done"), sem("scores_done"), sem("decay_done")
    weights_done, num_done, head_out = sem("weights_done"), sem("num_done"), sem("head_out")
    glr_done, glr_copied, z_done, z_ready, z_soft, b_ready = (
        sem("glr_done"), sem("glr_copied"), sem("z_done"), sem("z_ready"), sem("z_soft"), sem("b_ready"))
    glr_zero = sem("glr_zero")
    diffs_done, decays_exp, scaled_done, prod_done, placed = (
        sem("diffs_done"), sem("decays_exp"), sem("scaled_done"), sem("prod_done"), sem("placed"))
    diag_done, diag_placed, gla_out = sem("diag_done"), sem("diag_placed"), sem("gla_out")
    out_rows = sem("out_rows")
    logits_part, logits_copied, logits_done = sem("logits_part"), sem("logits_copied"), sem("logits_done")
    router_max, aff_exp, aff_ready, affT_done = (
        sem("router_max"), sem("aff_exp"), sem("aff_ready"), sem("affT_done"))
    slots_ready, slotsT_done, sel_ready, alpha_x = (
        sem("slots_ready"), sem("slotsT_done"), sem("sel_ready"), sem("alpha_x"))
    xin_done, xin_act, xin_dve = sem("xin_done"), sem("xin_act"), sem("xin_dve")
    exp_act, exp_dve, selg_ready, turned_copied = (
        sem("exp_act"), sem("exp_dve"), sem("selg_ready"), sem("turned_copied"))
    silu_done, hid_done, turned, comb_done = (
        sem("silu_done"), sem("hid_done"), sem("turned"), sem("comb_done"))
    relb_done, relb_copied, relb_stored = sem("relb_done"), sem("relb_copied"), sem("relb_stored")
    bias_landed = [sem("bias_landed0"), sem("bias_landed1")]
    var_ready = sem("var_ready")
    root_done = sem("root_done")
    x_sum = sem("x_sum")
    s_done, max_done, probs_exp, p_ready, pt_done, pt_copied, o_done, o_copied = (
        sem("s_done"), sem("max_done"), sem("probs_exp"), sem("p_ready"), sem("pt_done"),
        sem("pt_copied"), sem("o_done"), sem("o_copied"))
    convT_done, convT_copied, taps_done, conv_done, ff_silu, ff_ready = (
        sem("convT_done"), sem("convT_copied"), sem("taps_done"), sem("conv_done"),
        sem("ff_silu"), sem("ff_ready"))
    out_landed = sem("out_landed")

    def slot(n):
        s = n % SLOTS
        return ring[:, s * TILE:(s + 1) * TILE]

    def arrived(pe, n, more=0):
        pe.wait_ge(landed[n % SLOTS], 16 * (n // SLOTS + 1) + more)

    class Chain:
        def __init__(self, eng, s):
            self.eng, self.s, self.n = eng, s, 0

        def link(self, ins):
            self.n += 1
            ins.then_inc(self.s, 1)
            self.eng.wait_ge(self.s, self.n)

    U_X0, U_Y0, U_M0, U_X1, U_Y1, U_M1, U_ATT, U_FFN, U_OUT = range(9)

    def tokens_before(use):
        return TT * (use - 1 + (use >= U_ATT))

    def taken(stage, i):
        return (0, 4, 6)[stage] + i + 1

    def pieces_before(layer):
        return 4 * layer

    HEAD_NORMS, LAYER_NORMS, RMS_NORMS = (0, 3), (1, 2, 4, 5), (6, 7, 8)

    def roots_before(n):
        return TT * n

    block = ctx.enter_context(nc.Block())

    @block.sync
    def _(sp):
        def free(n):
            if n >= SLOTS:
                sp.wait_ge(tile_used, n - SLOTS + 1)

        def load(n, src, dst=None):
            free(n)
            sp.dma_start(slot(n) if dst is None else dst, src).then_inc(landed[n % SLOTS], 16)

        def columns(n, w, first, count):
            v = w.rearrange("(k p) n -> p k n", p=P)
            for j in range(count):
                load(n + j, v[:, :, first + 512 * j:first + 512 * (j + 1)],
                     slot(n + j).rearrange("p (k n) -> p k n", k=KC))

        def experts(layer):
            ws = [t[w][layer].rearrange("e (r k p) n -> e r p k n", p=P, k=4)
                  for w in ("moe_w_gate", "moe_w_up", "moe_w_down")]
            base = T_MOE[layer]
            with sp.Fori(0, NG) as g:
                for j in range(EG):
                    for c in range(TPE):
                        n = TPE * j + c
                        sp.wait_ge(tile_used, g * (EG * TPE) + (base + n - SLOTS + 1))
                        sp.dma_start(slot(n).rearrange("p (k n) -> p k n", k=4),
                                     ws[c // 2][bass.ds(g * EG + j, 1), c % 2].rearrange("e p k n -> p (e k) n")
                                     ).then_inc(landed[n % SLOTS], 16)

        sp.dma_start(x_tok, t["x"][0].rearrange("(t p) d -> p t d", p=P)).then_inc(x_landed, 16)
        sp.dma_start(consts[:, :], t["const_main"]).then_inc(const_landed, 16)
        sp.dma_start(rel_T, t["rel_bias_2"].rearrange("h b -> b h"), allow_slow_non_contiguous=True
                     ).then_inc(small_landed[1], 16)
        sp.dma_start(dist_hot, t["const_onehot"]).then_inc(small_landed[1], 16)
        sp.dma_start(wgate, t["mlstm_w_in"][0].rearrange("(k p) n -> p k n", p=P)[:, :, 3072:3088]
                     ).then_inc(small_landed[0], 16)
        sp.dma_start(gate_bias, t["mlstm_gate_b"][0].rearrange("a b (c o) -> (a b c) o", o=1)
                     ).then_inc(small_landed[0], 16)
        columns(T_MLSTM, t["mlstm_w_in"][0], 0, 6)
        columns(T_MLSTM + 6, t["mlstm_w_out"][0], 0, 2)
        experts(0)
        columns(T_GLA, t["gla_w_in"][0], 0, 6)
        columns(T_GLA + 6, t["gla_w_out"][0], 0, 2)
        experts(1)
        columns(T_QKV, t["w_qkv_2"][0], 0, 6)
        columns(T_WO, t["w_o_2"][0], 0, 2)
        up = t["w_up_2"][0].rearrange("(k p) (h n) -> p k h n", p=P, h=2)
        for i in range(UPT):
            n = T_UP + i
            free(n)
            dst = slot(n).rearrange("p (k h n) -> p k h n", k=KC, h=2)
            for h in range(2):
                sp.dma_start(dst[:, :, h, :], up[:, :, h, S * i:S * (i + 1)]).then_inc(landed[n % SLOTS], 16)
        down = t["w_down_2"][0].rearrange("(k p) n -> p k n", p=P)
        for i in range(N_DOWN):
            n = T_DOWN + i
            k = min(4, FB - 4 * i)
            load(n, down[:, 4 * i:4 * i + k, :], slot(n)[:, 0:k * D].rearrange("p (k n) -> p k n", k=k))

    def up_landed(n):
        twice = sum(1 for m in range(T_UP, min(n + 1, T_DOWN)) if m % SLOTS == n % SLOTS)
        return 16 * (n // SLOTS + 1 + twice)

    @block.gpsimd
    def _(pool):
        def row(dst, src, s):
            pool.dma_start(dst, src.partition_broadcast(P)).then_inc(s, 16)

        def norm_rows(g, b):
            row(gain_row, g, rows_landed)
            row(bias_row, b, rows_landed)

        nc.gpsimd.memset(ones[:, 0:1], 1.0)
        nc.gpsimd.memset(ln_eps, LN_EPS)
        nc.gpsimd.memset(rms_eps, RMS_EPS).then_inc(ones_ready, 1)
        nc.gpsimd.memset(v_aug[:, :, :, DV:VW], 1.0).then_inc(ones_ready, 1)
        nc.gpsimd.memset(bias_rows[:, S:WROW], -BIG).then_inc(ones_ready, 1)
        masks_f32 = acc_t[:, 0:2 * len(LEVELS) * 64]
        pool.dma_start(masks_f32, t["const_masks"]).then_inc(small_landed[2], 16)
        row(ng_t[:, :], t["mlstm_norm_g"][0], gain_landed)
        for layer in range(DEPTH):
            pool.dma_start(w_router[:, :, layer], t["moe_router"][layer].rearrange("(k p) n -> p k n", p=P)
                           ).then_inc(router_landed, 16)
        pool.dma_start(wglr, t["gla_w_in"][0].rearrange("(k p) n -> p k n", p=P)[:, :, 3072:3104]
                       ).then_inc(small_landed[5], 16)
        pool.wait_ge(small_landed[2], 16)
        nc.gpsimd.tensor_copy(level_masks[:, :], masks_f32).then_inc(masks_ready, 1)
        pool.wait_ge(relb_copied, 1)
        pool.wait_ge(ones_ready, 3)
        pool.dma_start(bias_dram.ap(), bias_rows).then_inc(relb_stored, 16)

        def output_gate(layer, j):
            pool.wait_ge(piece_out, pieces_before(layer) + (4 if layer else 0) + 2 * (j + 1))
            pool.wait_ge(gain_landed, 16 * (layer + 1))
            c = slice(j * 512, (j + 1) * 512)
            for i in range(TT):
                last = nc.gpsimd.tensor_tensor(gate[:, i, c], gate[:, i, c], ng_t[:, c], ALU.mult)
            last.then_inc(gate_ready, 1)

        def moe_small(layer, u_moe):
            pool.wait_ge(tokens_ready, tokens_before(u_moe) + TT)
            for i in range(TT):
                last = nc.gpsimd.tensor_scalar(acc[:, i], x_tok[:, i], ALPHA, 0.0, ALU.mult, ALU.add)
            last.then_inc(alpha_x, 1)
            norm_rows(t["ln_g"][layer, 1], t["ln_b"][layer, 1])

        output_gate(0, 0)
        output_gate(0, 1)
        pool.wait_ge(weights_done, H)
        norm_rows(t["ln_g"][0, 0], t["ln_b"][0, 0])
        moe_small(0, U_M0)
        row(ng_t[:, :], t["gla_norm_g"][0], gain_landed)
        nc.gpsimd.memset(gate_w_sb, 0.0).then_inc(glr_zero, 1)
        pool.wait_ge(glr_zero, 1)
        for d in range(2):
            pool.dma_start(gate_w_sb[RANK * d:RANK * (d + 1), d], t["gla_gate_w"][0, d]).then_inc(small_landed[3], 16)
        pool.dma_start(gate_b_rows, t["gla_gate_b"][0].rearrange("d (n p) -> (d n) p", p=P)
                       ).then_inc(small_landed[3], 16)
        pool.wait_ge(b_ready, 1)
        for i in range(2 * (len(LEVELS) + 1)):
            d, L = i % 2, P >> (i // 2)
            b = b_t[:, d * H * S:(d + 1) * H * S].rearrange("p (n w l) -> p n w l", w=2, l=L)
            left, right = b[:, :, 0, :], b[:, :, 1, :]
            nb = H * S // (2 * L)
            border = (left[:, :, L - 1:L] if d == 0 else right[:, :, 0:1]).to_broadcast([P, nb, L])
            qs, ks = (right, left) if d == 0 else (left, right)
            if i >= 1:
                pool.wait_ge(decays_exp, i)
            dq = diffs[:, 0].rearrange("p (n l) -> p n l", l=L)
            dk = diffs[:, 1].rearrange("p (n l) -> p n l", l=L)
            nc.gpsimd.tensor_tensor(dq, qs, border, ALU.subtract)
            nc.gpsimd.tensor_tensor(dk, border, ks, ALU.subtract).then_inc(diffs_done, 1)
            if i == 10:
                output_gate(1, 0)
        output_gate(1, 1)
        pool.wait_ge(gla_out, TT)
        norm_rows(t["ln_g"][1, 0], t["ln_b"][1, 0])
        moe_small(1, U_M1)
        row(attn_row, t["attn_norm_2"][0], attn_row_landed)
        for j in range(3):
            pool.dma_start(conv_rows[:, j], t["conv_w_2"][0, j].rearrange("(n p) -> n p", p=P)
                           ).then_inc(small_landed[4], 16)
        pool.dma_start(conv_rows[:, 3], t["conv_b_2"][0].rearrange("(n p) -> n p", p=P)
                       ).then_inc(small_landed[4], 16)
        row(ng_t[:, :], t["final_norm_2"], gain_landed)
        pool.wait_ge(tokens_ready, tokens_before(U_ATT))
        row(bias_row, t["ffn_norm_2"][0], rows_landed)
        pool.wait_ge(relb_stored, 16)
        pool.wait_ge(tr_done, 4 * (U_ATT + 1))
        for g in range(AH // 4):
            if g >= 2:
                pool.wait_ge(s_done, 4 * (g - 1))
            src = bass.AP(bias_dram, 4 * g * WROW, [[1, P], [WROW, 4], [1, S]])
            pool.dma_start(bias_flip[:, g % 2], src).then_inc(bias_landed[g % 2], 16)
        for tt in range(TT):
            pool.wait_ge(tokens_ready, tokens_before(U_OUT) + tt + 1)
            pool.dma_start(out[0, tt * P:(tt + 1) * P], acc[:, tt]).then_inc(out_landed, 16)
        pool.wait_ge(out_landed, 16 * TT)

    @block.tensor
    def _(pe):
        mm = nc.tensor.matmul
        turn = nc.tensor.transpose

        def transposes(src, use):
            if use == U_X0:
                pe.wait_ge(x_landed, 16)
                pe.wait_ge(const_landed, 16)
            for i in range(TT):
                if use > U_X0:
                    pe.wait_ge(tokens_ready, tokens_before(use) + i + 1)
                for b in range(KC // 2):
                    for kk in range(2):
                        k = 2 * b + kk
                        last = turn(PS[b][:, kk * S + i * P:kk * S + (i + 1) * P],
                                    src[:, i, k * P:(k + 1) * P], ident)
                    if i == TT - 1:
                        last.then_inc(tr_done, 1)
            pe.wait_ge(tr_act, 2 * (use + 1))
            pe.wait_ge(tr_dve, 2 * (use + 1))

        def project(n, stage, i, channel_tiles):
            b0 = 2 * (i % 2)
            arrived(pe, n + i)
            w = slot(n + i).rearrange("p (k n) -> p k n", k=KC)
            if i >= 2:
                pe.wait_ge(proj_act, taken(stage, i - 2))
                pe.wait_ge(proj_dve, taken(stage, i - 2))
            if i < channel_tiles:
                for c in range(4):
                    for k in range(KC):
                        last = mm(PS[b0 + c // 2][:, (c % 2) * S:(c % 2 + 1) * S], w[:, k, c * P:(c + 1) * P],
                                  xT[:, k, :], start=(k == 0), stop=(k == KC - 1))
            else:
                for tt in range(TT):
                    for k in range(KC):
                        last = mm(PS[b0 + tt][:, :], xT[:, k, tt * P:(tt + 1) * P], w[:, k, :],
                                  start=(k == 0), stop=(k == KC - 1))
            last.then_inc(tile_used, 1)

        def piece(layer, n, p, bank):
            if p % 2 == 0:
                arrived(pe, n + p // 2)
            w = slot(n + p // 2).rearrange("p (k n) -> p k n", k=KC)
            tt = p % 2
            for k in range(KC):
                last = mm(bank[:, :], xT[:, k, tt * P:(tt + 1) * P], w[:, k, :],
                          start=(k == 0), stop=(k == KC - 1))
            last.then_inc(piece_done, 1)
            if p % 2 == 1:
                pe.wait_ge(piece_done, pieces_before(layer) + p + 1)
                pe.sem_inc(tile_used, 1)

        def out_project(n):
            for j in range(2):
                arrived(pe, n + j)
                w = slot(n + j).rearrange("p (k n) -> p k n", k=KC)
                for tt in range(TT):
                    for k in range(KC):
                        last = mm(PS[4 + 2 * tt + j][:, :], xT[:, k, tt * P:(tt + 1) * P], w[:, k, :],
                                  start=(k == 0), stop=(k == KC - 1))
                    if j == 1 and tt == 0:
                        last.then_inc(out_rows, 1)
                last.then_inc(tile_used, 1)

        def mlstm():
            transposes(x_tok, U_X0)
            pe.wait_ge(small_landed[1], 32)
            mm(PS[7][0:AH, 0:S], rel_T, dist_hot, start=True, stop=True).then_inc(relb_done, 1)
            pe.wait_ge(small_landed[0], 32)
            for k in range(KC):
                last = mm(PS[4][0:16, 0:S], wgate[:, k, :], xT[:, k, :], start=(k == 0), stop=(k == KC - 1))
            last.then_inc(gates_done, 1)
            pe.wait_ge(gates_biased, 1)
            for d in range(2):
                for kind in range(2):
                    c = 4 * (2 * d + kind)
                    last = mm(PS[5 + kind][0:H, d * S:(d + 1) * S], ident[0:16, c:c + H], gates_all,
                              start=True, stop=True)
            last.then_inc(gates_split, 1)
            for i in range(4):
                project(T_MLSTM, 0, i, 2)
                if i == 1:
                    pe.wait_ge(gate_rows, 1)
                    pe.wait_ge(relb_copied, 1)
                    for q, rows in enumerate((row_a, row_m)):
                        for d in range(2):
                            for tt in range(TT):
                                c = ((q * 2 + d) * 2 + tt) * H
                                last = turn(PS[7][:, c:c + H], rows[:, d * S + tt * P:d * S + (tt + 1) * P],
                                            ident[0:H, 0:H])
                    last.then_inc(gate_colsd, 1)
            pe.wait_ge(gate_scalars, 1)
            pe.wait_ge(ones_ready, 3)
            pe.wait_ge(proj_act, taken(0, 3))
            pe.wait_ge(proj_dve, taken(0, 3))

            def head_scores(h):
                if h >= 1:
                    pe.wait_ge(decay_done, h)
                pick = ident[0:H, h:h + 1].to_broadcast([H, P])
                for d in range(2):
                    b = PS[4 + d]
                    for s in range(TT):
                        t0, t1 = (s, TT) if d == 0 else (0, s + 1)
                        c0 = (0, 2)[s] if d == 0 else (0, 1)[s]
                        mm(b[:, c0 * P:(c0 + t1 - t0) * P], pick, row_max[:, d * S + t0 * P:d * S + t1 * P],
                           start=True, stop=False, skip_group_check=True)
                        cm = (c0 + s - t0) * P
                        last = mm(b[:, cm:cm + P], ident, mask_after if d == 0 else mask_before,
                                  start=False, stop=True, skip_group_check=True)
                last.then_inc(mb_done, 1)
                if h >= 1:
                    pe.wait_ge(weights_done, h)
                for s in range(TT):
                    last = mm(PS[6][:, s * S:(s + 1) * S], kT[:, h * S + s * P:h * S + (s + 1) * P],
                              qT[:, h * S:(h + 1) * S], start=True, stop=True)
                last.then_inc(scores_done, 1)

            def head_sums(h):
                pe.wait_ge(weights_done, h + 1)
                if h >= 1:
                    pe.wait_ge(head_out, h)
                w = decay[:, h % 2]
                for tt in range(TT):
                    for d in range(2):
                        srcs = range(tt + 1) if d == 0 else range(tt, TT)
                        for s in srcs:
                            c = ((0, 2)[s] + tt - s if d == 0 else (0, 1)[s] + tt) * P
                            last = mm(PS[2 * tt + d][:, 0:VW], w[:, d, c:c + P], v_aug[:, s, h, :],
                                      start=(s == srcs[0]), stop=(s == srcs[-1]))
                last.then_inc(num_done, 1)

            for h in range(H):
                head_scores(h)
                if h >= 1:
                    pe.wait_ge(piece_out, h)
                piece(0, T_MLSTM + 4, h, PS[7])
                head_sums(h)
            transposes(acc, U_Y0)
            out_project(T_MLSTM + 6)

        def gla():
            transposes(x_tok, U_X1)
            pe.wait_ge(small_landed[5], 16)
            for k in range(KC):
                last = mm(PS[4][0:2 * RANK, 0:S], wglr[:, k, :], xT[:, k, :], start=(k == 0), stop=(k == KC - 1))
            last.then_inc(glr_done, 1)
            project(T_GLA, 1, 0, 2)
            pe.wait_ge(small_landed[3], 48)
            turn(PS[5][:, 0:8], gate_b_rows, ident[0:8, 0:8]).then_inc(glr_done, 1)
            pe.wait_ge(glr_copied, 2)
            for n in range(2 * H):
                last = mm(PS[4 + n // 2][:, (n % 2) * S:(n % 2 + 1) * S],
                          gate_w_sb[:, n // H, (n % H) * P:(n % H + 1) * P], glrT, start=True, stop=True)
            last.then_inc(z_done, 1)
            project(T_GLA, 1, 1, 2)
            pe.wait_ge(proj_act, taken(1, 1))
            pe.wait_ge(proj_dve, taken(1, 1))
            for n in range(2):
                piece(1, T_GLA + 2, n, PS[n])
            for tt in range(TT):
                for h in range(H):
                    c = h * S + tt * P
                    last = mm(PS[2 + tt][:, h * P:(h + 1) * P], kT[:, c:c + P], qT[:, c:c + P], start=True, stop=True)
                last.then_inc(diag_done, 1)
            pe.wait_ge(piece_out, pieces_before(1) + 2)
            pe.wait_ge(diag_placed, 1)
            for i in range(2 * (len(LEVELS) + 1)):
                d = i % 2
                if d == 0 and i // 2 + 2 < 8:
                    n = i // 2 + 2
                    if n >= 4:
                        pe.wait_ge(piece_out, pieces_before(1) + n - 1)
                    piece(1, T_GLA + 2, n, PS[2 + n % 2])
                pe.wait_ge(scaled_done, i + 1)
                if i >= 2:
                    pe.wait_ge(placed, i - 1)
                for h in range(H):
                    if i < 2:
                        last = mm(PS[d][:, h * P:(h + 1) * P], k_dec[:, d, h * S + d * P:h * S + (d + 1) * P],
                                  q_dec[:, d, h * P:(h + 1) * P], start=True, stop=True)
                        continue
                    for s in range(TT):
                        c = (s * H + h) * 64
                        last = mm(PS[d][:, c:c + 64], k_dec[:, d, h * S + s * P:h * S + (s + 1) * P],
                                  q_dec[:, d, h * P + s * 64:h * P + (s + 1) * 64], start=True, stop=True)
                last.then_inc(prod_done, 1)
            pe.wait_ge(placed, 2 * (len(LEVELS) + 1))
            pe.wait_ge(piece_out, pieces_before(1) + 8)
            for tt in range(TT):
                for h in range(H):
                    for s in range(TT):
                        last = mm(PS[4 + 2 * tt + h // 2][:, (h % 2) * DV:(h % 2 + 1) * DV],
                                  A[:, s, h, tt * P:(tt + 1) * P], v_aug[:, s, h, 0:DV],
                                  start=(s == 0), stop=(s == TT - 1))
                last.then_inc(gla_out, 1)
            transposes(acc, U_Y1)
            out_project(T_GLA + 6)

        def moe(layer, use):
            transposes(x_tok, use)
            pe.wait_ge(router_landed, 16 * DEPTH)
            for k in range(KC):
                q = k % 4
                last = mm(PS[0][q * DEPTH * E:(q + 1) * DEPTH * E, 0:S],
                          w_router[:, k].rearrange("p l n -> p (l n)"), xT[:, k, :],
                          start=(k < 4), stop=(k >= 4), skip_group_check=True)
            last.then_inc(logits_part, 1)
            pe.wait_ge(logits_copied, layer + 1)
            for tt in range(TT):
                last = mm(PS[1][:, tt * E:(tt + 1) * E], part_t[:, tt * P:(tt + 1) * P],
                          logit_of[:, layer * E:(layer + 1) * E], start=True, stop=True)
            last.then_inc(logits_done, 1)
            pe.wait_ge(aff_ready, layer + 1)
            for tt in range(TT):
                last = turn(PS[2][0:E, tt * P:(tt + 1) * P], aff[:, tt, :], ident)
            last.then_inc(affT_done, 1)
            pe.wait_ge(alpha_x, layer + 1)
            for tt in range(TT):
                for i in range(2):
                    mm(PS[4 + 2 * tt + i][:, :], ident, acc[:, tt, i * 512:(i + 1) * 512],
                       start=True, stop=True, skip_group_check=True)
            pe.wait_ge(slots_ready, layer + 1)
            for tt in range(TT):
                last = turn(PS[3][:, tt * E:(tt + 1) * E], picked_t[0:E, tt * P:(tt + 1) * P], ident[0:E, 0:E])
            last.then_inc(slotsT_done, 1)
            pe.wait_ge(sel_ready, layer + 1)
            base, n0, m0 = T_MOE[layer], E * layer, NG * layer
            with pe.Fori(0, NG) as g:
                def gather(half):
                    for k in range(4 * half, 4 * half + 4):
                        for tt in range(TT):
                            last = mm(PS[half][:, (k % 4) * P:(k % 4 + 1) * P], x_tok[:, tt, k * P:(k + 1) * P],
                                      sel[:, tt, bass.ts(g, P)], start=(tt == 0), stop=(tt == TT - 1))
                    last.then_inc(xin_done, 1)

                gather(0)
                for j in range(EG):

                    def tile(c):
                        n = TPE * j + c
                        pe.wait_ge(landed[n % SLOTS], g * (16 * EG * TPE // SLOTS)
                                   + 16 * ((base + n) // SLOTS + 1))
                        return slot(n).rearrange("p (k n) -> p k n", k=4)

                    def up_products(c, r, bank):
                        w = tile(c + r)
                        for k in range(4):
                            for q in range(4):
                                last = mm(bank[q * CAP:(q + 1) * CAP, 0:S],
                                          xinT[:, 4 * r + k, j * CAP:(j + 1) * CAP],
                                          w[:, k, q * S:(q + 1) * S],
                                          start=(r == 0 and k == 0), stop=(r == 1 and k == 3),
                                          skip_group_check=True)
                        last.then_inc(tile_used, 1)

                    if j == 0:
                        pe.wait_ge(xin_act, g + (m0 + 1))
                    pe.wait_ge(silu_done, g * EG + (n0 + j + 1))
                    up_products(0, 0, PS[2])
                    if j == 0:
                        gather(1)
                        pe.wait_ge(xin_dve, g + (m0 + 1))
                    up_products(0, 1, PS[2])
                    pe.wait_ge(hid_done, g * EG + (n0 + j + 1))
                    for r in range(2):
                        up_products(2, r, PS[3])
                    pe.wait_ge(selg_ready, g * EG + (n0 + j + 1))
                    pe.wait_ge(silu_done, g * EG + (n0 + j + 2))
                    for tt in range(TT):
                        turn(PS[2][:, S + tt * P:S + (tt + 1) * P], selg[:, tt], ident)
                    pe.wait_ge(hid_done, g * EG + (n0 + j + 2))
                    for c in range(2):
                        last = turn(PS[2][:, c * P:(c + 1) * P], hid[:, c * P:(c + 1) * P], ident)
                    last.then_inc(turned, 1)
                    pe.wait_ge(turned_copied, g * EG + (n0 + j + 1))
                    for r in range(2):
                        w = tile(4 + r)
                        for i in range(2):
                            for k in range(4):
                                kk = 4 * r + k
                                last = mm(PS[i][k * CAP:(k + 1) * CAP, :],
                                          hidT[:, kk % 2, (kk // 2) * CAP:(kk // 2 + 1) * CAP],
                                          w[:, k, i * 512:(i + 1) * 512],
                                          start=(r == 0), stop=(r == 1), skip_group_check=True)
                        last.then_inc(tile_used, 1)
                    pe.wait_ge(exp_act, g * EG + (n0 + j + 1))
                    pe.wait_ge(exp_dve, g * EG + (n0 + j + 1))
                    for tt in range(TT):
                        for i in range(2):
                            last = mm(PS[4 + 2 * tt + i][:, :], selT[:, tt * P:(tt + 1) * P],
                                      exp_t[:, i * 512:(i + 1) * 512], start=False, stop=True,
                                      skip_group_check=True)
                        last.then_inc(comb_done, 1)

        def attention():
            transposes(acc, U_ATT)
            for i in range(6):
                project(T_QKV, 2, i, 4)
            pe.wait_ge(proj_act, taken(2, 5))
            pe.wait_ge(proj_dve, taken(2, 5))

            def scores(h):
                if h >= 4:
                    pe.wait_ge(probs_exp, h - 3)
                if h % 4 == 0:
                    pe.wait_ge(bias_landed[(h // 4) % 2], 16 * (h // 8 + 1))
                b = PS[2 + h % 4]
                r = slice(AD * (h % 2), AD * (h % 2 + 1))
                bias = bias_flip[:, (h // 4) % 2, h % 4]
                mm(b[:, 0:P], flip, bias[:, P:S], start=True, stop=False, skip_group_check=True)
                mm(b[:, 0:P], aqk[r, h // 2, 0:P], aqk[r, 8 + h // 2, 0:P], start=False, stop=True,
                   skip_group_check=True)
                mm(b[:, P:P + S], flip, bias, start=True, stop=False, skip_group_check=True)
                mm(b[:, P:P + S], aqk[r, h // 2, P:S], aqk[r, 8 + h // 2, :], start=False, stop=True,
                   skip_group_check=True).then_inc(s_done, 1)

            def turn_probs(h):
                pe.wait_ge(p_ready, h + 1)
                if h >= 2:
                    pe.wait_ge(pt_copied, h - 1)
                b, pr = PS[6 + h % 2], probs[:, h % 2]
                for c in range(3):
                    last = turn(b[:, c * P:(c + 1) * P], pr[:, c * P:(c + 1) * P], ident)
                last.then_inc(pt_done, 1)

            def values(h):
                pe.wait_ge(pt_copied, h + 1)
                if h % 2 == 0 and h >= 4:
                    pe.wait_ge(o_copied, h // 2 - 1)
                r = slice(AD * (h % 2), AD * (h % 2 + 1))
                b, pT = PS[(h // 2) % 2], probsT[:, h % 2]
                mm(b[r, 0:S], av[:, 0, h * AD:(h + 1) * AD], pT[:, 0:S], start=True, stop=False,
                   skip_group_check=True)
                mm(b[r, P:S], av[:, 1, h * AD:(h + 1) * AD], pT[:, S:S + P], start=False, stop=True,
                   skip_group_check=True).then_inc(o_done, 1)

            scores(0)
            scores(1)
            for h in range(AH):
                if h + 2 < AH:
                    scores(h + 2)
                turn_probs(h)
                if h >= 1:
                    values(h - 1)
            values(AH - 1)
            pe.wait_ge(o_copied, AH // 2)
            out_project(T_WO)

        def ffn():
            transposes(acc, U_FFN)
            pe.wait_ge(small_landed[4], 64)
            for j in range(4):
                last = turn(PS[6][:, j * 2 * FB:(j + 1) * 2 * FB], conv_rows[:, j, :], ident[0:2 * FB, 0:2 * FB])
            last.then_inc(convT_done, 1)
            for i in range(UPT):
                n = T_UP + i
                pe.wait_ge(landed[n % SLOTS], up_landed(n))
                if i >= 3:
                    pe.wait_ge(conv_done, i - 2)
                w = slot(n).rearrange("p (k n) -> p k n", k=KC)
                b0 = 2 * (i % 3)
                for c in range(4):
                    for k in range(KC):
                        last = mm(PS[b0 + c // 2][:, (c % 2) * S:(c % 2 + 1) * S], w[:, k, c * P:(c + 1) * P],
                                  xT[:, k, :], start=(k == 0), stop=(k == KC - 1))
                last.then_inc(tile_used, 1)
            pe.wait_ge(ff_ready, UPT)
            for i in range(N_DOWN):
                n = T_DOWN + i
                pe.wait_ge(landed[n % SLOTS], up_landed(n))
                w = slot(n).rearrange("p (k n) -> p k n", k=4)
                for tt in range(TT):
                    for k in range(4 * i, min(4 * i + 4, FB)):
                        for j in range(2):
                            last = mm(PS[4 + 2 * tt + j][:, :], ffh[:, k, tt * P:(tt + 1) * P],
                                      w[:, k - 4 * i, j * 512:(j + 1) * 512], start=(k == 0), stop=(k == FB - 1))
                    if i == N_DOWN - 1 and tt == 0:
                        last.then_inc(out_rows, 1)
                last.then_inc(tile_used, 1)

        pe.sem_inc(turned, 1)
        pe.sem_inc(comb_done, 1)
        mlstm()
        moe(0, U_M0)
        gla()
        moe(1, U_M1)
        attention()
        ffn()

    @block.scalar
    def _(act):
        f = nc.scalar.activation
        chain = Chain(act, act_seq)
        link = chain.link

        def copy_transposes(use):
            for b in (0, 2):
                act.wait_ge(tr_done, 4 * use + b + 1)
                f(xT_t[:, b * 512:(b + 1) * 512], PS[b][:, :], ACT.Copy).then_inc(tr_act, 1)

        def take_projection(stage, n, i):
            act.wait_ge(tile_used, n + i + 1)
            b0 = 2 * (i % 2)
            if stage == 2:
                if i < 4:
                    dst = aqk_t[:, (4 * i) * S:(4 * i + 2) * S]
                    last = f(dst, PS[b0][:, :], ACT.Copy, scale=(AD ** -0.5 if i < 2 else 1.0))
                else:
                    last = f(av[:, 0, (i - 4) * 512:(i - 3) * 512], PS[b0][:, :], ACT.Copy)
            elif i < 2:
                last = f(qkT_t[:, i * H * S:i * H * S + 512], PS[b0][:, :], ACT.Copy,
                         scale=(DK ** -0.5 if i == 0 else 1.0))
            else:
                last = f(v_aug[:, 0, 2 * (i - 2):2 * (i - 1), 0:DV],
                         PS[b0][:, :].rearrange("p (h w) -> p h w", w=DV), ACT.Copy)
            last.then_inc(proj_act, 1)

        def take_values(n, bank):
            act.wait_ge(piece_done, pieces_before(1) + n + 1)
            f(v_aug[:, n % 2, 2 * (n // 2):2 * (n // 2 + 1), 0:DV], bank[:, :].rearrange("p (h w) -> p h w", w=DV),
              ACT.Copy).then_inc(piece_out, 1)

        def take_gate(first, n, bank, fn):
            act.wait_ge(piece_done, first + n + 1)
            c = slice((n // 2) * 512, (n // 2 + 1) * 512)
            if n % 2 == 0:
                f(gate[:, 0, c], bank[:, :], ACT.Copy).then_inc(piece_out, 1)
            else:
                act.wait_ge(piece_out, first + n)
                f(gate[:, 0, c], gate[:, 0, c], fn)
                f(gate[:, 1, c], bank[:, :], fn).then_inc(piece_out, 1)

        def roots(norm, heads=1):
            for tt in range(TT):
                c = slice(tt * heads, (tt + 1) * heads)
                act.wait_ge(var_ready, roots_before(norm) + tt + 1)
                f(deviation[:, c], meanvar[:, c, 1], ACT.Sqrt, bias=ln_eps).then_inc(root_done, 1)

        def mlstm():
            copy_transposes(U_X0)
            act.wait_ge(relb_done, 1)
            f(bias_rows[:, 0:S], PS[7][0:AH, 0:S], ACT.Copy).then_inc(relb_copied, 1)
            act.wait_ge(gates_done, 1)
            f(gates_all, PS[4][0:16, 0:S], ACT.Identity, bias=gate_bias).then_inc(gates_biased, 1)
            act.wait_ge(gates_split, 1)
            link(f(row_soft, PS[6][0:H, :], ACT.Abs))
            link(f(row_soft, row_soft, ACT.Exp, scale=-1.0))
            f(row_soft, row_soft, ACT.Ln, bias=1.0).then_inc(gate_soft, 1)
            for i in range(4):
                take_projection(0, T_MLSTM, i)
                if i == 1:
                    act.wait_ge(gate_colsd, 1)
                    f(a_cols, PS[7][:, 0:16], ACT.Copy)
                    link(f(floor_cols, PS[7][:, 16:32], ACT.Exp, scale=-1.0))
                    act.sem_inc(gate_scalars, 1)
            act.wait_ge(relb_stored, 16)
            for h in range(H):
                act.wait_ge(mb_done, h + 1)
                if h >= 2:
                    act.wait_ge(num_done, h - 1)
                w = decay[:, h % 2]
                for d in range(2):
                    for s in range(TT):
                        c0, c1 = ((0, 256), (256, 384))[s] if d == 0 else ((0, 128), (128, 384))[s]
                        col = (d * 2 + s) * H + h
                        last = f(w[:, d, c0:c1], PS[4 + d][:, c0:c1], ACT.Exp, bias=a_cols[:, col:col + 1],
                                 scale=-1.0)
                last.then_inc(decay_done, 1)
                take_gate(pieces_before(0), h, PS[7], ACT.Sigmoid)
            roots(HEAD_NORMS[0], H)
            copy_transposes(U_Y0)
            roots(LAYER_NORMS[0])

        def gla():
            copy_transposes(U_X1)
            act.wait_ge(glr_done, 1)
            f(glrT, PS[4][0:2 * RANK, 0:S], ACT.Copy).then_inc(glr_copied, 1)
            take_projection(1, T_GLA, 0)
            act.wait_ge(glr_done, 2)
            f(gate_b_cols, PS[5][:, 0:8], ACT.Copy).then_inc(glr_copied, 1)
            act.wait_ge(z_ready, 1)
            link(f(acc_t[:, :], b_t, ACT.Abs))
            link(f(acc_t[:, :], acc_t[:, :], ACT.Exp, scale=-1.0))
            f(acc_t[:, :], acc_t[:, :], ACT.Ln, bias=1.0).then_inc(z_soft, 1)
            take_projection(1, T_GLA, 1)
            for n in range(2):
                take_values(n, PS[n])
            for i in range(2 * (len(LEVELS) + 1)):
                d = i % 2
                act.wait_ge(diffs_done, i + 1)
                if i >= 2:
                    act.wait_ge(scaled_done, i - 1)
                for w in range(2):
                    last = f(PS[4 + 2 * d + w][:, :], diffs[:, w], ACT.Exp, scale=1.0 / GLA_TAU)
                last.then_inc(decays_exp, 1)
                n = i // 2 + 2
                if d == 1 and n < 4:
                    take_values(n, PS[2 + n % 2])
                elif d == 1 and n < 6:
                    take_gate(pieces_before(1) + 4, n - 4, PS[2 + n % 2], ACT.Silu)
            act.wait_ge(decays_exp, 2 * (len(LEVELS) + 1))
            for n in (2, 3):
                take_gate(pieces_before(1) + 4, n, PS[2 + n % 2], ACT.Silu)
            roots(HEAD_NORMS[1], H)
            copy_transposes(U_Y1)
            roots(LAYER_NORMS[2])

        def moe(layer, use):
            copy_transposes(use)
            act.wait_ge(logits_part, layer + 1)
            f(part_t, PS[0][:, 0:S], ACT.Copy).then_inc(logits_copied, 1)
            act.wait_ge(router_max, layer + 1)
            for tt in range(TT):
                last = f(aff[:, tt, :], PS[1][:, tt * E:(tt + 1) * E], ACT.Exp, bias=row_max_r[:, tt:tt + 1],
                         accum_out=row_sum_r[:, tt:tt + 1])
            last.then_inc(aff_exp, 1)
            base, n0, m0 = T_MOE[layer], E * layer, NG * layer
            with act.Fori(0, NG) as g:
                act.wait_ge(xin_done, g * 2 + (2 * m0 + 1))
                f(xin_t[:, 0:512], PS[0][:, :], ACT.Copy).then_inc(xin_act, 1)
                for j in range(EG):
                    act.wait_ge(tile_used, g * (EG * TPE) + (base + TPE * j + 2))
                    act.wait_ge(hid_done, g * EG + (n0 + j + 1))
                    f(silu_g, PS[2][:, 0:S], ACT.Silu).then_inc(silu_done, 1)
                    act.wait_ge(turned, g * EG + (n0 + j + 2))
                    act.wait_ge(comb_done, g * (2 * EG) + (2 * (n0 + j) + 1))
                    f(turned_t, PS[2][:, :], ACT.Copy).then_inc(turned_copied, 1)
                    act.wait_ge(tile_used, g * (EG * TPE) + (base + TPE * j + 6))
                    f(exp_t[:, 0:512], PS[0][:, :], ACT.Copy).then_inc(exp_act, 1)
            roots(LAYER_NORMS[2 * layer + 1])

        def rms_roots(u):
            for tt in range(TT):
                c = slice(tt, tt + 1)
                act.wait_ge(x_sum, TT * u + tt + 1)
                link(f(acc[:, tt], x_tok[:, tt], ACT.Square, accum_out=square_sum[:, c]))
                f(deviation[:, c], square_sum[:, c], ACT.Sqrt, scale=1.0 / D, bias=rms_eps).then_inc(root_done, 1)

        def attention():
            rms_roots(0)
            copy_transposes(U_ATT)
            for i in range(6):
                take_projection(2, T_QKV, i)

            def exps(h):
                act.wait_ge(max_done, h + 1)
                if h >= 2:
                    act.wait_ge(pt_done, h - 1)
                b, c = PS[2 + h % 4], 2 * (h % 2)
                f(probs[:, h % 2, 0:P], b[:, 0:P], ACT.Exp, bias=neg_max[:, c:c + 1],
                  accum_out=prob_sum[:, c:c + 1])
                f(probs[:, h % 2, P:P + S], b[:, P:P + S], ACT.Exp, bias=neg_max[:, c + 1:c + 2],
                  accum_out=prob_sum[:, c + 1:c + 2]).then_inc(probs_exp, 1)

            exps(0)
            for h in range(AH):
                if h + 1 < AH:
                    exps(h + 1)
                act.wait_ge(pt_done, h + 1)
                if h >= 2:
                    act.wait_ge(o_done, h - 1)
                f(probsT[:, h % 2], PS[6 + h % 2][:, 0:3 * P], ACT.Copy).then_inc(pt_copied, 1)

        def ffn():
            rms_roots(1)
            copy_transposes(U_FFN)
            act.wait_ge(convT_done, 1)
            f(convw_t, PS[6][:, 0:8 * FB], ACT.Copy).then_inc(convT_copied, 1)
            act.wait_ge(convT_copied, 1)

            def taps(i):
                act.wait_ge(tile_used, T_UP + i + 1)
                if i >= 2:
                    act.wait_ge(ff_ready, i - 1)
                for c in range(4):
                    n = 2 * i + c % 2 + FB * (c // 2)
                    last = f(conv[:, i % 2, c], PS[2 * (i % 3) + c // 2][:, (c % 2) * S:(c % 2 + 1) * S],
                             ACT.Identity, scale=conv_cols[:, 2, n:n + 1], bias=conv_cols[:, 3, n:n + 1])
                last.then_inc(taps_done, 1)

            taps(0)
            for i in range(UPT):
                if i + 1 < UPT:
                    taps(i + 1)
                act.wait_ge(conv_done, i + 1)
                f(conv[:, i % 2, 0:2], conv[:, i % 2, 0:2], ACT.Silu).then_inc(ff_silu, 1)
            rms_roots(2)

        act.sem_inc(silu_done, 1)
        mlstm()
        moe(0, U_M0)
        gla()
        moe(1, U_M1)
        attention()
        ffn()

    @block.vector
    def _(dve):
        v = nc.vector
        chain = Chain(dve, dve_seq)
        link = chain.link

        def copy_transposes(use):
            for b in (1, 3):
                dve.wait_ge(tr_done, 4 * use + b + 1)
                v.tensor_copy(xT_t[:, b * 512:(b + 1) * 512], PS[b][:, :]).then_inc(tr_dve, 1)

        def take_projection(stage, n, i):
            dve.wait_ge(tile_used, n + i + 1)
            b = PS[2 * (i % 2) + 1]
            if stage == 2:
                if i < 4:
                    last = v.tensor_scalar(aqk_t[:, (4 * i + 2) * S:(4 * i + 4) * S], b[:, :],
                                           AD ** -0.5 if i < 2 else 1.0, None, ALU.mult)
                else:
                    last = v.tensor_copy(av[:, 1, (i - 4) * 512:(i - 3) * 512], b[:, :])
            elif i < 2:
                last = v.tensor_scalar(qkT_t[:, i * H * S + 512:(i + 1) * H * S], b[:, :],
                                       DK ** -0.5 if i == 0 else 1.0, None, ALU.mult)
            else:
                last = v.tensor_copy(v_aug[:, 1, 2 * (i - 2):2 * (i - 1), 0:DV],
                                     b[:, :].rearrange("p (h w) -> p h w", w=DV))
            last.then_inc(proj_dve, 1)

        def head_norm(layer, tt, src):
            n0 = tt * H
            dve.wait_ge(root_done, roots_before(HEAD_NORMS[layer]) + tt + 1)
            link(v.reciprocal(inv_spread[:, n0:n0 + H], deviation[:, n0:n0 + H]))
            for h in range(H):
                last = v.tensor_scalar(PS[4 + 2 * tt + h // 2][:, (h % 2) * DV:(h % 2 + 1) * DV], src(h),
                                       meanvar[:, n0 + h, 0:1], inv_spread[:, n0 + h:n0 + h + 1],
                                       ALU.subtract, ALU.mult)
            link(last)
            dve.wait_ge(gate_ready, 2 * (layer + 1))
            for j in range(2):
                c = slice(j * 512, (j + 1) * 512)
                last = v.tensor_tensor(acc[:, tt, c], PS[4 + 2 * tt + j][:, :], gate[:, tt, c], ALU.mult)
            last.then_inc(tokens_ready, 1)

        def layer_norm(use, tt):
            halves = [PS[4 + 2 * tt][:, :], PS[5 + 2 * tt][:, :]]
            for j in range(2):
                last = v.bn_stats(stats[:, 2 * tt + j], halves[j])
            link(last)
            v.bn_aggr(meanvar[:, tt], stats[:, 2 * tt:2 * tt + 2].rearrange("p n s -> p (n s)")
                      ).then_inc(var_ready, 1)
            dve.wait_ge(var_ready, roots_before(LAYER_NORMS[use]) + tt + 1)
            if tt == 0:
                dve.wait_ge(rows_landed, 32 * (use + 1))
            for j in range(2):
                v.scalar_tensor_tensor(halves[j], halves[j], meanvar[:, tt, 0:1],
                                       gain_row[:, j * 512:(j + 1) * 512], ALU.subtract, ALU.mult)
            dve.wait_ge(root_done, roots_before(LAYER_NORMS[use]) + tt + 1)
            link(v.reciprocal(inv_spread[:, tt:tt + 1], deviation[:, tt:tt + 1]))
            for j in range(2):
                c = slice(j * 512, (j + 1) * 512)
                last = v.scalar_tensor_tensor(x_tok[:, tt, c], halves[j], inv_spread[:, tt:tt + 1],
                                              bias_row[:, c], ALU.mult, ALU.add)
            last.then_inc(tokens_ready, 1)

        def residual_norm(use, n):
            def add(tt, j):
                return v.scalar_tensor_tensor(PS[4 + 2 * tt + j][:, :], x_tok[:, tt, j * 512:(j + 1) * 512], ALPHA,
                                              PS[4 + 2 * tt + j][:, :], ALU.mult, ALU.add)
            dve.wait_ge(tile_used, n + 1)
            add(0, 0)
            add(1, 0)
            for tt in range(TT):
                if tt == 0:
                    dve.wait_ge(out_rows, use // 2 + 1)
                else:
                    dve.wait_ge(tile_used, n + 2)
                link(add(tt, 1))
                layer_norm(use, tt)

        def mlstm():
            copy_transposes(U_X0)
            dve.wait_ge(gates_split, 1)
            fg, ig = PS[6][0:H, :], PS[5][0:H, :]
            dve.wait_ge(gate_soft, 1)
            link(v.scalar_tensor_tensor(row_m, fg, 0.0, row_soft, ALU.min, ALU.subtract))
            dve.wait_ge(ones_ready, 1)
            one = ones[0:H, 0:1].to_broadcast([H, S])

            def along(ap, d):
                r = ap[:, d * S:(d + 1) * S]
                return r if d == 0 else r[:, ::-1]

            for d in range(2):
                last = v.tensor_tensor_scan(along(row_b, d), one, along(row_m, d), 0.0, ALU.mult, ALU.add)
            link(last)
            link(v.tensor_tensor(row_a, ig, row_b, ALU.subtract))
            for d in range(2):
                last = v.tensor_tensor_scan(along(row_max, d), one, along(row_a, d), 0.0, ALU.mult, ALU.max)
            link(last)
            v.tensor_tensor(row_m, row_b, row_max, ALU.add).then_inc(gate_rows, 1)
            for i in range(4):
                take_projection(0, T_MLSTM, i)

            def weigh(h):
                dve.wait_ge(decay_done, h + 1)
                dve.wait_ge(scores_done, h + 1)
                w, sc = decay[:, h % 2], PS[6]
                for d, c, n, q in ((0, 0, 256, 0), (0, 256, 128, 384), (1, 0, 128, 0), (1, 128, 256, 256)):
                    last = v.tensor_tensor(w[:, d, c:c + n], w[:, d, c:c + n], sc[:, q:q + n], ALU.mult)
                last.then_inc(weights_done, 1)

            def take_head(h):
                dve.wait_ge(num_done, h + 1)
                for o in range(4):
                    last = v.tensor_reduce(den[:, o:o + 1], PS[o][:, DV:VW], AX.X, ALU.max,
                                           apply_absolute_value=True)
                link(last)
                floor = floor_cols.rearrange("p (d t h) -> p t d h", d=2, t=TT)[:, :, :, h]
                dens = den.rearrange("p (t d) -> p t d", t=TT)
                link(v.tensor_tensor(dens, dens, floor, ALU.max))
                link(v.reciprocal(inv_den, den))
                for tt in range(TT):
                    last = v.tensor_scalar(acc[:, tt, h * DV:(h + 1) * DV], PS[2 * tt][:, 0:DV],
                                           inv_den[:, 2 * tt:2 * tt + 1], None, ALU.mult)
                link(last)
                for tt in range(TT):
                    last = v.scalar_tensor_tensor(acc[:, tt, h * DV:(h + 1) * DV], PS[2 * tt + 1][:, 0:DV],
                                                  inv_den[:, 2 * tt + 1:2 * tt + 2], acc[:, tt, h * DV:(h + 1) * DV],
                                                  ALU.mult, ALU.add)
                last.then_inc(head_out, 1)
                dve.wait_ge(head_out, h + 1)
                for tt in range(TT):
                    last = v.bn_stats(stats[:, tt * H + h], acc[:, tt, h * DV:(h + 1) * DV])
                link(last)
                for tt in range(TT):
                    last = v.bn_aggr(meanvar[:, tt * H + h], stats[:, tt * H + h])
                if h == H - 1:
                    last.then_inc(var_ready, 2)

            dve.wait_ge(gate_scalars, 1)
            dve.wait_ge(masks_ready, 1)
            for h in range(H):
                weigh(h)
                take_head(h)
            dve.wait_ge(var_ready, 2)
            for tt in range(TT):
                head_norm(0, tt, lambda h: acc[:, tt, h * DV:(h + 1) * DV])
            copy_transposes(U_Y0)
            residual_norm(0, T_MLSTM + 6)

        def gla():
            copy_transposes(U_X1)
            take_projection(1, T_GLA, 0)
            dve.wait_ge(z_done, 1)
            dve.wait_ge(glr_copied, 2)
            for n in range(2 * H):
                last = v.tensor_scalar(b_cum[:, n], PS[4 + n // 2][:, (n % 2) * S:(n % 2 + 1) * S],
                                       gate_b_cols[:, n:n + 1], None, ALU.add)
            last.then_inc(z_ready, 1)
            dve.wait_ge(z_soft, 1)
            link(v.scalar_tensor_tensor(acc_t[:, :], b_t, 0.0, acc_t[:, :], ALU.min, ALU.subtract))
            for n in range(2 * H):
                o, i = b_cum[:, n], acc_t[:, n * S:(n + 1) * S]
                if n >= H:
                    o, i = o[:, ::-1], i[:, ::-1]
                last = v.tensor_tensor_scan(o, ones[:, 0:1].to_broadcast([P, S]), i, 0.0, ALU.mult, ALU.add)
            last.then_inc(b_ready, 1)
            dve.wait_ge(b_ready, 1)
            take_projection(1, T_GLA, 1)
            dve.wait_ge(proj_act, taken(1, 1))
            dve.wait_ge(proj_dve, taken(1, 1))

            def scale(i):
                d, L = i % 2, P >> (i // 2)
                dve.wait_ge(decays_exp, i + 1)
                if i >= 2:
                    dve.wait_ge(prod_done, i - 1)
                qv = qT.rearrange("p (n w l) -> p n w l", w=2, l=L)
                kv = kT.rearrange("p (n w l) -> p n w l", w=2, l=L)
                ko = k_dec[:, d].rearrange("p (n w l) -> p n w l", w=2, l=L)
                hq, hk = (1, 0) if d == 0 else (0, 1)
                v.tensor_tensor(q_dec[:, d].rearrange("p (n l) -> p n l", l=L), qv[:, :, hq, :],
                                PS[4 + 2 * d][:, :].rearrange("p (n l) -> p n l", l=L), ALU.mult)
                v.tensor_tensor(ko[:, :, hk, :], kv[:, :, hk, :],
                                PS[5 + 2 * d][:, :].rearrange("p (n l) -> p n l", l=L), ALU.mult
                                ).then_inc(scaled_done, 1)

            def place(i):
                d, L = i % 2, P >> (i // 2)
                dve.wait_ge(prod_done, i + 1)
                if i >= 1:
                    dve.wait_ge(placed, i)
                if i < 2:
                    last = v.tensor_copy(A[:, d, :, (1 - d) * P:(2 - d) * P],
                                         PS[d][:, :].rearrange("p (h n) -> p h n", h=H))
                else:
                    mask = level_masks[:, (d * len(LEVELS) + i // 2 - 1) * 64:(d * len(LEVELS) + i // 2) * 64]
                    for s in range(TT):
                        to = A[:, s, :, s * P:(s + 1) * P].rearrange("p h (n w l) -> p h n w l", w=2, l=L)
                        src = PS[d][:, s * H * 64:(s + 1) * H * 64]
                        pick = mask.rearrange("p (n l) -> p n l", l=L).unsqueeze(1)
                        last = v.copy_predicated(to[:, :, :, 1 - d, :], pick.to_broadcast([P, H, 64 // L, L]),
                                                 src.rearrange("p (h n l) -> p h n l", h=H, l=L))
                last.then_inc(placed, 1)

            for tt in range(TT):
                dve.wait_ge(diag_done, tt + 1)
                last = v.scalar_tensor_tensor(A[:, tt, :, tt * P:(tt + 1) * P],
                                              PS[2 + tt][:, :].rearrange("p (h n) -> p h n", h=H), 2.0,
                                              ident.unsqueeze(1).to_broadcast([P, H, P]), ALU.mult, ALU.mult)
            last.then_inc(diag_placed, 1)
            dve.wait_ge(diag_placed, 1)
            scale(0)
            scale(1)
            n_levels = 2 * (len(LEVELS) + 1)
            for i in range(n_levels):
                place(i)
                if i + 2 < n_levels:
                    scale(i + 2)
            for tt in range(TT):
                def out_of(h):
                    return PS[4 + 2 * tt + h // 2][:, (h % 2) * DV:(h % 2 + 1) * DV]
                dve.wait_ge(gla_out, tt + 1)
                for h in range(H):
                    last = v.bn_stats(stats[:, tt * H + h], out_of(h))
                link(last)
                for h in range(H):
                    last = v.bn_aggr(meanvar[:, tt * H + h], stats[:, tt * H + h])
                last.then_inc(var_ready, 1)
                dve.wait_ge(var_ready, roots_before(HEAD_NORMS[1]) + tt + 1)
                head_norm(1, tt, out_of)
            copy_transposes(U_Y1)
            residual_norm(2, T_GLA + 6)

        def moe(layer, use):
            copy_transposes(use)
            dve.wait_ge(logits_done, layer + 1)
            v.tensor_reduce(row_max_r, PS[1][:, 0:TT * E].rearrange("p (t e) -> p t e", t=TT), AX.X, ALU.max,
                            negate=True).then_inc(router_max, 1)
            dve.wait_ge(aff_exp, layer + 1)
            link(v.reciprocal(inv_sum_r, row_sum_r))
            for tt in range(TT):
                last = v.tensor_scalar(aff[:, tt, :], aff[:, tt, :], inv_sum_r[:, tt:tt + 1], None, ALU.mult)
            last.then_inc(aff_ready, 1)
            dve.wait_ge(affT_done, layer + 1)
            work, pick, count = affT_t[0:E, :], picked_t[0:E, :], work_t[0:E, :]
            link(v.tensor_copy(work, PS[2][0:E, 0:S]))
            for r in range(CAP // 8):
                top = top8[:, 8 * r:8 * r + 8]
                link(v.max(top, work))
                link(v.match_replace(work, top, work, -1.0))
            link(v.tensor_scalar(pick, work, 0.0, None, ALU.is_lt))
            link(v.tensor_tensor_scan(count, ones[0:E, 0:1].to_broadcast([E, S]), pick, 0.0, ALU.mult, ALU.add))
            v.tensor_tensor(pick, pick, count, ALU.mult).then_inc(slots_ready, 1)
            dve.wait_ge(slotsT_done, layer + 1)
            for tt in range(TT):
                last = v.tensor_tensor(sel[:, tt].rearrange("p (e c) -> p e c", c=CAP),
                                       slot_ids.unsqueeze(1).to_broadcast([P, E, CAP]),
                                       PS[3][:, tt * E:(tt + 1) * E].unsqueeze(2).to_broadcast([P, E, CAP]),
                                       ALU.is_equal)
            last.then_inc(sel_ready, 1)
            dve.wait_ge(sel_ready, layer + 1)
            base, n0, m0 = T_MOE[layer], E * layer, NG * layer
            with dve.Fori(0, NG) as g:
                for j in range(EG):
                    dve.wait_ge(turned, g * EG + (n0 + j + 1))
                    for tt in range(TT):
                        last = v.tensor_tensor(
                            selg[:, tt].rearrange("p (q c) -> p q c", c=CAP),
                            sel[:, tt, bass.ds(g * P + j * CAP, CAP)].unsqueeze(1).to_broadcast([P, 4, CAP]),
                            aff[:, tt, bass.ds(g * EG + j, 1)].unsqueeze(2).to_broadcast([P, 4, CAP]), ALU.mult)
                    last.then_inc(selg_ready, 1)
                    if j == 0:
                        dve.wait_ge(xin_done, g * 2 + (2 * m0 + 2))
                        v.tensor_copy(xin_t[:, 512:1024], PS[1][:, :]).then_inc(xin_dve, 1)
                    dve.wait_ge(silu_done, g * EG + (n0 + j + 2))
                    dve.wait_ge(tile_used, g * (EG * TPE) + (base + TPE * j + 4))
                    v.tensor_tensor(hid, silu_g, PS[3][:, 0:S], ALU.mult).then_inc(hid_done, 1)
                    dve.wait_ge(tile_used, g * (EG * TPE) + (base + TPE * j + 6))
                    dve.wait_ge(comb_done, g * (2 * EG) + (2 * (n0 + j) + 1))
                    v.tensor_copy(exp_t[:, 512:1024], PS[1][:, :]).then_inc(exp_dve, 1)
            for tt in range(TT):
                dve.wait_ge(comb_done, 2 * (n0 + E) + tt)
                layer_norm(2 * layer + 1, tt)
                if layer == 1:
                    dve.wait_ge(tokens_ready, tokens_before(U_ATT) - TT + tt + 1)
                    dve.sem_inc(x_sum, 1)

        def rms(u, gain, gain_sem, gain_count):
            for tt in range(TT):
                dve.wait_ge(root_done, roots_before(RMS_NORMS[u]) + tt + 1)
                link(v.reciprocal(inv_spread[:, tt:tt + 1], deviation[:, tt:tt + 1]))
                if tt == 0:
                    dve.wait_ge(gain_sem, gain_count)
                v.scalar_tensor_tensor(acc[:, tt], x_tok[:, tt], inv_spread[:, tt:tt + 1], gain,
                                       ALU.mult, ALU.mult).then_inc(tokens_ready, 1)

        def add_to_stream(u, n):
            for tt in range(TT):
                if tt == 0:
                    dve.wait_ge(out_rows, u + 2)
                else:
                    dve.wait_ge(tile_used, n + 1)
                for j in range(2):
                    dst = x_tok[:, tt, j * 512:(j + 1) * 512]
                    last = v.tensor_tensor(dst, dst, PS[4 + 2 * tt + j][:, :], ALU.add)
                last.then_inc(x_sum, 1)

        def attention():
            rms(0, attn_row, attn_row_landed, 16)
            copy_transposes(U_ATT)
            for i in range(6):
                take_projection(2, T_QKV, i)

            def maxima(h):
                dve.wait_ge(s_done, h + 1)
                b, c = PS[2 + h % 4], 2 * (h % 2)
                v.tensor_reduce(neg_max[:, c:c + 1], b[:, 0:P], AX.X, ALU.max, negate=True)
                v.tensor_reduce(neg_max[:, c + 1:c + 2], b[:, P:P + S], AX.X, ALU.max, negate=True
                                ).then_inc(max_done, 1)

            maxima(0)
            for h in range(AH):
                if h + 1 < AH:
                    maxima(h + 1)
                dve.wait_ge(probs_exp, h + 1)
                c, pr = 2 * (h % 2), probs[:, h % 2]
                link(v.reciprocal(inv_prob[:, c:c + 2], prob_sum[:, c:c + 2]))
                v.tensor_scalar(pr[:, 0:P], pr[:, 0:P], inv_prob[:, c:c + 1], None, ALU.mult)
                v.tensor_scalar(pr[:, P:P + S], pr[:, P:P + S], inv_prob[:, c + 1:c + 2], None, ALU.mult
                                ).then_inc(p_ready, 1)
                if h % 2 == 0 and h >= 2:
                    copy_heads(h // 2 - 1)
            copy_heads(AH // 2 - 1)
            add_to_stream(1, T_WO + 1)

        def copy_heads(pair):
            dve.wait_ge(o_done, 2 * pair + 2)
            v.tensor_copy(xT[:, pair, :], PS[pair % 2][:, 0:S]).then_inc(o_copied, 1)

        def ffn():
            rms(1, bias_row, rows_landed, 32 * 4 + 16)
            copy_transposes(U_FFN)
            dve.wait_ge(convT_copied, 1)

            def convolve(i):
                dve.wait_ge(taps_done, i + 1)
                for back in (1, 2):
                    for c in range(4):
                        n = 2 * i + c % 2 + FB * (c // 2)
                        u = PS[2 * (i % 3) + c // 2][:, (c % 2) * S:(c % 2 + 1) * S - back]
                        dst = conv[:, i % 2, c, back:S]
                        last = v.scalar_tensor_tensor(dst, u, conv_cols[:, 2 - back, n:n + 1], dst, ALU.mult, ALU.add)
                    if back == 1:
                        link(last)
                last.then_inc(conv_done, 1)

            convolve(0)
            for i in range(UPT):
                if i + 1 < UPT:
                    convolve(i + 1)
                dve.wait_ge(ff_silu, i + 1)
                dve.wait_ge(conv_done, i + 1)
                v.tensor_tensor(ffh[:, 2 * i:2 * i + 2, :], conv[:, i % 2, 0:2], conv[:, i % 2, 2:4], ALU.mult
                                ).then_inc(ff_ready, 1)
            add_to_stream(2, T_DOWN + N_DOWN - 1)
            rms(2, ng_t[:, :], gain_landed, 48)

        dve.sem_inc(hid_done, 1)
        mlstm()
        moe(0, U_M0)
        gla()
        moe(1, U_M1)
        attention()
        ffn()


_INS = ["x", "mlstm_w_in", "mlstm_gate_b", "mlstm_norm_g", "mlstm_w_out", "gla_w_in", "gla_gate_w",
        "gla_gate_b", "gla_norm_g", "gla_w_out", "moe_router", "moe_w_gate", "moe_w_up", "moe_w_down",
        "ln_g", "ln_b", "attn_norm_2", "w_qkv_2", "w_o_2", "rel_bias_2", "ffn_norm_2", "w_up_2",
        "conv_w_2", "conv_b_2", "w_down_2", "final_norm_2"]


def kernel(**inputs):
    import concourse.bacc as bacc
    from concourse.bass_utils import run_bass_kernel_spmd

    nc = bacc.Bacc("TRN2", target_bir_lowering=False, num_devices=1)
    main, masks, onehot = constants()
    arrays = {name: np.ascontiguousarray(inputs[name]) for name in _INS}
    arrays |= {"const_main": main, "const_masks": masks, "const_onehot": onehot}
    tensors = {name: nc.dram_tensor(f"in_{name}", a.shape, mybir.dt.from_np(a.dtype), kind="ExternalInput").ap()
               for name, a in arrays.items()}
    out = nc.dram_tensor("out_x", (1, S, D), F32, kind="ExternalOutput").ap()
    build(nc, tensors, out)
    r = run_bass_kernel_spmd(nc, [{f"in_{name}": a for name, a in arrays.items()}], core_ids=[0])
    return r.results[0]["out_x"]
```

```python
import math
from contextlib import ExitStack

import numpy as np
import concourse.bass as bass
from concourse import mybir

ALU = mybir.AluOpType
ACT = mybir.ActivationFunctionType
AX = mybir.AxisListType
F32 = mybir.dt.float32
U8 = mybir.dt.uint8

P = 128
S = 256
TT = S // P
D = 1024
KC = D // P
DEPTH = 2
ALPHA = (2 * DEPTH) ** 0.25
LN_EPS = 1e-5
RMS_EPS = 1e-6
BIG = 1e30

H = 4
DK = 128
DV = 256
VW = DV + 1
GLA_TAU = 16.0
RANK = 16

E = 16
CAP = 2 * S // E
EG = P // CAP
NG = E // EG

AH = 16
AD = 64
BUCKETS = 32
MAXDIST = 128
FF = 2816
FB = FF // P
UPT = FF // S

SLOTS = 8
TILE = 4096
TPE = 6
T_MLSTM = 0
T_MOE = [8, 112]
T_GLA = 104
T_QKV = 208
T_WO = 214
T_UP = 216
T_DOWN = T_UP + UPT
N_DOWN = (FB + 3) // 4
LEVELS = [64, 32, 16, 8, 4, 2, 1]
WROW = 3 * P


def constants():
    i = np.arange(P)
    ident = np.eye(P, dtype=np.float32)
    flip = ident[::-1].copy()
    after = np.where(i[:, None] > i[None, :], BIG, 0).astype(np.float32)
    before = np.where(i[:, None] < i[None, :], BIG, 0).astype(np.float32)
    slots = np.tile(np.arange(1, CAP + 1, dtype=np.float32), (P, 1))
    n = np.arange(DEPTH * E)
    logit_of = (i[:, None] % (DEPTH * E) == n[None, :]).astype(np.float32)
    main = np.concatenate([ident, flip, after, before, slots, logit_of], 1)
    n = np.arange(64)
    masks = np.zeros((P, 2, len(LEVELS), 64), np.float32)
    for lv, L in enumerate(LEVELS):
        same = (i[:, None] // (2 * L)) == (n[None, :] // L)
        left = ((i % (2 * L)) < L)[:, None]
        masks[:, 0, lv] = same & left
        masks[:, 1, lv] = same & ~left
    dist = np.arange(S)[::-1]
    half = BUCKETS // 2
    nf = np.maximum(dist, 1).astype(np.float32)
    large = half + (np.log(nf / np.float32(half)) / np.float32(math.log(MAXDIST / half))
                    * np.float32(BUCKETS - half)).astype(np.int32)
    bucket = np.where(dist < half, dist, np.minimum(large, BUCKETS - 1))
    onehot = (np.arange(BUCKETS)[:, None] == bucket[None, :]).astype(np.float32)
    return main, masks.reshape(P, -1), onehot


def build(nc, t, out):
    with ExitStack() as ctx:
        build_in(nc, t, out, ctx)


def build_in(nc, t, out, ctx):
    def sem(name):
        return ctx.enter_context(nc.semaphore(name))

    def sbuf(name, cols, dt=F32):
        return ctx.enter_context(nc.sbuf_tensor(name, [P, cols], dt))

    ring = sbuf("weight_ring", SLOTS * TILE)
    consts = sbuf("consts", 4 * P + CAP + DEPTH * E)
    ident = consts[:, 0:P]
    flip = consts[:, P:2 * P]
    mask_after = consts[:, 2 * P:3 * P]
    mask_before = consts[:, 3 * P:4 * P]
    slot_ids = consts[:, 4 * P:4 * P + CAP]
    logit_of = consts[:, 4 * P + CAP:4 * P + CAP + DEPTH * E]
    ones = sbuf("ones", 8)
    ln_eps, rms_eps = ones[:, 1:2], ones[:, 2:3]
    router_t = sbuf("router", DEPTH * KC * E)
    level_masks = sbuf("level_masks", 2 * len(LEVELS) * 64, U8)
    x_tok_t = sbuf("x_tok", TT * D)
    xT_t = sbuf("xT", KC * S)
    acc_t = sbuf("acc", TT * D)
    gb_t = sbuf("norm_rows", 2 * D)
    ng_t = sbuf("head_gain", D)
    small = sbuf("small", 256)
    wglr_t = sbuf("gla_gate_columns", KC * 2 * RANK)
    room = sbuf("phase_room", 9600)

    x_tok = x_tok_t[:, :].rearrange("p (t d) -> p t d", t=TT)
    acc = acc_t[:, :].rearrange("p (t d) -> p t d", t=TT)
    xT = xT_t[:, :].rearrange("p (k s) -> p k s", k=KC)
    gain_row = gb_t[:, 0:D]
    bias_row = gb_t[:, D:2 * D]

    def rooms(*sizes):
        at, got = 0, []
        for n in sizes:
            got.append(room[:, at:at + n])
            at += n
        assert at <= 9600, at
        return got

    stats = small[:, 0:48].rearrange("p (n s) -> p n s", s=6)
    meanvar = small[:, 48:64].rearrange("p (n s) -> p n s", s=2)
    inv_spread = small[:, 72:80]
    deviation = small[:, 64:72]

    qkT_t, v_t, gate_t, mix_t = rooms(2 * H * S, TT * H * VW, TT * D, 3448)
    qT = qkT_t[:, 0:H * S]
    kT = qkT_t[:, H * S:2 * H * S]
    v_aug = v_t.rearrange("p (t h w) -> p t h w", t=TT, w=VW)
    gate = gate_t.rearrange("p (t d) -> p t d", t=TT)
    gates_all = gate_t[0:16, 0:S]
    row_soft = mix_t[0:H, 248:760]
    row_m = mix_t[0:H, 760:1272]
    row_b = mix_t[0:H, 1272:1784]
    row_a = gb_t[0:H, 0:512]
    row_max = gb_t[0:H, 512:1024]
    wgate = mix_t[:, 1784:1784 + 128].rearrange("p (k n) -> p k n", k=KC)
    decay = mix_t[:, 1912:1912 + 2 * 2 * 384].rearrange("p (b d n) -> p b d n", b=2, d=2)
    gate_bias = small[0:16, 80:81]
    a_cols = small[:, 96:112]
    floor_cols = small[:, 112:128]
    den = small[:, 128:132]
    inv_den = small[:, 132:136]
    b_t = mix_t[:, 0:2 * H * S]
    b_cum = b_t.rearrange("p (n s) -> p n s", s=S)
    q_dec = mix_t[:, 2048:3072].rearrange("p (d n) -> p d n", d=2)
    wglr = wglr_t[:, :].rearrange("p (k n) -> p k n", k=KC)
    k_dec = acc_t[:, :].rearrange("p (d n) -> p d n", d=2)
    diffs = gate[:, :, 512:1024]
    gate_w_sb = room[0:2 * RANK, 7840:8864].rearrange("p (d n) -> p d n", d=2)
    gate_b_rows = room[0:8, 8864:8992]
    glrT = room[0:2 * RANK, 8992:9248]
    attn_row = room[:, 7840:8864]
    gate_b_cols = small[:, 80:88]
    A = gb_t[:, :].rearrange("p (s h t) -> p s h t", s=TT, h=H)

    (xin_t, sel_t, selg_t, turned_t, hid, silu_g, exp_t, aff_t,
     affT_t, work_t, picked_t, part_t) = rooms(
        1024, 1024, S, 2 * S, S, S, 1024, 32, 256, 256, 256, S)
    xinT = xin_t.rearrange("p (k n) -> p k n", k=KC)
    sel = sel_t.rearrange("p (t n) -> p t n", t=TT)
    selg = selg_t.rearrange("p (t n) -> p t n", t=TT)
    hidT = turned_t[:, 0:S].rearrange("p (c n) -> p c n", c=2)
    selT = turned_t[:, S:2 * S]
    w_router = router_t[:, :].rearrange("p (k l n) -> p k l n", l=DEPTH, k=KC)
    aff = aff_t.rearrange("p (t e) -> p t e", t=TT)
    top8 = small[0:E, 160:192]
    row_max_r = small[:, 136:138]
    row_sum_r = small[:, 138:140]
    inv_sum_r = small[:, 140:142]

    aqk_t, av_t, prob_t, probT_t = rooms(16 * S, TT * D, 768, 768)
    aqk = aqk_t.rearrange("p (n s) -> p n s", s=S)
    av = av_t.rearrange("p (t d) -> p t d", t=TT)
    probs = prob_t.rearrange("p (b n) -> p b n", b=2)
    probsT = probT_t.rearrange("p (b n) -> p b n", b=2)
    bias_flip = acc_t[:, :].rearrange("p (b h n) -> p b h n", b=2, h=4)
    neg_max = small[:, 144:148]
    prob_sum = small[:, 148:152]
    inv_prob = small[:, 152:156]
    rel_T = room[0:BUCKETS, 8900:8916]
    dist_hot = room[0:BUCKETS, 8400:8400 + S]
    bias_rows = room[0:AH, 8960:8960 + WROW]

    ffh_t, conv_t, convw_t, _ = rooms(FB * S, 2 * 1024, 4 * 2 * FB, 984)
    convrow_t = room[:, 8864:8864 + 4 * P]
    ffh = ffh_t.rearrange("p (n s) -> p n s", s=S)
    conv = conv_t.rearrange("p (b n s) -> p b n s", b=2, s=S)
    conv_cols = convw_t.rearrange("p (j n) -> p j n", j=4)
    conv_rows = convrow_t[0:2 * FB, :].rearrange("p (j n) -> p j n", j=4)
    square_sum = small[:, 156:158]

    PS = [ctx.enter_context(nc.psum_tensor(f"bank{i}", [P, 512], F32)) for i in range(8)]

    bias_dram = nc.dram_tensor("bias_rows_dram", (AH, WROW), F32, kind="Internal")

    landed = [sem(f"landed{i}") for i in range(SLOTS)]
    tile_used = sem("tile_used")
    const_landed = sem("const_landed")
    x_landed = [sem(f"x_landed{i}") for i in range(TT)]
    first_half_landed = sem("first_half_landed")
    small_landed = [sem(f"small_landed{i}") for i in range(6)]
    rows_landed = sem("rows_landed")
    gain_landed = sem("gain_landed")
    router_landed = sem("router_landed")
    attn_row_landed = sem("attn_row_landed")
    ones_ready = sem("ones_ready")
    masks_ready = sem("masks_ready")
    tokens_ready = sem("tokens_ready")
    tr_done = sem("tr_done")
    tr_act, tr_dve = sem("tr_act"), sem("tr_dve")
    proj_act, proj_dve = sem("proj_act"), sem("proj_dve")
    piece_done = sem("piece_done")
    piece_out = sem("piece_out")
    gate_ready = sem("gate_ready")
    out_rows = sem("out_rows")
    var_ready = sem("var_ready")
    root_done = sem("root_done")
    x_sum = sem("x_sum")
    dve_seq, act_seq = sem("dve_seq"), sem("act_seq")
    gates_done = sem("gates_done")
    gates_biased = sem("gates_biased")
    gates_split = sem("gates_split")
    gate_soft = sem("gate_soft")
    gate_rows = sem("gate_rows")
    gate_columns = sem("gate_columns")
    gate_scalars = sem("gate_scalars")
    mb_done, scores_done = sem("mb_done"), sem("scores_done")
    decay_done = sem("decay_done")
    weights_done = sem("weights_done")
    num_done = sem("num_done")
    head_out = sem("head_out")
    glr_done, glr_copied = sem("glr_done"), sem("glr_copied")
    glr_zero = sem("glr_zero")
    z_done, z_ready, z_soft = sem("z_done"), sem("z_ready"), sem("z_soft")
    b_ready = sem("b_ready")
    diffs_done = sem("diffs_done")
    decays_exp = sem("decays_exp")
    scaled_done = sem("scaled_done")
    prod_done = sem("prod_done")
    placed = sem("placed")
    diag_done, diag_placed = sem("diag_done"), sem("diag_placed")
    gla_out = sem("gla_out")
    logits_part, logits_copied = sem("logits_part"), sem("logits_copied")
    logits_done = sem("logits_done")
    router_max, aff_exp, aff_ready = (
        sem("router_max"), sem("aff_exp"), sem("aff_ready"))
    affT_done = sem("affT_done")
    slots_ready, slotsT_done = sem("slots_ready"), sem("slotsT_done")
    sel_ready = sem("sel_ready")
    alpha_x = sem("alpha_x")
    xin_done, xin_act, xin_dve = (
        sem("xin_done"), sem("xin_act"), sem("xin_dve"))
    selg_ready = sem("selg_ready")
    turned_copied = sem("turned_copied")
    exp_act, exp_dve = sem("exp_act"), sem("exp_dve")
    silu_done = sem("silu_done")
    hid_done = sem("hid_done")
    turned = sem("turned")
    comb_done = sem("comb_done")
    relb_done, relb_copied, relb_stored = sem("relb_done"), sem("relb_copied"), sem("relb_stored")
    bias_landed = [sem("bias_landed0"), sem("bias_landed1")]
    s_done, max_done, probs_exp, p_ready = sem("s_done"), sem("max_done"), sem("probs_exp"), sem("p_ready")
    pt_done, pt_copied, o_done, o_copied = sem("pt_done"), sem("pt_copied"), sem("o_done"), sem("o_copied")
    convT_done, convT_copied = sem("convT_done"), sem("convT_copied")
    taps_done, conv_done, ff_silu, ff_ready = sem("taps_done"), sem("conv_done"), sem("ff_silu"), sem("ff_ready")
    out_landed = sem("out_landed")

    def slot(n):
        s = n % SLOTS
        return ring[:, s * TILE:(s + 1) * TILE]

    def arrived(pe, n, more=0):
        pe.wait_ge(landed[n % SLOTS], 16 * (n // SLOTS + 1) + more)

    class Chain:
        def __init__(self, eng, s):
            self.eng, self.s, self.n = eng, s, 0

        def link(self, ins):
            self.n += 1
            ins.then_inc(self.s, 1)
            self.eng.wait_ge(self.s, self.n)

    U_X0, U_Y0, U_M0, U_X1, U_Y1, U_M1, U_ATT, U_FFN, U_OUT = range(9)

    def tokens_count(use, tt):
        if use == U_ATT:
            return TT * (use - 1) + 2 * (tt + 1)
        return TT * (use - 1 + (use >= U_ATT)) + tt + 1

    def taken(stage, i):
        return (0, 4, 6)[stage] + i + 1

    def pieces_before(layer):
        return 4 * layer

    HEAD_NORMS, LAYER_NORMS, RMS_NORMS = (0, 3), (1, 2, 4, 5), (6, 7, 8)

    def root_count(n, tt):
        if n in (LAYER_NORMS[3], RMS_NORMS[0]):
            return TT * LAYER_NORMS[3] + 2 * tt + (1 if n == LAYER_NORMS[3] else 2)
        return TT * n + tt + 1

    def var_count(n, tt):
        return TT * n + tt + 1

    block = ctx.enter_context(nc.Block())

    @block.sync
    def _(sp):
        def free(n):
            if n >= SLOTS:
                sp.wait_ge(tile_used, n - SLOTS + 1)

        def load(n, src, dst=None):
            free(n)
            sp.dma_start(slot(n) if dst is None else dst, src).then_inc(landed[n % SLOTS], 16)

        def columns(n, w, first, count):
            v = w.rearrange("(k p) n -> p k n", p=P)
            for j in range(count):
                load(n + j, v[:, :, first + 512 * j:first + 512 * (j + 1)],
                     slot(n + j).rearrange("p (k n) -> p k n", k=KC))

        def experts(layer):
            ws = [t[w][layer].rearrange("e (r k p) n -> e r p k n", p=P, k=4)
                  for w in ("moe_w_gate", "moe_w_up", "moe_w_down")]
            base = T_MOE[layer]
            with sp.Fori(0, NG) as g:
                for j in range(EG):
                    for c in range(TPE):
                        n = TPE * j + c
                        sp.wait_ge(tile_used, g * (EG * TPE) + (base + n - SLOTS + 1))
                        sp.dma_start(slot(n).rearrange("p (k n) -> p k n", k=4),
                                     ws[c // 2][bass.ds(g * EG + j, 1), c % 2].rearrange("e p k n -> p (e k) n")
                                     ).then_inc(landed[n % SLOTS], 16)

        for tt in range(TT):
            sp.dma_start(x_tok[:, tt], t["x"][0, tt * P:(tt + 1) * P]).then_inc(x_landed[tt], 16)
            if tt == 0:
                sp.dma_start(consts[:, :], t["const_main"]).then_inc(const_landed, 16)
        w_in = t["mlstm_w_in"][0].rearrange("(k p) n -> p k n", p=P)
        for c, s_ in ((0, first_half_landed), (S, landed[0])):
            sp.dma_start(slot(0).rearrange("p (k n) -> p k n", k=KC)[:, :, c:c + S], w_in[:, :, c:c + S]
                         ).then_inc(s_, 16)
        sp.dma_start(wgate, w_in[:, :, 3072:3088]).then_inc(small_landed[0], 16)
        sp.dma_start(gate_bias, t["mlstm_gate_b"][0].rearrange("a b (c o) -> (a b c) o", o=1)
                     ).then_inc(small_landed[0], 16)
        sp.dma_start(rel_T, t["rel_bias_2"].rearrange("h b -> b h"), allow_slow_non_contiguous=True
                     ).then_inc(small_landed[1], 16)
        sp.dma_start(dist_hot, t["const_onehot"]).then_inc(small_landed[1], 16)
        columns(T_MLSTM + 1, t["mlstm_w_in"][0], 512, 5)
        columns(T_MLSTM + 6, t["mlstm_w_out"][0], 0, 2)
        experts(0)
        columns(T_GLA, t["gla_w_in"][0], 2 * H * DK, 1)
        columns(T_GLA + 1, t["gla_w_in"][0], 0, 2)
        columns(T_GLA + 3, t["gla_w_in"][0], 2 * H * DK + 512, 3)
        columns(T_GLA + 6, t["gla_w_out"][0], 0, 2)
        experts(1)
        columns(T_QKV, t["w_qkv_2"][0], 2 * D, 1)
        columns(T_QKV + 1, t["w_qkv_2"][0], 0, 4)
        columns(T_QKV + 5, t["w_qkv_2"][0], 2 * D + 512, 1)
        columns(T_WO, t["w_o_2"][0], 0, 2)
        up = t["w_up_2"][0].rearrange("(k p) (h n) -> p k h n", p=P, h=2)
        for i in range(UPT):
            n = T_UP + i
            free(n)
            dst = slot(n).rearrange("p (k h n) -> p k h n", k=KC, h=2)
            for h in range(2):
                sp.dma_start(dst[:, :, h, :], up[:, :, h, S * i:S * (i + 1)]).then_inc(landed[n % SLOTS], 16)
        down = t["w_down_2"][0].rearrange("(k p) n -> p k n", p=P)
        for i in range(N_DOWN):
            n = T_DOWN + i
            k = min(4, FB - 4 * i)
            load(n, down[:, 4 * i:4 * i + k, :], slot(n)[:, 0:k * D].rearrange("p (k n) -> p k n", k=k))

    def up_landed(n):
        twice = sum(1 for m in range(T_UP, min(n + 1, T_DOWN)) if m % SLOTS == n % SLOTS)
        return 16 * (n // SLOTS + 1 + twice)

    @block.gpsimd
    def _(pool):
        def row(dst, src, s):
            pool.dma_start(dst, src.partition_broadcast(P)).then_inc(s, 16)

        def norm_rows(g, b):
            row(gain_row, g, rows_landed)
            row(bias_row, b, rows_landed)

        nc.gpsimd.memset(ones[:, 0:1], 1.0)
        nc.gpsimd.memset(ln_eps, LN_EPS)
        nc.gpsimd.memset(rms_eps, RMS_EPS).then_inc(ones_ready, 1)
        nc.gpsimd.memset(v_aug[:, :, :, DV:VW], 1.0).then_inc(ones_ready, 1)
        nc.gpsimd.memset(bias_rows[:, S:WROW], -BIG).then_inc(ones_ready, 1)
        masks_f32 = acc_t[:, 0:2 * len(LEVELS) * 64]
        pool.dma_start(masks_f32, t["const_masks"]).then_inc(small_landed[2], 16)
        row(ng_t[:, :], t["mlstm_norm_g"][0], gain_landed)
        for layer in range(DEPTH):
            pool.dma_start(w_router[:, :, layer], t["moe_router"][layer].rearrange("(k p) n -> p k n", p=P)
                           ).then_inc(router_landed, 16)
        pool.dma_start(wglr, t["gla_w_in"][0].rearrange("(k p) n -> p k n", p=P)[:, :, 3072:3104]
                       ).then_inc(small_landed[5], 16)
        pool.wait_ge(small_landed[2], 16)
        nc.gpsimd.tensor_copy(level_masks[:, :], masks_f32).then_inc(masks_ready, 1)
        pool.wait_ge(relb_copied, 1)
        pool.wait_ge(ones_ready, 3)
        pool.dma_start(bias_dram.ap(), bias_rows).then_inc(relb_stored, 16)

        def output_gate(layer, part):
            pool.wait_ge(piece_out, pieces_before(layer) + (4 if layer else 0) + 2 + part)
            pool.wait_ge(gain_landed, 16 * (layer + 1))
            c = slice(512 * min(part, 1), 512 * min(part, 1) + 512)
            for i in (range(TT) if part == 0 else (part - 1,)):
                last = nc.gpsimd.tensor_tensor(gate[:, i, c], gate[:, i, c], ng_t[:, c], ALU.mult)
            last.then_inc(gate_ready, 1)

        def moe_small(layer, u_moe):
            pool.wait_ge(tokens_ready, tokens_count(u_moe, TT - 1))
            for i in range(TT):
                last = nc.gpsimd.tensor_scalar(acc[:, i], x_tok[:, i], ALPHA, 0.0, ALU.mult, ALU.add)
            last.then_inc(alpha_x, 1)
            norm_rows(t["ln_g"][layer, 1], t["ln_b"][layer, 1])

        for part in range(3):
            output_gate(0, part)
        pool.wait_ge(weights_done, H)
        norm_rows(t["ln_g"][0, 0], t["ln_b"][0, 0])
        moe_small(0, U_M0)
        row(ng_t[:, :], t["gla_norm_g"][0], gain_landed)
        nc.gpsimd.memset(gate_w_sb, 0.0).then_inc(glr_zero, 1)
        pool.wait_ge(glr_zero, 1)
        for d in range(2):
            pool.dma_start(gate_w_sb[RANK * d:RANK * (d + 1), d], t["gla_gate_w"][0, d]).then_inc(small_landed[3], 16)
        pool.dma_start(gate_b_rows, t["gla_gate_b"][0].rearrange("d (n p) -> (d n) p", p=P)
                       ).then_inc(small_landed[3], 16)
        pool.wait_ge(b_ready, 1)
        for i in range(2 * (len(LEVELS) + 1)):
            d, L = i % 2, P >> (i // 2)
            b = b_t[:, d * H * S:(d + 1) * H * S].rearrange("p (n w l) -> p n w l", w=2, l=L)
            left, right = b[:, :, 0, :], b[:, :, 1, :]
            nb = H * S // (2 * L)
            border = (left[:, :, L - 1:L] if d == 0 else right[:, :, 0:1]).to_broadcast([P, nb, L])
            qs, ks = (right, left) if d == 0 else (left, right)
            if i >= 1:
                pool.wait_ge(decays_exp, i)
            dq = diffs[:, 0].rearrange("p (n l) -> p n l", l=L)
            dk = diffs[:, 1].rearrange("p (n l) -> p n l", l=L)
            nc.gpsimd.tensor_tensor(dq, qs, border, ALU.subtract)
            nc.gpsimd.tensor_tensor(dk, border, ks, ALU.subtract).then_inc(diffs_done, 1)
            if i == 10:
                output_gate(1, 0)
        for part in (1, 2):
            output_gate(1, part)
        pool.wait_ge(gla_out, TT)
        norm_rows(t["ln_g"][1, 0], t["ln_b"][1, 0])
        moe_small(1, U_M1)
        row(attn_row, t["attn_norm_2"][0], attn_row_landed)
        for j in range(3):
            pool.dma_start(conv_rows[:, j], t["conv_w_2"][0, j].rearrange("(n p) -> n p", p=P)
                           ).then_inc(small_landed[4], 16)
        pool.dma_start(conv_rows[:, 3], t["conv_b_2"][0].rearrange("(n p) -> n p", p=P)
                       ).then_inc(small_landed[4], 16)
        row(ng_t[:, :], t["final_norm_2"], gain_landed)
        pool.wait_ge(tokens_ready, tokens_count(U_ATT, TT - 1))
        row(bias_row, t["ffn_norm_2"][0], rows_landed)
        pool.wait_ge(relb_stored, 16)
        pool.wait_ge(tr_done, 4 * (U_ATT + 1))
        for g in range(AH // 4):
            if g >= 2:
                pool.wait_ge(s_done, 4 * (g - 1))
            src = bass.AP(bias_dram, 4 * g * WROW, [[1, P], [WROW, 4], [1, S]])
            pool.dma_start(bias_flip[:, g % 2], src).then_inc(bias_landed[g % 2], 16)
        for tt in range(TT):
            pool.wait_ge(tokens_ready, tokens_count(U_OUT, tt))
            pool.dma_start(out[0, tt * P:(tt + 1) * P], acc[:, tt]).then_inc(out_landed, 16)
        pool.wait_ge(out_landed, 16 * TT)

    @block.tensor
    def _(pe):
        mm = nc.tensor.matmul
        turn = nc.tensor.transpose

        def turn_tile(src, use, i):
            if use == U_X0:
                pe.wait_ge(x_landed[i], 16)
                pe.wait_ge(const_landed, 16)
            else:
                pe.wait_ge(tokens_ready, tokens_count(use, i))
            for k in range(KC):
                last = turn(PS[2 * i + k // 4][:, (k % 4) * P:(k % 4 + 1) * P], src[:, i, k * P:(k + 1) * P], ident)
                if k % 4 == 3:
                    last.then_inc(tr_done, 1)
            pe.wait_ge(tr_act, 3 * use + 2 + i)
            if i == 1:
                pe.wait_ge(tr_dve, use + 1)

        def transposes(src, use):
            for i in range(TT):
                turn_tile(src, use, i)

        def project(n, stage, i, channel_tiles):
            b0 = 2 * (i % 2)
            if n == 0:
                pe.wait_ge(first_half_landed, 16)
            else:
                arrived(pe, n)
            w = slot(n).rearrange("p (k n) -> p k n", k=KC)
            if i >= 2:
                pe.wait_ge(proj_act, taken(stage, i - 2))
                pe.wait_ge(proj_dve, taken(stage, i - 2))
            if i in channel_tiles:
                for c in range(4):
                    if n == 0 and c == 2:
                        arrived(pe, n)
                    for k in range(KC):
                        last = mm(PS[b0 + c // 2][:, (c % 2) * S:(c % 2 + 1) * S], w[:, k, c * P:(c + 1) * P],
                                  xT[:, k, :], start=(k == 0), stop=(k == KC - 1))
            else:
                for tt in range(TT):
                    for k in range(KC):
                        last = mm(PS[b0 + tt][:, :], xT[:, k, tt * P:(tt + 1) * P], w[:, k, :],
                                  start=(k == 0), stop=(k == KC - 1))
            last.then_inc(tile_used, 1)

        def piece(layer, n, p, bank, chunks=range(KC)):
            if p % 2 == 0 and chunks[0] == 0:
                arrived(pe, n)
            w = slot(n).rearrange("p (k n) -> p k n", k=KC)
            tt = p % 2
            for k in chunks:
                last = mm(bank[:, :], xT[:, k, tt * P:(tt + 1) * P], w[:, k, :],
                          start=(k == 0), stop=(k == KC - 1), skip_group_check=True)
            if chunks[-1] < KC - 1:
                return
            last.then_inc(piece_done, 1)
            if p % 2 == 1:
                pe.wait_ge(piece_done, pieces_before(layer) + p + 1)
                pe.sem_inc(tile_used, 1)

        def out_project(n, use=None):
            for j in range(2):
                if j == 1 or use is None:
                    arrived(pe, n + j)
                w = slot(n + j).rearrange("p (k n) -> p k n", k=KC)
                for tt in range(TT):
                    if j == 0 and use is not None:
                        turn_tile(acc, use, tt)
                        if tt == 0:
                            arrived(pe, n)
                    for k in range(KC):
                        last = mm(PS[4 + 2 * tt + j][:, :], xT[:, k, tt * P:(tt + 1) * P], w[:, k, :],
                                  start=(k == 0), stop=(k == KC - 1))
                    if j == 1 and tt == 0:
                        last.then_inc(out_rows, 1)
                last.then_inc(tile_used, 1)

        def mlstm():
            transposes(x_tok, U_X0)
            project(T_MLSTM, 0, 0, (0, 1))
            pe.wait_ge(small_landed[1], 32)
            mm(PS[7][0:AH, 0:S], rel_T, dist_hot, start=True, stop=True).then_inc(relb_done, 1)
            pe.wait_ge(small_landed[0], 32)
            for k in range(KC):
                last = mm(PS[4][0:16, 0:S], wgate[:, k, :], xT[:, k, :], start=(k == 0), stop=(k == KC - 1))
            last.then_inc(gates_done, 1)
            pe.wait_ge(gates_biased, 1)
            for d in range(2):
                for kind in range(2):
                    c = 4 * (2 * d + kind)
                    last = mm(PS[5 + kind][0:H, d * S:(d + 1) * S], ident[0:16, c:c + H], gates_all,
                              start=True, stop=True)
            last.then_inc(gates_split, 1)
            for i in range(1, 4):
                project(T_MLSTM + i, 0, i, (0, 1))
                if i == 1:
                    pe.wait_ge(gate_rows, 1)
                    pe.wait_ge(relb_copied, 1)
                    for q, rows in enumerate((row_a, row_m)):
                        for d in range(2):
                            for tt in range(TT):
                                c = ((q * 2 + d) * 2 + tt) * H
                                last = turn(PS[7][:, c:c + H], rows[:, d * S + tt * P:d * S + (tt + 1) * P],
                                            ident[0:H, 0:H])
                    last.then_inc(gate_columns, 1)
            pe.wait_ge(gate_scalars, 1)
            pe.wait_ge(ones_ready, 3)
            pe.wait_ge(proj_act, taken(0, 3))
            pe.wait_ge(proj_dve, taken(0, 3))

            def head_scores(h):
                if h >= 1:
                    pe.wait_ge(decay_done, h)
                pick = ident[0:H, h:h + 1].to_broadcast([H, P])
                for d in range(2):
                    b = PS[4 + d]
                    for s in range(TT):
                        t0, t1 = (s, TT) if d == 0 else (0, s + 1)
                        c0 = (0, 2)[s] if d == 0 else (0, 1)[s]
                        mm(b[:, c0 * P:(c0 + t1 - t0) * P], pick, row_max[:, d * S + t0 * P:d * S + t1 * P],
                           start=True, stop=False, skip_group_check=True)
                        cm = (c0 + s - t0) * P
                        last = mm(b[:, cm:cm + P], ident, mask_after if d == 0 else mask_before,
                                  start=False, stop=True, skip_group_check=True)
                last.then_inc(mb_done, 1)
                if h >= 1:
                    pe.wait_ge(weights_done, h)
                for s in range(TT):
                    last = mm(PS[6][:, s * S:(s + 1) * S], kT[:, h * S + s * P:h * S + (s + 1) * P],
                              qT[:, h * S:(h + 1) * S], start=True, stop=True)
                last.then_inc(scores_done, 1)

            def head_sums(h):
                pe.wait_ge(weights_done, h + 1)
                if h >= 1:
                    pe.wait_ge(head_out, h)
                w = decay[:, h % 2]
                for tt in range(TT):
                    for d in range(2):
                        srcs = range(tt + 1) if d == 0 else range(tt, TT)
                        for s in srcs:
                            c = ((0, 2)[s] + tt - s if d == 0 else (0, 1)[s] + tt) * P
                            last = mm(PS[2 * tt + d][:, 0:VW], w[:, d, c:c + P], v_aug[:, s, h, :],
                                      start=(s == srcs[0]), stop=(s == srcs[-1]))
                last.then_inc(num_done, 1)

            for h in range(H):
                head_scores(h)
                if h in (1, 2):
                    pe.wait_ge(piece_out, h)
                n, chunks = ((0, range(KC)), (1, range(KC)), (2, range(0, 4)), (2, range(4, KC)))[h]
                piece(0, T_MLSTM + 4 + n // 2, n, PS[7], chunks)
                head_sums(h)
            pe.wait_ge(piece_out, 3)
            piece(0, T_MLSTM + 5, 3, PS[7])
            out_project(T_MLSTM + 6, U_Y0)

        def gla():
            turn_tile(x_tok, U_X1, 0)
            piece(1, T_GLA, 0, PS[0])
            turn_tile(x_tok, U_X1, 1)
            pe.wait_ge(small_landed[5], 16)
            for k in range(KC):
                last = mm(PS[4][0:2 * RANK, 0:S], wglr[:, k, :], xT[:, k, :], start=(k == 0), stop=(k == KC - 1))
            last.then_inc(glr_done, 1)
            piece(1, T_GLA, 1, PS[1])
            pe.wait_ge(piece_out, pieces_before(1) + 2)
            project(T_GLA + 1, 1, 0, (0, 1))
            pe.wait_ge(small_landed[3], 48)
            turn(PS[5][:, 0:8], gate_b_rows, ident[0:8, 0:8]).then_inc(glr_done, 1)
            pe.wait_ge(glr_copied, 2)
            for n in range(2 * H):
                last = mm(PS[4 + n // 2][:, (n % 2) * S:(n % 2 + 1) * S],
                          gate_w_sb[:, n // H, (n % H) * P:(n % H + 1) * P], glrT, start=True, stop=True)
            last.then_inc(z_done, 1)
            project(T_GLA + 2, 1, 1, (0, 1))
            pe.wait_ge(proj_act, taken(1, 1))
            pe.wait_ge(proj_dve, taken(1, 1))
            for n in (2, 3):
                piece(1, T_GLA + 3, n, PS[n % 2])
            for tt in range(TT):
                for h in range(H):
                    c = h * S + tt * P
                    last = mm(PS[2 + tt][:, h * P:(h + 1) * P], kT[:, c:c + P], qT[:, c:c + P], start=True, stop=True)
                last.then_inc(diag_done, 1)
            pe.wait_ge(piece_out, pieces_before(1) + 4)
            pe.wait_ge(diag_placed, 1)
            for i in range(2 * (len(LEVELS) + 1)):
                d = i % 2
                if d == 0:
                    n, half = 4 + i // 4, (i // 2) % 2
                    if n >= 6 and half == 0:
                        pe.wait_ge(piece_out, pieces_before(1) + n - 1)
                    piece(1, T_GLA + 4 + (n - 4) // 2, n, PS[2 + n % 2], range(4 * half, 4 * half + 4))
                pe.wait_ge(scaled_done, i + 1)
                if i >= 2:
                    pe.wait_ge(placed, i - 1)
                for h in range(H):
                    if i < 2:
                        last = mm(PS[d][:, h * P:(h + 1) * P], k_dec[:, d, h * S + d * P:h * S + (d + 1) * P],
                                  q_dec[:, d, h * P:(h + 1) * P], start=True, stop=True)
                        continue
                    for s in range(TT):
                        c = (s * H + h) * 64
                        last = mm(PS[d][:, c:c + 64], k_dec[:, d, h * S + s * P:h * S + (s + 1) * P],
                                  q_dec[:, d, h * P + s * 64:h * P + (s + 1) * 64], start=True, stop=True)
                last.then_inc(prod_done, 1)
            pe.wait_ge(placed, 2 * (len(LEVELS) + 1))
            for tt in range(TT):
                for h in range(H):
                    for s in range(TT):
                        last = mm(PS[4 + 2 * tt + h // 2][:, (h % 2) * DV:(h % 2 + 1) * DV],
                                  A[:, s, h, tt * P:(tt + 1) * P], v_aug[:, s, h, 0:DV],
                                  start=(s == 0), stop=(s == TT - 1))
                last.then_inc(gla_out, 1)
            out_project(T_GLA + 6, U_Y1)

        def moe(layer, use):
            transposes(x_tok, use)
            pe.wait_ge(router_landed, 16 * DEPTH)
            for k in range(KC):
                q = k % 4
                last = mm(PS[0][q * DEPTH * E:(q + 1) * DEPTH * E, 0:S],
                          w_router[:, k].rearrange("p l n -> p (l n)"), xT[:, k, :],
                          start=(k < 4), stop=(k >= 4), skip_group_check=True)
            last.then_inc(logits_part, 1)
            pe.wait_ge(logits_copied, layer + 1)
            for tt in range(TT):
                last = mm(PS[1][:, tt * E:(tt + 1) * E], part_t[:, tt * P:(tt + 1) * P],
                          logit_of[:, layer * E:(layer + 1) * E], start=True, stop=True)
            last.then_inc(logits_done, 1)
            pe.wait_ge(aff_ready, layer + 1)
            for tt in range(TT):
                last = turn(PS[2][0:E, tt * P:(tt + 1) * P], aff[:, tt, :], ident)
            last.then_inc(affT_done, 1)
            pe.wait_ge(alpha_x, layer + 1)
            for tt in range(TT):
                for i in range(2):
                    mm(PS[4 + 2 * tt + i][:, :], ident, acc[:, tt, i * 512:(i + 1) * 512],
                       start=True, stop=True, skip_group_check=True)
            pe.wait_ge(slots_ready, layer + 1)
            for tt in range(TT):
                last = turn(PS[3][:, tt * E:(tt + 1) * E], picked_t[0:E, tt * P:(tt + 1) * P], ident[0:E, 0:E])
            last.then_inc(slotsT_done, 1)
            pe.wait_ge(sel_ready, 2 * layer + 1)
            base, n0, m0 = T_MOE[layer], E * layer, NG * layer
            with pe.Fori(0, NG) as g:
                def gather(half):
                    for k in range(4 * half, 4 * half + 4):
                        for tt in range(TT):
                            last = mm(PS[half][:, (k % 4) * P:(k % 4 + 1) * P], x_tok[:, tt, k * P:(k + 1) * P],
                                      sel[:, tt, bass.ts(g, P)], start=(tt == 0), stop=(tt == TT - 1))
                    last.then_inc(xin_done, 1)

                gather(0)
                for j in range(EG):

                    def tile(c):
                        n = TPE * j + c
                        pe.wait_ge(landed[n % SLOTS], g * (16 * EG * TPE // SLOTS)
                                   + 16 * ((base + n) // SLOTS + 1))
                        return slot(n).rearrange("p (k n) -> p k n", k=4)

                    def up_products(c, r, bank):
                        w = tile(c + r)
                        for k in range(4):
                            for q in range(4):
                                last = mm(bank[q * CAP:(q + 1) * CAP, 0:S],
                                          xinT[:, 4 * r + k, j * CAP:(j + 1) * CAP],
                                          w[:, k, q * S:(q + 1) * S],
                                          start=(r == 0 and k == 0), stop=(r == 1 and k == 3),
                                          skip_group_check=True)
                        last.then_inc(tile_used, 1)

                    if j == 0:
                        pe.wait_ge(xin_act, g + (m0 + 1))
                    pe.wait_ge(silu_done, g * EG + (n0 + j + 1))
                    up_products(0, 0, PS[2])
                    if j == 0:
                        gather(1)
                        pe.wait_ge(xin_dve, g + (m0 + 1))
                    up_products(0, 1, PS[2])
                    pe.wait_ge(hid_done, g * EG + (n0 + j + 1))
                    for r in range(2):
                        up_products(2, r, PS[3])
                    pe.wait_ge(selg_ready, g * EG + (n0 + j + 1))
                    pe.wait_ge(silu_done, g * EG + (n0 + j + 2))
                    for tt in range(TT):
                        turn(PS[2][:, S + tt * P:S + (tt + 1) * P], selg[:, tt], ident)
                    pe.wait_ge(hid_done, g * EG + (n0 + j + 2))
                    for c in range(2):
                        last = turn(PS[2][:, c * P:(c + 1) * P], hid[:, c * P:(c + 1) * P], ident)
                    last.then_inc(turned, 1)
                    pe.wait_ge(turned_copied, g * EG + (n0 + j + 1))
                    for r in range(2):
                        w = tile(4 + r)
                        for i in range(2):
                            for k in range(4):
                                kk = 4 * r + k
                                last = mm(PS[i][k * CAP:(k + 1) * CAP, :],
                                          hidT[:, kk % 2, (kk // 2) * CAP:(kk // 2 + 1) * CAP],
                                          w[:, k, i * 512:(i + 1) * 512],
                                          start=(r == 0), stop=(r == 1), skip_group_check=True)
                        last.then_inc(tile_used, 1)
                    pe.wait_ge(exp_act, g * EG + (n0 + j + 1))
                    pe.wait_ge(exp_dve, g * EG + (n0 + j + 1))
                    for tt in range(TT):
                        for i in range(2):
                            last = mm(PS[4 + 2 * tt + i][:, :], selT[:, tt * P:(tt + 1) * P],
                                      exp_t[:, i * 512:(i + 1) * 512], start=False, stop=True,
                                      skip_group_check=True)
                        last.then_inc(comb_done, 1)

        def attention():
            for tt in range(TT):
                turn_tile(acc, U_ATT, tt)
                if tt == 0:
                    arrived(pe, T_QKV)
                w = slot(T_QKV).rearrange("p (k n) -> p k n", k=KC)
                for k in range(KC):
                    last = mm(PS[4 + tt][:, :], xT[:, k, tt * P:(tt + 1) * P], w[:, k, :],
                              start=(k == 0), stop=(k == KC - 1))
            last.then_inc(tile_used, 1)
            for i in range(1, 6):
                project(T_QKV + i, 2, i, range(1, 5))
            pe.wait_ge(proj_act, taken(2, 5))
            pe.wait_ge(proj_dve, taken(2, 5))

            def scores(h):
                if h >= 4:
                    pe.wait_ge(probs_exp, h - 3)
                if h % 4 == 0:
                    pe.wait_ge(bias_landed[(h // 4) % 2], 16 * (h // 8 + 1))
                b = PS[2 + h % 4]
                r = slice(AD * (h % 2), AD * (h % 2 + 1))
                bias = bias_flip[:, (h // 4) % 2, h % 4]
                mm(b[:, 0:P], flip, bias[:, P:S], start=True, stop=False, skip_group_check=True)
                mm(b[:, 0:P], aqk[r, h // 2, 0:P], aqk[r, 8 + h // 2, 0:P], start=False, stop=True,
                   skip_group_check=True)
                mm(b[:, P:P + S], flip, bias, start=True, stop=False, skip_group_check=True)
                mm(b[:, P:P + S], aqk[r, h // 2, P:S], aqk[r, 8 + h // 2, :], start=False, stop=True,
                   skip_group_check=True).then_inc(s_done, 1)

            def turn_probs(h):
                pe.wait_ge(p_ready, h + 1)
                if h >= 2:
                    pe.wait_ge(pt_copied, h - 1)
                b, pr = PS[6 + h % 2], probs[:, h % 2]
                for c in range(3):
                    last = turn(b[:, c * P:(c + 1) * P], pr[:, c * P:(c + 1) * P], ident)
                last.then_inc(pt_done, 1)

            def values(h):
                pe.wait_ge(pt_copied, h + 1)
                if h % 2 == 0 and h >= 4:
                    pe.wait_ge(o_copied, h // 2 - 1)
                r = slice(AD * (h % 2), AD * (h % 2 + 1))
                b, pT = PS[(h // 2) % 2], probsT[:, h % 2]
                mm(b[r, 0:S], av[:, 0, h * AD:(h + 1) * AD], pT[:, 0:S], start=True, stop=False,
                   skip_group_check=True)
                mm(b[r, P:S], av[:, 1, h * AD:(h + 1) * AD], pT[:, S:S + P], start=False, stop=True,
                   skip_group_check=True).then_inc(o_done, 1)

            scores(0)
            scores(1)
            for h in range(AH):
                if h + 2 < AH:
                    scores(h + 2)
                if h >= 1:
                    values(h - 1)
                turn_probs(h)
            values(AH - 1)
            pe.wait_ge(o_copied, AH // 2)
            out_project(T_WO)

        def ffn():
            def up(n, bank_pair, tokens):
                w = slot(n).rearrange("p (k n) -> p k n", k=KC)
                for c in range(4):
                    at = (c % 2) * S
                    for k in range(KC):
                        last = mm(PS[bank_pair + c // 2][:, at + tokens.start:at + tokens.stop],
                                  w[:, k, c * P:(c + 1) * P], xT[:, k, tokens],
                                  start=(k == 0), stop=(k == KC - 1), skip_group_check=True)
                return last

            for tt in range(TT):
                turn_tile(acc, U_FFN, tt)
                if tt == 0:
                    pe.wait_ge(landed[T_UP % SLOTS], up_landed(T_UP))
                last = up(T_UP, 0, slice(tt * P, (tt + 1) * P))
            last.then_inc(tile_used, 1)
            pe.wait_ge(small_landed[4], 64)
            for j in range(4):
                last = turn(PS[6][:, j * 2 * FB:(j + 1) * 2 * FB], conv_rows[:, j, :], ident[0:2 * FB, 0:2 * FB])
            last.then_inc(convT_done, 1)
            for i in range(1, UPT):
                n = T_UP + i
                pe.wait_ge(landed[n % SLOTS], up_landed(n))
                if i >= 3:
                    pe.wait_ge(conv_done, i - 2)
                up(n, 2 * (i % 3), slice(0, S)).then_inc(tile_used, 1)
            pe.wait_ge(conv_done, (UPT - 3) // 3 * 3 + 3)
            for i in range(N_DOWN):
                n = T_DOWN + i
                pe.wait_ge(ff_ready, min(2 * i + 2, UPT))
                pe.wait_ge(landed[n % SLOTS], up_landed(n))
                w = slot(n).rearrange("p (k n) -> p k n", k=4)
                for tt in range(TT):
                    for k in range(4 * i, min(4 * i + 4, FB)):
                        for j in range(2):
                            last = mm(PS[4 + 2 * tt + j][:, :], ffh[:, k, tt * P:(tt + 1) * P],
                                      w[:, k - 4 * i, j * 512:(j + 1) * 512], start=(k == 0), stop=(k == FB - 1))
                    if i == N_DOWN - 1 and tt == 0:
                        last.then_inc(out_rows, 1)
                last.then_inc(tile_used, 1)

        pe.sem_inc(turned, 1)
        pe.sem_inc(comb_done, 1)
        mlstm()
        moe(0, U_M0)
        gla()
        moe(1, U_M1)
        attention()
        ffn()

    @block.scalar
    def _(act):
        f = nc.scalar.activation
        chain = Chain(act, act_seq)
        link = chain.link

        def copy_turned(use, tt):
            for b in ((0, 1), (2,))[tt]:
                act.wait_ge(tr_done, 4 * use + b + 1)
                half = 4 * (b % 2)
                f(xT[:, half:half + 4, tt * P:(tt + 1) * P], PS[b][:, :].rearrange("p (k n) -> p k n", k=4), ACT.Copy
                  ).then_inc(tr_act, 1)

        def copy_transposes(use):
            for tt in range(TT):
                copy_turned(use, tt)

        def take_projection(stage, n, i):
            act.wait_ge(tile_used, n + 1)
            b0 = 2 * (i % 2)
            if stage == 2:
                if 1 <= i < 5:
                    dst = aqk_t[:, (4 * i - 4) * S:(4 * i - 2) * S]
                    last = f(dst, PS[b0][:, :], ACT.Copy, scale=(AD ** -0.5 if i < 3 else 1.0))
                else:
                    last = f(av[:, 0, (i // 5) * 512:(i // 5 + 1) * 512], PS[4 if i == 0 else b0][:, :], ACT.Copy)
            elif i < 2:
                last = f(qkT_t[:, i * H * S:i * H * S + 512], PS[b0][:, :], ACT.Copy,
                         scale=(DK ** -0.5 if i == 0 else 1.0))
            else:
                last = f(v_aug[:, 0, 2 * (i - 2):2 * (i - 1), 0:DV],
                         PS[b0][:, :].rearrange("p (h w) -> p h w", w=DV), ACT.Copy)
            last.then_inc(proj_act, 1)

        def take_values(n, bank):
            act.wait_ge(piece_done, pieces_before(1) + n + 1)
            f(v_aug[:, n % 2, 2 * (n // 2):2 * (n // 2 + 1), 0:DV], bank[:, :].rearrange("p (h w) -> p h w", w=DV),
              ACT.Copy).then_inc(piece_out, 1)

        def take_gate(first, n, bank, fn):
            act.wait_ge(piece_done, first + n + 1)
            c = slice((n // 2) * 512, (n // 2 + 1) * 512)
            if n == 0:
                f(gate[:, 0, c], bank[:, :], ACT.Copy).then_inc(piece_out, 1)
            elif n >= 2:
                f(gate[:, n % 2, c], bank[:, :], fn).then_inc(piece_out, 1)
            else:
                act.wait_ge(piece_out, first + n)
                f(gate[:, 0, c], gate[:, 0, c], fn)
                f(gate[:, 1, c], bank[:, :], fn).then_inc(piece_out, 1)

        def root(norm, tt, heads=1):
            c = slice(tt * heads, (tt + 1) * heads)
            act.wait_ge(var_ready, var_count(norm, tt))
            f(deviation[:, c], meanvar[:, c, 1], ACT.Sqrt, bias=ln_eps).then_inc(root_done, 1)

        def roots(norm, heads=1):
            for tt in range(TT):
                root(norm, tt, heads)

        def mlstm():
            copy_transposes(U_X0)
            take_projection(0, T_MLSTM, 0)
            act.wait_ge(relb_done, 1)
            f(bias_rows[:, 0:S], PS[7][0:AH, 0:S], ACT.Copy).then_inc(relb_copied, 1)
            act.wait_ge(gates_done, 1)
            f(gates_all, PS[4][0:16, 0:S], ACT.Identity, bias=gate_bias).then_inc(gates_biased, 1)
            act.wait_ge(gates_split, 1)
            link(f(row_soft, PS[6][0:H, :], ACT.Abs))
            link(f(row_soft, row_soft, ACT.Exp, scale=-1.0))
            f(row_soft, row_soft, ACT.Ln, bias=1.0).then_inc(gate_soft, 1)
            for i in range(1, 4):
                take_projection(0, T_MLSTM + i, i)
                if i == 1:
                    act.wait_ge(gate_columns, 1)
                    f(a_cols, PS[7][:, 0:16], ACT.Copy)
                    link(f(floor_cols, PS[7][:, 16:32], ACT.Exp, scale=-1.0))
                    act.sem_inc(gate_scalars, 1)
            act.wait_ge(relb_stored, 16)
            for h in range(H):
                act.wait_ge(mb_done, h + 1)
                if h >= 2:
                    act.wait_ge(num_done, h - 1)
                w = decay[:, h % 2]
                for d in range(2):
                    for s in range(TT):
                        c0, c1 = ((0, 256), (256, 384))[s] if d == 0 else ((0, 128), (128, 384))[s]
                        col = (d * 2 + s) * H + h
                        last = f(w[:, d, c0:c1], PS[4 + d][:, c0:c1], ACT.Exp, bias=a_cols[:, col:col + 1],
                                 scale=-1.0)
                last.then_inc(decay_done, 1)
                if h != 2:
                    take_gate(pieces_before(0), (0, 1, None, 2)[h], PS[7], ACT.Sigmoid)
            roots(HEAD_NORMS[0], H)
            take_gate(pieces_before(0), 3, PS[7], ACT.Sigmoid)
            copy_transposes(U_Y0)
            root(LAYER_NORMS[0], 0)
            copy_turned(U_M0, 0)
            root(LAYER_NORMS[0], 1)

        def gla():
            copy_turned(U_X1, 1)
            act.wait_ge(glr_done, 1)
            f(glrT, PS[4][0:2 * RANK, 0:S], ACT.Copy).then_inc(glr_copied, 1)
            for n in range(2):
                take_values(n, PS[n])
            take_projection(1, T_GLA + 1, 0)
            act.wait_ge(glr_done, 2)
            f(gate_b_cols, PS[5][:, 0:8], ACT.Copy).then_inc(glr_copied, 1)
            act.wait_ge(z_ready, 1)
            link(f(acc_t[:, :], b_t, ACT.Abs))
            link(f(acc_t[:, :], acc_t[:, :], ACT.Exp, scale=-1.0))
            f(acc_t[:, :], acc_t[:, :], ACT.Ln, bias=1.0).then_inc(z_soft, 1)
            take_projection(1, T_GLA + 2, 1)
            for n in (2, 3):
                take_values(n, PS[n % 2])
            for i in range(2 * (len(LEVELS) + 1)):
                d = i % 2
                act.wait_ge(diffs_done, i + 1)
                if i >= 2:
                    act.wait_ge(scaled_done, i - 1)
                for w in range(2):
                    last = f(PS[4 + 2 * d + w][:, :], diffs[:, w], ACT.Exp, scale=1.0 / GLA_TAU)
                last.then_inc(decays_exp, 1)
                if i in (3, 7):
                    n = i // 4
                    take_gate(pieces_before(1) + 4, n, PS[2 + n % 2], ACT.Silu)
            act.wait_ge(decays_exp, 2 * (len(LEVELS) + 1))
            for n in (2, 3):
                take_gate(pieces_before(1) + 4, n, PS[2 + n % 2], ACT.Silu)
            for tt in range(TT):
                root(HEAD_NORMS[1], tt, H)
                copy_turned(U_Y1, tt)
            root(LAYER_NORMS[2], 0)
            copy_turned(U_M1, 0)
            root(LAYER_NORMS[2], 1)

        def moe(layer, use):
            copy_turned(use, 1)
            act.wait_ge(logits_part, layer + 1)
            f(part_t, PS[0][:, 0:S], ACT.Copy).then_inc(logits_copied, 1)
            act.wait_ge(router_max, layer + 1)
            for tt in range(TT):
                last = f(aff[:, tt, :], PS[1][:, tt * E:(tt + 1) * E], ACT.Exp, bias=row_max_r[:, tt:tt + 1],
                         accum_out=row_sum_r[:, tt:tt + 1])
            last.then_inc(aff_exp, 1)
            base, n0, m0 = T_MOE[layer], E * layer, NG * layer
            with act.Fori(0, NG) as g:
                act.wait_ge(xin_done, g * 2 + (2 * m0 + 1))
                f(xin_t[:, 0:512], PS[0][:, :], ACT.Copy).then_inc(xin_act, 1)
                for j in range(EG):
                    act.wait_ge(tile_used, g * (EG * TPE) + (base + TPE * j + 2))
                    act.wait_ge(hid_done, g * EG + (n0 + j + 1))
                    f(silu_g, PS[2][:, 0:S], ACT.Silu).then_inc(silu_done, 1)
                    act.wait_ge(turned, g * EG + (n0 + j + 2))
                    act.wait_ge(comb_done, g * (2 * EG) + (2 * (n0 + j) + 1))
                    f(turned_t, PS[2][:, :], ACT.Copy).then_inc(turned_copied, 1)
                    act.wait_ge(tile_used, g * (EG * TPE) + (base + TPE * j + 6))
                    f(exp_t[:, 0:512], PS[0][:, :], ACT.Copy).then_inc(exp_act, 1)
            root(LAYER_NORMS[2 * layer + 1], 0)
            if layer == 0:
                copy_turned(U_X1, 0)
            else:
                rms_root(0, 0)
                copy_turned(U_ATT, 0)
            root(LAYER_NORMS[2 * layer + 1], 1)

        def rms_root(u, tt):
            c, r = slice(tt, tt + 1), slice(2 + tt, 3 + tt)
            act.wait_ge(x_sum, TT * u + tt + 1)
            link(f(acc[:, tt], x_tok[:, tt], ACT.Square, accum_out=square_sum[:, c]))
            f(deviation[:, r], square_sum[:, c], ACT.Sqrt, scale=1.0 / D, bias=rms_eps).then_inc(root_done, 1)

        def attention():
            rms_root(0, 1)
            copy_turned(U_ATT, 1)
            for i in range(6):
                take_projection(2, T_QKV + i, i)

            def exps(h):
                act.wait_ge(max_done, h + 1)
                if h >= 2:
                    act.wait_ge(pt_done, h - 1)
                b, c = PS[2 + h % 4], 2 * (h % 2)
                f(probs[:, h % 2, 0:P], b[:, 0:P], ACT.Exp, bias=neg_max[:, c:c + 1],
                  accum_out=prob_sum[:, c:c + 1])
                f(probs[:, h % 2, P:P + S], b[:, P:P + S], ACT.Exp, bias=neg_max[:, c + 1:c + 2],
                  accum_out=prob_sum[:, c + 1:c + 2]).then_inc(probs_exp, 1)

            exps(0)
            for h in range(AH):
                if h + 1 < AH:
                    exps(h + 1)
                act.wait_ge(pt_done, h + 1)
                if h >= 2:
                    act.wait_ge(o_done, h - 1)
                f(probsT[:, h % 2], PS[6 + h % 2][:, 0:3 * P], ACT.Copy).then_inc(pt_copied, 1)

        def ffn():
            for tt in range(TT):
                rms_root(1, tt)
                copy_turned(U_FFN, tt)
            act.wait_ge(convT_done, 1)
            f(convw_t, PS[6][:, 0:8 * FB], ACT.Copy).then_inc(convT_copied, 1)
            act.wait_ge(convT_copied, 1)

            def taps(i):
                act.wait_ge(tile_used, T_UP + i + 1)
                if i >= 2:
                    act.wait_ge(ff_ready, i - 1)
                for c in range(4):
                    n = 2 * i + c % 2 + FB * (c // 2)
                    last = f(conv[:, i % 2, c], PS[2 * (i % 3) + c // 2][:, (c % 2) * S:(c % 2 + 1) * S],
                             ACT.Identity, scale=conv_cols[:, 2, n:n + 1], bias=conv_cols[:, 3, n:n + 1])
                last.then_inc(taps_done, 1)

            taps(0)
            for i in range(UPT):
                if i + 1 < UPT:
                    taps(i + 1)
                act.wait_ge(conv_done, i + 1)
                f(conv[:, i % 2, 0:2], conv[:, i % 2, 0:2], ACT.Silu).then_inc(ff_silu, 1)
            for tt in range(TT):
                rms_root(2, tt)

        act.sem_inc(silu_done, 1)
        mlstm()
        moe(0, U_M0)
        gla()
        moe(1, U_M1)
        attention()
        ffn()

    @block.vector
    def _(dve):
        v = nc.vector
        chain = Chain(dve, dve_seq)
        link = chain.link

        def copy_transposes(use):
            dve.wait_ge(tr_done, 4 * use + 4)
            v.tensor_copy(xT[:, 4:8, P:S], PS[3][:, :].rearrange("p (k n) -> p k n", k=4)).then_inc(tr_dve, 1)

        def take_projection(stage, n, i):
            dve.wait_ge(tile_used, n + 1)
            b = PS[2 * (i % 2) + 1]
            if stage == 2:
                if 1 <= i < 5:
                    last = v.tensor_scalar(aqk_t[:, (4 * i - 2) * S:4 * i * S], b[:, :],
                                           AD ** -0.5 if i < 3 else 1.0, None, ALU.mult)
                else:
                    last = v.tensor_copy(av[:, 1, (i // 5) * 512:(i // 5 + 1) * 512], (PS[5] if i == 0 else b)[:, :])
            elif i < 2:
                last = v.tensor_scalar(qkT_t[:, i * H * S + 512:(i + 1) * H * S], b[:, :],
                                       DK ** -0.5 if i == 0 else 1.0, None, ALU.mult)
            else:
                last = v.tensor_copy(v_aug[:, 1, 2 * (i - 2):2 * (i - 1), 0:DV],
                                     b[:, :].rearrange("p (h w) -> p h w", w=DV))
            last.then_inc(proj_dve, 1)

        def head_norm(layer, tt, src):
            n0 = tt * H
            dve.wait_ge(root_done, root_count(HEAD_NORMS[layer], tt))
            link(v.reciprocal(inv_spread[:, n0:n0 + H], deviation[:, n0:n0 + H]))
            for h in range(H):
                last = v.tensor_scalar(PS[4 + 2 * tt + h // 2][:, (h % 2) * DV:(h % 2 + 1) * DV], src(h),
                                       meanvar[:, n0 + h, 0:1], inv_spread[:, n0 + h:n0 + h + 1],
                                       ALU.subtract, ALU.mult)
            link(last)
            dve.wait_ge(gate_ready, 3 * layer + 2 + tt)
            for j in range(2):
                c = slice(j * 512, (j + 1) * 512)
                last = v.tensor_tensor(acc[:, tt, c], PS[4 + 2 * tt + j][:, :], gate[:, tt, c], ALU.mult)
            last.then_inc(tokens_ready, 1)

        def layer_norm(use, tt, first_half_done=False):
            halves = [PS[4 + 2 * tt][:, :], PS[5 + 2 * tt][:, :]]
            for j in ((1,) if first_half_done else (0, 1)):
                last = v.bn_stats(stats[:, 2 * tt + j], halves[j])
            link(last)
            v.bn_aggr(meanvar[:, tt], stats[:, 2 * tt:2 * tt + 2].rearrange("p n s -> p (n s)")
                      ).then_inc(var_ready, 1)
            dve.wait_ge(var_ready, var_count(LAYER_NORMS[use], tt))
            if tt == 0:
                dve.wait_ge(rows_landed, 32 * (use + 1))
            for j in range(2):
                v.scalar_tensor_tensor(halves[j], halves[j], meanvar[:, tt, 0:1],
                                       gain_row[:, j * 512:(j + 1) * 512], ALU.subtract, ALU.mult)
            dve.wait_ge(root_done, root_count(LAYER_NORMS[use], tt))
            link(v.reciprocal(inv_spread[:, tt:tt + 1], deviation[:, tt:tt + 1]))
            for j in range(2):
                c = slice(j * 512, (j + 1) * 512)
                last = v.scalar_tensor_tensor(x_tok[:, tt, c], halves[j], inv_spread[:, tt:tt + 1],
                                              bias_row[:, c], ALU.mult, ALU.add)
            last.then_inc(tokens_ready, 1)

        def residual_norm(use, n):
            def add(tt, j):
                return v.scalar_tensor_tensor(PS[4 + 2 * tt + j][:, :], x_tok[:, tt, j * 512:(j + 1) * 512], ALPHA,
                                              PS[4 + 2 * tt + j][:, :], ALU.mult, ALU.add)
            dve.wait_ge(tile_used, n + 1)
            for tt in range(TT):
                last = add(tt, 0)
            link(last)
            for tt in range(TT):
                v.bn_stats(stats[:, 2 * tt], PS[4 + 2 * tt][:, :])
            for tt in range(TT):
                if tt == 0:
                    dve.wait_ge(out_rows, use // 2 + 1)
                else:
                    dve.wait_ge(tile_used, n + 2)
                link(add(tt, 1))
                layer_norm(use, tt, first_half_done=True)

        def mlstm():
            copy_transposes(U_X0)
            take_projection(0, T_MLSTM, 0)
            dve.wait_ge(gates_split, 1)
            fg, ig = PS[6][0:H, :], PS[5][0:H, :]
            dve.wait_ge(gate_soft, 1)
            link(v.scalar_tensor_tensor(row_m, fg, 0.0, row_soft, ALU.min, ALU.subtract))
            dve.wait_ge(ones_ready, 1)
            one = ones[0:H, 0:1].to_broadcast([H, S])

            def along(ap, d):
                r = ap[:, d * S:(d + 1) * S]
                return r if d == 0 else r[:, ::-1]

            for d in range(2):
                last = v.tensor_tensor_scan(along(row_b, d), one, along(row_m, d), 0.0, ALU.mult, ALU.add)
            link(last)
            link(v.tensor_tensor(row_a, ig, row_b, ALU.subtract))
            for d in range(2):
                last = v.tensor_tensor_scan(along(row_max, d), one, along(row_a, d), 0.0, ALU.mult, ALU.max)
            link(last)
            v.tensor_tensor(row_m, row_b, row_max, ALU.add).then_inc(gate_rows, 1)
            for i in range(1, 4):
                take_projection(0, T_MLSTM + i, i)

            def weigh(h):
                dve.wait_ge(decay_done, h + 1)
                dve.wait_ge(scores_done, h + 1)
                w, sc = decay[:, h % 2], PS[6]
                for d, c, n, q in ((0, 0, 256, 0), (0, 256, 128, 384), (1, 0, 128, 0), (1, 128, 256, 256)):
                    last = v.tensor_tensor(w[:, d, c:c + n], w[:, d, c:c + n], sc[:, q:q + n], ALU.mult)
                last.then_inc(weights_done, 1)

            def take_head(h):
                dve.wait_ge(num_done, h + 1)
                for o in range(4):
                    last = v.tensor_reduce(den[:, o:o + 1], PS[o][:, DV:VW], AX.X, ALU.max,
                                           apply_absolute_value=True)
                link(last)
                floor = floor_cols.rearrange("p (d t h) -> p t d h", d=2, t=TT)[:, :, :, h]
                dens = den.rearrange("p (t d) -> p t d", t=TT)
                link(v.tensor_tensor(dens, dens, floor, ALU.max))
                link(v.reciprocal(inv_den, den))
                for tt in range(TT):
                    last = v.tensor_scalar(acc[:, tt, h * DV:(h + 1) * DV], PS[2 * tt][:, 0:DV],
                                           inv_den[:, 2 * tt:2 * tt + 1], None, ALU.mult)
                link(last)
                for tt in range(TT):
                    last = v.scalar_tensor_tensor(acc[:, tt, h * DV:(h + 1) * DV], PS[2 * tt + 1][:, 0:DV],
                                                  inv_den[:, 2 * tt + 1:2 * tt + 2], acc[:, tt, h * DV:(h + 1) * DV],
                                                  ALU.mult, ALU.add)
                last.then_inc(head_out, 1)
                dve.wait_ge(head_out, h + 1)
                for tt in range(TT):
                    last = v.bn_stats(stats[:, tt * H + h], acc[:, tt, h * DV:(h + 1) * DV])
                link(last)
                for tt in range(TT):
                    last = v.bn_aggr(meanvar[:, tt * H + h], stats[:, tt * H + h])
                if h == H - 1:
                    last.then_inc(var_ready, 2)

            dve.wait_ge(gate_scalars, 1)
            dve.wait_ge(masks_ready, 1)
            for h in range(H):
                weigh(h)
                take_head(h)
            dve.wait_ge(var_ready, 2)
            for tt in range(TT):
                if tt == 1:
                    dve.wait_ge(piece_out, 4)
                head_norm(0, tt, lambda h: acc[:, tt, h * DV:(h + 1) * DV])
            copy_transposes(U_Y0)
            residual_norm(0, T_MLSTM + 6)

        def gla():
            copy_transposes(U_X1)
            take_projection(1, T_GLA + 1, 0)
            dve.wait_ge(z_done, 1)
            dve.wait_ge(glr_copied, 2)
            for n in range(2 * H):
                last = v.tensor_scalar(b_cum[:, n], PS[4 + n // 2][:, (n % 2) * S:(n % 2 + 1) * S],
                                       gate_b_cols[:, n:n + 1], None, ALU.add)
            last.then_inc(z_ready, 1)
            dve.wait_ge(z_soft, 1)
            link(v.scalar_tensor_tensor(acc_t[:, :], b_t, 0.0, acc_t[:, :], ALU.min, ALU.subtract))
            take_projection(1, T_GLA + 2, 1)
            for n in range(2 * H):
                o, i = b_cum[:, n], acc_t[:, n * S:(n + 1) * S]
                if n >= H:
                    o, i = o[:, ::-1], i[:, ::-1]
                last = v.tensor_tensor_scan(o, ones[:, 0:1].to_broadcast([P, S]), i, 0.0, ALU.mult, ALU.add)
            last.then_inc(b_ready, 1)
            dve.wait_ge(b_ready, 1)
            dve.wait_ge(proj_act, taken(1, 1))
            dve.wait_ge(proj_dve, taken(1, 1))

            def scale(i):
                d, L = i % 2, P >> (i // 2)
                dve.wait_ge(decays_exp, i + 1)
                if i >= 2:
                    dve.wait_ge(prod_done, i - 1)
                qv = qT.rearrange("p (n w l) -> p n w l", w=2, l=L)
                kv = kT.rearrange("p (n w l) -> p n w l", w=2, l=L)
                ko = k_dec[:, d].rearrange("p (n w l) -> p n w l", w=2, l=L)
                hq, hk = (1, 0) if d == 0 else (0, 1)
                v.tensor_tensor(q_dec[:, d].rearrange("p (n l) -> p n l", l=L), qv[:, :, hq, :],
                                PS[4 + 2 * d][:, :].rearrange("p (n l) -> p n l", l=L), ALU.mult)
                v.tensor_tensor(ko[:, :, hk, :], kv[:, :, hk, :],
                                PS[5 + 2 * d][:, :].rearrange("p (n l) -> p n l", l=L), ALU.mult
                                ).then_inc(scaled_done, 1)

            def place(i):
                d, L = i % 2, P >> (i // 2)
                dve.wait_ge(prod_done, i + 1)
                if i >= 1:
                    dve.wait_ge(placed, i)
                if i < 2:
                    last = v.tensor_copy(A[:, d, :, (1 - d) * P:(2 - d) * P],
                                         PS[d][:, :].rearrange("p (h n) -> p h n", h=H))
                else:
                    mask = level_masks[:, (d * len(LEVELS) + i // 2 - 1) * 64:(d * len(LEVELS) + i // 2) * 64]
                    for s in range(TT):
                        to = A[:, s, :, s * P:(s + 1) * P].rearrange("p h (n w l) -> p h n w l", w=2, l=L)
                        src = PS[d][:, s * H * 64:(s + 1) * H * 64]
                        pick = mask.rearrange("p (n l) -> p n l", l=L).unsqueeze(1)
                        last = v.copy_predicated(to[:, :, :, 1 - d, :], pick.to_broadcast([P, H, 64 // L, L]),
                                                 src.rearrange("p (h n l) -> p h n l", h=H, l=L))
                last.then_inc(placed, 1)

            for tt in range(TT):
                dve.wait_ge(diag_done, tt + 1)
                last = v.scalar_tensor_tensor(A[:, tt, :, tt * P:(tt + 1) * P],
                                              PS[2 + tt][:, :].rearrange("p (h n) -> p h n", h=H), 2.0,
                                              ident.unsqueeze(1).to_broadcast([P, H, P]), ALU.mult, ALU.mult)
            last.then_inc(diag_placed, 1)
            dve.wait_ge(diag_placed, 1)
            scale(0)
            scale(1)
            n_levels = 2 * (len(LEVELS) + 1)
            for i in range(n_levels):
                place(i)
                if i + 2 < n_levels:
                    scale(i + 2)
            for tt in range(TT):
                def out_of(h):
                    return PS[4 + 2 * tt + h // 2][:, (h % 2) * DV:(h % 2 + 1) * DV]
                dve.wait_ge(gla_out, tt + 1)
                for h in range(H):
                    last = v.bn_stats(stats[:, tt * H + h], out_of(h))
                link(last)
                for h in range(H):
                    last = v.bn_aggr(meanvar[:, tt * H + h], stats[:, tt * H + h])
                last.then_inc(var_ready, 1)
                dve.wait_ge(var_ready, var_count(HEAD_NORMS[1], tt))
                head_norm(1, tt, out_of)
            copy_transposes(U_Y1)
            residual_norm(2, T_GLA + 6)

        def rms(u, tt, gain):
            n = 2 + tt
            dve.wait_ge(root_done, root_count(RMS_NORMS[u], tt))
            link(v.reciprocal(inv_spread[:, n:n + 1], deviation[:, n:n + 1]))
            if tt == 0:
                dve.wait_ge(*((attn_row_landed, 16), (rows_landed, 32 * 4 + 16), (gain_landed, 48))[u])
            v.scalar_tensor_tensor(acc[:, tt], x_tok[:, tt], inv_spread[:, n:n + 1], gain,
                                   ALU.mult, ALU.mult).then_inc(tokens_ready, 1)

        def moe(layer, use):
            copy_transposes(use)
            dve.wait_ge(logits_done, layer + 1)
            v.tensor_reduce(row_max_r, PS[1][:, 0:TT * E].rearrange("p (t e) -> p t e", t=TT), AX.X, ALU.max,
                            negate=True).then_inc(router_max, 1)
            dve.wait_ge(aff_exp, layer + 1)
            link(v.reciprocal(inv_sum_r, row_sum_r))
            for tt in range(TT):
                last = v.tensor_scalar(aff[:, tt, :], aff[:, tt, :], inv_sum_r[:, tt:tt + 1], None, ALU.mult)
            last.then_inc(aff_ready, 1)
            dve.wait_ge(affT_done, layer + 1)
            work, pick, count = affT_t[0:E, :], picked_t[0:E, :], work_t[0:E, :]
            for r in range(CAP // 8):
                top, left = top8[:, 8 * r:8 * r + 8], PS[2][0:E, 0:S] if r == 0 else work
                link(v.max(top, left))
                link(v.match_replace(work, top, left, -1.0))
            link(v.tensor_scalar(pick, work, 0.0, None, ALU.is_lt))
            link(v.tensor_tensor_scan(count, ones[0:E, 0:1].to_broadcast([E, S]), pick, 0.0, ALU.mult, ALU.add))
            v.tensor_tensor(pick, pick, count, ALU.mult).then_inc(slots_ready, 1)
            dve.wait_ge(slotsT_done, layer + 1)
            for e0, e1 in ((0, EG), (EG, E)):
                for tt in range(TT):
                    last = v.tensor_tensor(
                        sel[:, tt, e0 * CAP:e1 * CAP].rearrange("p (e c) -> p e c", c=CAP),
                        slot_ids.unsqueeze(1).to_broadcast([P, e1 - e0, CAP]),
                        PS[3][:, tt * E + e0:tt * E + e1].unsqueeze(2).to_broadcast([P, e1 - e0, CAP]),
                        ALU.is_equal)
                last.then_inc(sel_ready, 1)
            dve.wait_ge(sel_ready, 2 * layer + 2)
            base, n0, m0 = T_MOE[layer], E * layer, NG * layer
            with dve.Fori(0, NG) as g:
                for j in range(EG):
                    dve.wait_ge(turned, g * EG + (n0 + j + 1))
                    for tt in range(TT):
                        last = v.tensor_tensor(
                            selg[:, tt].rearrange("p (q c) -> p q c", c=CAP),
                            sel[:, tt, bass.ds(g * P + j * CAP, CAP)].unsqueeze(1).to_broadcast([P, 4, CAP]),
                            aff[:, tt, bass.ds(g * EG + j, 1)].unsqueeze(2).to_broadcast([P, 4, CAP]), ALU.mult)
                    last.then_inc(selg_ready, 1)
                    if j == 0:
                        dve.wait_ge(xin_done, g * 2 + (2 * m0 + 2))
                        v.tensor_copy(xin_t[:, 512:1024], PS[1][:, :]).then_inc(xin_dve, 1)
                    dve.wait_ge(silu_done, g * EG + (n0 + j + 2))
                    dve.wait_ge(tile_used, g * (EG * TPE) + (base + TPE * j + 4))
                    v.tensor_tensor(hid, silu_g, PS[3][:, 0:S], ALU.mult).then_inc(hid_done, 1)
                    dve.wait_ge(tile_used, g * (EG * TPE) + (base + TPE * j + 6))
                    dve.wait_ge(comb_done, g * (2 * EG) + (2 * (n0 + j) + 1))
                    v.tensor_copy(exp_t[:, 512:1024], PS[1][:, :]).then_inc(exp_dve, 1)
            for tt in range(TT):
                dve.wait_ge(comb_done, 2 * (n0 + E) + tt)
                layer_norm(2 * layer + 1, tt)
                if layer == 1:
                    dve.wait_ge(tokens_ready, tokens_count(U_ATT, tt) - 1)
                    dve.sem_inc(x_sum, 1)
                    rms(0, tt, attn_row)

        def add_to_stream(u, n, gain):
            for tt in range(TT):
                if tt == 0:
                    dve.wait_ge(out_rows, u + 2)
                else:
                    dve.wait_ge(tile_used, n + 1)
                for j in range(2):
                    dst = x_tok[:, tt, j * 512:(j + 1) * 512]
                    last = v.tensor_tensor(dst, dst, PS[4 + 2 * tt + j][:, :], ALU.add)
                last.then_inc(x_sum, 1)
                dve.wait_ge(x_sum, TT * u + tt + 1)
                rms(u, tt, gain)

        def attention():
            copy_transposes(U_ATT)
            for i in range(6):
                take_projection(2, T_QKV + i, i)

            def maxima(h):
                dve.wait_ge(s_done, h + 1)
                b, c = PS[2 + h % 4], 2 * (h % 2)
                v.tensor_reduce(neg_max[:, c:c + 1], b[:, 0:P], AX.X, ALU.max, negate=True)
                v.tensor_reduce(neg_max[:, c + 1:c + 2], b[:, P:P + S], AX.X, ALU.max, negate=True
                                ).then_inc(max_done, 1)

            maxima(0)
            for h in range(AH):
                if h + 1 < AH:
                    maxima(h + 1)
                dve.wait_ge(probs_exp, h + 1)
                c, pr = 2 * (h % 2), probs[:, h % 2]
                link(v.reciprocal(inv_prob[:, c:c + 2], prob_sum[:, c:c + 2]))
                v.tensor_scalar(pr[:, 0:P], pr[:, 0:P], inv_prob[:, c:c + 1], None, ALU.mult)
                v.tensor_scalar(pr[:, P:P + S], pr[:, P:P + S], inv_prob[:, c + 1:c + 2], None, ALU.mult
                                ).then_inc(p_ready, 1)
                if h % 2 == 0 and h >= 2:
                    copy_heads(h // 2 - 1)
            copy_heads(AH // 2 - 1)
            add_to_stream(1, T_WO + 1, bias_row)

        def copy_heads(pair):
            dve.wait_ge(o_done, 2 * pair + 2)
            v.tensor_copy(xT[:, pair, :], PS[pair % 2][:, 0:S]).then_inc(o_copied, 1)

        def ffn():
            copy_transposes(U_FFN)
            dve.wait_ge(convT_copied, 1)

            def convolve(i):
                dve.wait_ge(taps_done, i + 1)
                for back in (1, 2):
                    for c in range(4):
                        n = 2 * i + c % 2 + FB * (c // 2)
                        u = PS[2 * (i % 3) + c // 2][:, (c % 2) * S:(c % 2 + 1) * S - back]
                        dst = conv[:, i % 2, c, back:S]
                        last = v.scalar_tensor_tensor(dst, u, conv_cols[:, 2 - back, n:n + 1], dst, ALU.mult, ALU.add)
                    if back == 1:
                        link(last)
                last.then_inc(conv_done, 1)

            convolve(0)
            for i in range(UPT):
                if i + 1 < UPT:
                    convolve(i + 1)
                dve.wait_ge(ff_silu, i + 1)
                dve.wait_ge(conv_done, i + 1)
                v.tensor_tensor(ffh[:, 2 * i:2 * i + 2, :], conv[:, i % 2, 0:2], conv[:, i % 2, 2:4], ALU.mult
                                ).then_inc(ff_ready, 1)
            add_to_stream(2, T_DOWN + N_DOWN - 1, ng_t[:, :])

        dve.sem_inc(hid_done, 1)
        mlstm()
        moe(0, U_M0)
        gla()
        moe(1, U_M1)
        attention()
        ffn()


_INS = ["x", "mlstm_w_in", "mlstm_gate_b", "mlstm_norm_g", "mlstm_w_out", "gla_w_in", "gla_gate_w",
        "gla_gate_b", "gla_norm_g", "gla_w_out", "moe_router", "moe_w_gate", "moe_w_up", "moe_w_down",
        "ln_g", "ln_b", "attn_norm_2", "w_qkv_2", "w_o_2", "rel_bias_2", "ffn_norm_2", "w_up_2",
        "conv_w_2", "conv_b_2", "w_down_2", "final_norm_2"]


def kernel(**inputs):
    import concourse.bacc as bacc
    from concourse.bass_utils import run_bass_kernel_spmd

    nc = bacc.Bacc("TRN2", target_bir_lowering=False, num_devices=1)
    main, masks, onehot = constants()
    arrays = {name: np.ascontiguousarray(inputs[name]) for name in _INS}
    arrays |= {"const_main": main, "const_masks": masks, "const_onehot": onehot}
    tensors = {name: nc.dram_tensor(f"in_{name}", a.shape, mybir.dt.from_np(a.dtype), kind="ExternalInput").ap()
               for name, a in arrays.items()}
    out = nc.dram_tensor("out_x", (1, S, D), F32, kind="ExternalOutput").ap()
    build(nc, tensors, out)
    r = run_bass_kernel_spmd(nc, [{f"in_{name}": a for name, a in arrays.items()}], core_ids=[0])
    return r.results[0]["out_x"]
```
